# Optimizing a Trainium2 kernel written in Bass

```python
import math
import jax, jax.numpy as jnp
from jax import lax
import numpy as np

D_MODEL = 2048
BATCH = 1
SEQ = 256
DEPTH = 1

HEAD_DIM = 128
A_Q_HEADS = 8
A_KV_HEADS = 2
A_GROUP = A_Q_HEADS // A_KV_HEADS
WINDOW = 128
A_BLOCK = 128
B_HEADS = 8
GRID_W = 64
WIN_H = 8
WIN_W = 16
Q_COL_BLOCK = 16
K_COL_SPAN = Q_COL_BLOCK + WIN_W
D_FF = 5632
CONV_W = 3
ROPE_THETA = 10000.0
EPS = 1e-6
NEG = -1e30

A_Q_DIM = A_Q_HEADS * HEAD_DIM
A_KV_DIM = A_KV_HEADS * HEAD_DIM
B_DIM = B_HEADS * HEAD_DIM
IN_SPLITS = [A_Q_DIM, A_KV_DIM, A_KV_DIM, B_DIM, B_DIM, B_DIM, D_MODEL, D_MODEL]
IN_COLS = sum(IN_SPLITS)


def rmsnorm(x, g):
    xf = x.astype(jnp.float32)
    y = xf * lax.rsqrt(jnp.mean(xf * xf, axis=-1, keepdims=True) + EPS)
    return (y * g.astype(jnp.float32)).astype(x.dtype)

def rope(x, pos):
    half = x.shape[-1] // 2
    inv_freq = ROPE_THETA ** (-jnp.arange(half, dtype=jnp.float32) * (2.0 / x.shape[-1]))
    ang = pos[:, None] * inv_freq[None, :]
    cos = jnp.cos(ang)[None, :, None, :]
    sin = jnp.sin(ang)[None, :, None, :]
    xf = x.astype(jnp.float32)
    x1, x2 = xf[..., :half], xf[..., half:]
    return jnp.concatenate([x1 * cos - x2 * sin, x2 * cos + x1 * sin], axis=-1).astype(x.dtype)

def window_attention(q, k, v, sink):
    b, s_len, _, d = q.shape
    nb = s_len // A_BLOCK
    qb = q.reshape(b, nb, A_BLOCK, A_KV_HEADS, A_GROUP, d)
    pad = ((0, 0), (A_BLOCK, A_BLOCK), (0, 0), (0, 0))
    kp = jnp.pad(k, pad).reshape(b, nb + 2, A_BLOCK, A_KV_HEADS, d)
    vp = jnp.pad(v, pad).reshape(b, nb + 2, A_BLOCK, A_KV_HEADS, d)
    kb = jnp.concatenate([kp[:, 0:nb], kp[:, 1:nb + 1], kp[:, 2:nb + 2]], axis=2)
    vb = jnp.concatenate([vp[:, 0:nb], vp[:, 1:nb + 1], vp[:, 2:nb + 2]], axis=2)
    s = jnp.einsum('bnqhgd,bnkhd->bnhgqk', qb, kb,
                   preferred_element_type=jnp.float32) * (1.0 / math.sqrt(d))
    qpos = np.arange(nb)[:, None] * A_BLOCK + np.arange(A_BLOCK)[None, :]
    kpos = (np.arange(nb)[:, None] - 1) * A_BLOCK + np.arange(3 * A_BLOCK)[None, :]
    valid = ((np.abs(qpos[:, :, None] - kpos[:, None, :]) <= WINDOW)
             & (kpos >= 0)[:, None, :] & (kpos < s_len)[:, None, :])
    s = jnp.where(jnp.asarray(valid)[None, :, None, None], s, NEG)
    sink_b = sink.astype(jnp.float32).reshape(A_KV_HEADS, A_GROUP)[None, None, :, :, None, None]
    m = jnp.maximum(jnp.max(s, axis=-1, keepdims=True), sink_b)
    p = jnp.exp(s - m)
    p = p / (jnp.sum(p, axis=-1, keepdims=True) + jnp.exp(sink_b - m))
    o = jnp.einsum('bnhgqk,bnkhd->bnqhgd', p.astype(v.dtype), vb)
    return o.reshape(b, s_len, A_Q_HEADS * d)

def neighbourhood_attention(q, k, v, rpb):
    b, s_len, h, d = q.shape
    rows = s_len // GRID_W
    kh = min(WIN_H, rows)
    rb = kh
    nrb = -(-rows // rb)
    rows_p = nrb * rb
    kspan = min(rb + kh, rows)
    ncb = GRID_W // Q_COL_BLOCK
    nq = rb * Q_COL_BLOCK
    nk = kspan * K_COL_SPAN

    qg = jnp.pad(q.reshape(b, rows, GRID_W, h, d), ((0, 0), (0, rows_p - rows), (0, 0), (0, 0), (0, 0)))
    qb = qg.reshape(b, nrb, rb, ncb, Q_COL_BLOCK, h, d).transpose(0, 1, 3, 2, 4, 5, 6)
    qb = qb.reshape(b, nrb, ncb, nq, h, d)

    r0 = np.arange(nrb) * rb
    krows = np.clip(r0 - kh // 2, 0, rows - kspan)[:, None] + np.arange(kspan)[None, :]
    c0 = np.arange(ncb) * Q_COL_BLOCK
    kcols = np.clip(c0 - WIN_W // 2, 0, GRID_W - K_COL_SPAN)[:, None] + np.arange(K_COL_SPAN)[None, :]

    kg = k.reshape(b, rows, GRID_W, h, d)
    vg = v.reshape(b, rows, GRID_W, h, d)
    ridx = krows[:, None, :, None]
    cidx = kcols[None, :, None, :]
    kb = kg[:, ridx, cidx].reshape(b, nrb, ncb, nk, h, d)
    vb = vg[:, ridx, cidx].reshape(b, nrb, ncb, nk, h, d)

    shp_q = (nrb, ncb, rb, Q_COL_BLOCK)
    shp_k = (nrb, ncb, kspan, K_COL_SPAN)
    qr = np.broadcast_to((r0[:, None] + np.arange(rb)[None, :])[:, None, :, None], shp_q).reshape(nrb, ncb, nq)
    qc = np.broadcast_to((c0[:, None] + np.arange(Q_COL_BLOCK)[None, :])[None, :, None, :], shp_q).reshape(nrb, ncb, nq)
    kr = np.broadcast_to(krows[:, None, :, None], shp_k).reshape(nrb, ncb, nk)
    kc = np.broadcast_to(kcols[None, :, None, :], shp_k).reshape(nrb, ncb, nk)
    qr, qc = qr[..., :, None], qc[..., :, None]
    kr, kc = kr[..., None, :], kc[..., None, :]
    rs = np.clip(qr - kh // 2, 0, rows - kh)
    cs = np.clip(qc - WIN_W // 2, 0, GRID_W - WIN_W)
    valid = (kr >= rs) & (kr < rs + kh) & (kc >= cs) & (kc < cs + WIN_W)
    idx_r = np.clip(kr - qr + WIN_H - 1, 0, 2 * WIN_H - 2).astype(np.int32)
    idx_c = np.clip(kc - qc + WIN_W - 1, 0, 2 * WIN_W - 2).astype(np.int32)
    bias = rpb.astype(jnp.float32)[:, idx_r, idx_c].transpose(1, 2, 0, 3, 4)

    s = jnp.einsum('bncqhd,bnckhd->bnchqk', qb, kb,
                   preferred_element_type=jnp.float32) * (1.0 / math.sqrt(d))
    s = jnp.where(jnp.asarray(valid)[None, :, :, None], s + bias[None], NEG)
    p = jax.nn.softmax(s, axis=-1)
    o = jnp.einsum('bnchqk,bnckhd->bncqhd', p.astype(v.dtype), vb)
    o = o.reshape(b, nrb, ncb, rb, Q_COL_BLOCK, h, d).transpose(0, 1, 3, 2, 4, 5, 6)
    o = o.reshape(b, rows_p, GRID_W, h * d)[:, :rows]
    return o.reshape(b, s_len, h * d)

def first_inputs(seed: int = 0) -> dict:
    key = jax.random.key(seed)
    ks = jax.random.split(key, 20)
    f32 = jnp.float32

    def nrm(k, shape, scale):
        return jax.random.normal(k, shape, f32) * scale

    L = DEPTH
    return {
        "x": jax.random.normal(ks[0], (BATCH, SEQ, D_MODEL), f32),
        "norm_mix": 1.0 + nrm(ks[1], (L, D_MODEL), 0.02),
        "w_in": nrm(ks[2], (L, D_MODEL, IN_COLS), D_MODEL ** -0.5),
        "a_q_norm": 1.0 + nrm(ks[3], (L, HEAD_DIM), 0.02),
        "a_k_norm": 1.0 + nrm(ks[4], (L, HEAD_DIM), 0.02),
        "a_sink": nrm(ks[5], (L, A_Q_HEADS), 0.5),
        "b_q_norm": 1.0 + nrm(ks[6], (L, HEAD_DIM), 0.02),
        "b_k_norm": 1.0 + nrm(ks[7], (L, HEAD_DIM), 0.02),
        "b_rpb": nrm(ks[8], (L, B_HEADS, 2 * WIN_H - 1, 2 * WIN_W - 1), 0.1),
        "w_branch_a": nrm(ks[9], (L, A_Q_DIM, D_MODEL), A_Q_DIM ** -0.5),
        "w_branch_b": nrm(ks[10], (L, B_DIM, D_MODEL), B_DIM ** -0.5),
        "w_out": nrm(ks[11], (L, D_MODEL, D_MODEL), D_MODEL ** -0.5),
        "norm_ffn": 1.0 + nrm(ks[12], (L, D_MODEL), 0.02),
        "w_up": nrm(ks[13], (L, D_MODEL, 2 * D_FF), D_MODEL ** -0.5),
        "conv_w": nrm(ks[14], (L, CONV_W, 2 * D_FF), CONV_W ** -0.5),
        "conv_b": nrm(ks[15], (L, 2 * D_FF), 0.01),
        "w_down": nrm(ks[16], (L, D_FF, D_MODEL), D_FF ** -0.5),
    }

def first_block(x, norm_mix, w_in, a_q_norm, a_k_norm, a_sink, b_q_norm, b_k_norm, b_rpb,
              w_branch_a, w_branch_b, w_out, norm_ffn, w_up, conv_w, conv_b, w_down):
    b, s_len, _ = x.shape
    pos = jnp.arange(s_len, dtype=jnp.float32)
    split_points = np.cumsum(IN_SPLITS)[:-1].tolist()
    for l in range(DEPTH):
        h = rmsnorm(x, norm_mix[l])
        proj = h @ w_in[l]
        qa, ka, va, qb, kb, vb, ga, gb = jnp.split(proj, split_points, axis=-1)

        qa = rope(rmsnorm(qa.reshape(b, s_len, A_Q_HEADS, HEAD_DIM), a_q_norm[l]), pos)
        ka = rope(rmsnorm(ka.reshape(b, s_len, A_KV_HEADS, HEAD_DIM), a_k_norm[l]), pos)
        va = va.reshape(b, s_len, A_KV_HEADS, HEAD_DIM)
        out_a = window_attention(qa, ka, va, a_sink[l])

        qb = rmsnorm(qb.reshape(b, s_len, B_HEADS, HEAD_DIM), b_q_norm[l])
        kb = rmsnorm(kb.reshape(b, s_len, B_HEADS, HEAD_DIM), b_k_norm[l])
        vb = vb.reshape(b, s_len, B_HEADS, HEAD_DIM)
        out_b = neighbourhood_attention(qb, kb, vb, b_rpb[l])

        merged = (jax.nn.sigmoid(ga) * (out_a @ w_branch_a[l])
                  + jax.nn.sigmoid(gb) * (out_b @ w_branch_b[l]))
        x = x + merged @ w_out[l]

        h2 = rmsnorm(x, norm_ffn[l])
        u = h2 @ w_up[l]
        up = jnp.pad(u, ((0, 0), (1, 1), (0, 0)))
        cw = conv_w[l]
        u = up[:, :-2] * cw[0] + up[:, 1:-1] * cw[1] + up[:, 2:] * cw[2] + conv_b[l]
        gate, val = jnp.split(u, 2, axis=-1)
        x = x + (jax.nn.silu(gate) * val) @ w_down[l]
    return x


CTX_LEN = 256
CHUNK = 128
ROWS_PER_CHUNK = CHUNK // GRID_W
MIX_W = D_MODEL
A_WIDTH = MIX_W // 2
A_HEADS = 8
A_HEAD_DIM = A_WIDTH // A_HEADS
B_WIDTH = MIX_W - A_WIDTH
B_HEADS_2 = 4
B_DV = B_WIDTH // B_HEADS_2
B_DK = B_DV // 2
B_KEY_W = B_HEADS_2 * B_DK
GATE_RANK = 16
GATE_TAU = 16.0
FFN_HIDDEN = -(-8 * D_MODEL // (3 * 256)) * 256
P_IN = 2 * A_WIDTH + 2 * B_KEY_W + 2 * B_WIDTH + 2 * GATE_RANK


def rms_norm(x, g):
    xf = x.astype(jnp.float32)
    y = xf * lax.rsqrt(jnp.mean(xf * xf, axis=-1, keepdims=True) + EPS)
    return (y * g.astype(jnp.float32)).astype(x.dtype)

def layer_norm(x, g, b):
    xf = x.astype(jnp.float32)
    mu = jnp.mean(xf, axis=-1, keepdims=True)
    var = jnp.mean(jnp.square(xf - mu), axis=-1, keepdims=True)
    y = (xf - mu) * lax.rsqrt(var + EPS)
    return (y * g.astype(jnp.float32) + b.astype(jnp.float32)).astype(x.dtype)

def modulate(h, shift, scale):
    return h * (1 + scale) + shift

def split_proj(p):
    sizes = (A_WIDTH, A_WIDTH, B_KEY_W, B_KEY_W, B_WIDTH, B_WIDTH, GATE_RANK, GATE_RANK)
    out, start = [], 0
    for s in sizes:
        out.append(p[..., start:start + s])
        start += s
    return out

def spatial_gating(u, v, ln_g, ln_b, w_s, b_s, n_chunks):
    bsz, length, _ = u.shape
    u = jax.nn.gelu(u).reshape(bsz, n_chunks, CHUNK, A_HEADS, A_HEAD_DIM)
    v = jax.nn.gelu(v).reshape(bsz, length, A_HEADS, A_HEAD_DIM)
    v = layer_norm(v, ln_g.reshape(A_HEADS, A_HEAD_DIM), ln_b.reshape(A_HEADS, A_HEAD_DIM))
    v = v.reshape(bsz, n_chunks, CHUNK, A_HEADS, A_HEAD_DIM)
    mixed = jnp.einsum('hij,bnjhd->bnihd', w_s, v) + b_s.T[None, None, :, :, None]
    return (u * mixed).reshape(bsz, length, A_WIDTH)

def gla_prep(q, k, v, d_f, d_b, wd2_f, bd_f, wd2_b, bd_b):
    bsz, length, _ = q.shape
    def heads(t, d):
        return t.astype(jnp.float32).reshape(bsz, length, B_HEADS_2, d)
    q = heads(q, B_DK) * (B_DK ** -0.5)
    k = heads(k, B_DK)
    v = heads(v, B_DV)
    la_f = heads(jax.nn.log_sigmoid((d_f @ wd2_f + bd_f).astype(jnp.float32)) / GATE_TAU, B_DK)
    la_b = heads(jax.nn.log_sigmoid((d_b @ wd2_b + bd_b).astype(jnp.float32)) / GATE_TAU, B_DK)
    return q, k, v, la_f, la_b

def gla_scan(q, k, v, log_a, s0):
    bsz, length, nh, _ = q.shape
    n = length // CHUNK
    def to_chunks(t):
        return t.reshape(bsz, n, CHUNK, nh, t.shape[-1]).transpose(1, 0, 3, 2, 4)
    tri = jnp.tril(jnp.ones((CHUNK, CHUNK), dtype=bool))[None, None, :, :, None]
    def step(s, inp):
        qc, kc, vc, gc = inp
        b = jnp.cumsum(gc, axis=2)
        b_last = b[:, :, -1:, :]
        rel = jnp.where(tri, b[:, :, :, None, :] - b[:, :, None, :, :], -jnp.inf)
        scores = jnp.einsum('bhid,bhjd,bhijd->bhij', qc, kc, jnp.exp(rel))
        o = jnp.einsum('bhij,bhje->bhie', scores, vc) + jnp.einsum('bhid,bhde->bhie', qc * jnp.exp(b), s)
        s = jnp.exp(b_last[:, :, 0, :, None]) * s + jnp.einsum('bhjd,bhje->bhde', kc * jnp.exp(b_last - b), vc)
        return s, o
    s_fin, o = lax.scan(step, s0, (to_chunks(q), to_chunks(k), to_chunks(v), to_chunks(log_a)))
    o = o.transpose(1, 0, 3, 2, 4).reshape(bsz, length, nh, -1)
    return o, s_fin

def bidir_gla(px, pc):
    qx, kx, vx, fx, bx = px
    qc, kc, vc, fc, bc = pc
    s0 = jnp.zeros((qx.shape[0], B_HEADS_2, B_DK, B_DV), jnp.float32)
    flip = lambda t: jnp.flip(t, axis=1)
    oc_f, sc_f = gla_scan(qc, kc, vc, fc, s0)
    ox_f, _ = gla_scan(qx, kx, vx, fx, sc_f)
    oc_b, sc_b = gla_scan(flip(qc), flip(kc), flip(vc), flip(bc), s0)
    ox_b, _ = gla_scan(flip(qx), flip(kx), flip(vx), flip(bx), sc_b)
    return ox_f + flip(ox_b), oc_f + flip(oc_b)

def gla_out(o, g, out_g):
    bsz, length = o.shape[:2]
    y = o * lax.rsqrt(jnp.mean(o * o, axis=-1, keepdims=True) + EPS) * out_g.astype(jnp.float32).reshape(B_HEADS_2, B_DV)
    return y.reshape(bsz, length, B_WIDTH).astype(g.dtype) * jax.nn.silu(g)

def swiglu(h, w_in, w_out):
    a, b = jnp.split(h @ w_in, 2, axis=-1)
    return (jax.nn.silu(a) * b) @ w_out

def trunk_layer(x, xc, c_act, cc_act, w_mod, b_mod, g_pre_mix, g_post_mix, g_pre_ffn, g_post_ffn, w_in, ln_g, ln_b, w_s, b_s, wd2_f, bd_f, wd2_b, bd_b, out_g, w_out, w_ffn_in, w_ffn_out, rows, update_ctx):
    mod_x = jnp.split((c_act @ w_mod + b_mod)[:, None, :], 6, axis=-1)
    mod_c = jnp.split(cc_act @ w_mod + b_mod, 6, axis=-1)
    hx = modulate(rms_norm(x, g_pre_mix), mod_x[0], mod_x[1])
    hc = modulate(rms_norm(xc, g_pre_mix), mod_c[0], mod_c[1])
    ux, vx, qx, kx, vvx, gx, dfx, dbx = split_proj(hx @ w_in)
    uc, vc, qc, kc, vvc, gc, dfc, dbc = split_proj(hc @ w_in)
    gla_x, gla_c = bidir_gla(gla_prep(qx, kx, vvx, dfx, dbx, wd2_f, bd_f, wd2_b, bd_b),
                             gla_prep(qc, kc, vvc, dfc, dbc, wd2_f, bd_f, wd2_b, bd_b))
    a_x = spatial_gating(ux, vx, ln_g, ln_b, w_s, b_s, rows // ROWS_PER_CHUNK)
    y_x = jnp.concatenate([a_x, gla_out(gla_x, gx, out_g)], axis=-1) @ w_out
    x = x + mod_x[2] * rms_norm(y_x, g_post_mix)
    f_x = swiglu(modulate(rms_norm(x, g_pre_ffn), mod_x[3], mod_x[4]), w_ffn_in, w_ffn_out)
    x = x + mod_x[5] * rms_norm(f_x, g_post_ffn)
    if update_ctx:
        a_c = spatial_gating(uc, vc, ln_g, ln_b, w_s, b_s, xc.shape[1] // CHUNK)
        y_c = jnp.concatenate([a_c, gla_out(gla_c, gc, out_g)], axis=-1) @ w_out
        xc = xc + mod_c[2] * rms_norm(y_c, g_post_mix)
        f_c = swiglu(modulate(rms_norm(xc, g_pre_ffn), mod_c[3], mod_c[4]), w_ffn_in, w_ffn_out)
        xc = xc + mod_c[5] * rms_norm(f_c, g_post_ffn)
    return x, xc

def second_inputs(seed: int = 0) -> dict:
    key = jax.random.key(seed)
    ks = iter(jax.random.split(key, 32))
    f32 = jnp.float32
    def nrm(shape, scale=1.0):
        return jax.random.normal(next(ks), shape, f32) * scale
    def gain(shape):
        return 1.0 + nrm(shape, 0.05)
    L = DEPTH
    return {
        'x': nrm((BATCH, SEQ, D_MODEL)),
        'c': nrm((BATCH, D_MODEL)),
        'ctx': nrm((BATCH, CTX_LEN, D_MODEL)),
        'c_ctx': nrm((D_MODEL,)),
        'w_mod': nrm((L, D_MODEL, 6 * D_MODEL), 0.5 * D_MODEL ** -0.5),
        'b_mod': nrm((L, 6 * D_MODEL), 0.01),
        'g_pre_mix': gain((L, D_MODEL)),
        'g_post_mix': gain((L, D_MODEL)),
        'g_pre_ffn': gain((L, D_MODEL)),
        'g_post_ffn': gain((L, D_MODEL)),
        'w_in': nrm((L, D_MODEL, P_IN), D_MODEL ** -0.5),
        'gmlp_ln_g': gain((L, A_WIDTH)),
        'gmlp_ln_b': nrm((L, A_WIDTH), 0.01),
        'gmlp_ws': nrm((L, A_HEADS, CHUNK, CHUNK), CHUNK ** -0.5),
        'gmlp_bs': gain((L, A_HEADS, CHUNK)),
        'gla_wd2_fwd': nrm((L, GATE_RANK, B_KEY_W), GATE_RANK ** -0.5),
        'gla_bd_fwd': nrm((L, B_KEY_W), 0.1),
        'gla_wd2_bwd': nrm((L, GATE_RANK, B_KEY_W), GATE_RANK ** -0.5),
        'gla_bd_bwd': nrm((L, B_KEY_W), 0.1),
        'gla_out_g': gain((L, B_WIDTH)),
        'w_out': nrm((L, MIX_W, D_MODEL), MIX_W ** -0.5),
        'w_ffn_in': nrm((L, D_MODEL, 2 * FFN_HIDDEN), D_MODEL ** -0.5),
        'w_ffn_out': nrm((L, FFN_HIDDEN, D_MODEL), FFN_HIDDEN ** -0.5),
    }

def second_block(x, c, ctx, c_ctx, w_mod, b_mod, g_pre_mix, g_post_mix, g_pre_ffn, g_post_ffn, w_in, gmlp_ln_g, gmlp_ln_b, gmlp_ws, gmlp_bs, gla_wd2_fwd, gla_bd_fwd, gla_wd2_bwd, gla_bd_bwd, gla_out_g, w_out, w_ffn_in, w_ffn_out):
    rows = x.shape[1] // GRID_W
    c_act = jax.nn.silu(c)
    cc_act = jax.nn.silu(c_ctx)
    xc = ctx
    for i in range(DEPTH):
        x, xc = trunk_layer(x, xc, c_act, cc_act, w_mod[i], b_mod[i], g_pre_mix[i], g_post_mix[i], g_pre_ffn[i], g_post_ffn[i], w_in[i], gmlp_ln_g[i], gmlp_ln_b[i], gmlp_ws[i], gmlp_bs[i], gla_wd2_fwd[i], gla_bd_fwd[i], gla_wd2_bwd[i], gla_bd_bwd[i], gla_out_g[i], w_out[i], w_ffn_in[i], w_ffn_out[i], rows, i < DEPTH - 1)
    return x


def setup_inputs(seed=0):
    out = dict(first_inputs(seed))
    for name, value in second_inputs(seed + 1).items():
        if name != "x":
            out[name + "_2"] = value
    return out


def reference(
    x, norm_mix, w_in, a_q_norm, a_k_norm, a_sink, b_q_norm, b_k_norm, b_rpb, w_branch_a,
    w_branch_b, w_out, norm_ffn, w_up, conv_w, conv_b, w_down, c_2, ctx_2, c_ctx_2, w_mod_2,
    b_mod_2, g_pre_mix_2, g_post_mix_2, g_pre_ffn_2, g_post_ffn_2, w_in_2, gmlp_ln_g_2,
    gmlp_ln_b_2, gmlp_ws_2, gmlp_bs_2, gla_wd2_fwd_2, gla_bd_fwd_2, gla_wd2_bwd_2, gla_bd_bwd_2,
    gla_out_g_2, w_out_2, w_ffn_in_2, w_ffn_out_2,
):
    x = first_block(
        x, norm_mix, w_in, a_q_norm, a_k_norm, a_sink, b_q_norm, b_k_norm, b_rpb, w_branch_a,
        w_branch_b, w_out, norm_ffn, w_up, conv_w, conv_b, w_down,
    )
    return second_block(
        x, c_2, ctx_2, c_ctx_2, w_mod_2, b_mod_2, g_pre_mix_2, g_post_mix_2, g_pre_ffn_2,
        g_post_ffn_2, w_in_2, gmlp_ln_g_2, gmlp_ln_b_2, gmlp_ws_2, gmlp_bs_2, gla_wd2_fwd_2,
        gla_bd_fwd_2, gla_wd2_bwd_2, gla_bd_bwd_2, gla_out_g_2, w_out_2, w_ffn_in_2,
        w_ffn_out_2,
    )


_drawn_inputs = setup_inputs


def setup_inputs(seed=0):
    import zlib

    import numpy as np

    out = dict(_drawn_inputs(seed))
    spreads = {}
    factors = {'norm_mix': 8.0,
     'a_q_norm': 8.0,
     'a_k_norm': 8.0,
     'a_sink': 8.0,
     'b_q_norm': 8.0,
     'b_k_norm': 8.0,
     'b_rpb': 4.734,
     'norm_ffn': 3.664,
     'conv_b': 7.294,
     'c_ctx_2': 19.023,
     'b_mod_2': 4.143,
     'g_pre_mix_2': 17.337,
     'g_post_mix_2': 36.792,
     'g_pre_ffn_2': 20.932,
     'g_post_ffn_2': 38.392,
     'gmlp_ln_g_2': 56.128,
     'gmlp_ln_b_2': 64.0,
     'gmlp_bs_2': 60.76,
     'gla_wd2_fwd_2': 8.402,
     'gla_bd_fwd_2': 64.0,
     'gla_wd2_bwd_2': 9.875,
     'gla_bd_bwd_2': 64.0,
     'gla_out_g_2': 59.416,
     'ctx_2': 4.876}
    for name, (base, spread) in spreads.items():
        noise = np.random.default_rng([zlib.crc32(name.encode()), seed]).standard_normal(out[name].shape)
        drawn = base * np.exp(spread * noise) if base else spread * noise
        out[name] = __import__('jax').numpy.asarray(drawn.astype(out[name].dtype))
    for name, factor in factors.items():
        out[name] = (out[name] * factor).astype(out[name].dtype)
    return out
```

```python
import math
from contextlib import ExitStack

import numpy as np

import concourse.bass as bass
from concourse import mybir

F32 = mybir.dt.float32
I32 = mybir.dt.int32
ALU = mybir.AluOpType
ACT = mybir.ActivationFunctionType
AX = mybir.AxisListType.X

P = 128
T = 256
D = 2048
KD = D // P
HD = 128
FF = 5632
KF = FF // P
EPS = 1e-6
NEG = -1e30
GRID = 64
TAU = 16.0
GH = 4
RANK = 16

CK, CN = 4, 512
CHUNK = CK * CN
SLOTS = 8
LEVELS = [64, 32, 16, 8, 4, 2, 1]

N_PROJ = 0
N_GATE = N_PROJ + 9 * 4
N_BRANCH = N_GATE + 8 * 4
N_WOUT = N_BRANCH + 4 * 4
N_UP = N_WOUT + 4 * 4
N_DOWN = N_UP + 22 * 4
N_CTX = N_DOWN + 4 * 11
N_MIX = N_CTX + 3 * 4
N_WOUT2 = N_MIX + 10 * 4
N_UP2 = N_WOUT2 + 4 * 4
N_DOWN2 = N_UP2 + 22 * 4

JOBS = 32
LOOP_JOBS = 2


def host_tables():
    half = HD // 2
    inv = np.float32(10000.0) ** (-np.arange(half, dtype=np.float32) * np.float32(2.0 / HD))
    ang = np.arange(T, dtype=np.float32)[:, None] * inv[None, :].astype(np.float32)
    cos, sin = np.cos(ang), np.sin(ang)
    cos2 = np.concatenate([cos, cos], 1).reshape(2, P, HD).transpose(1, 0, 2)
    sin2 = np.concatenate([-sin, sin], 1).reshape(2, P, HD).transpose(1, 0, 2)
    q, k = np.arange(T)[:, None], np.arange(T)[None, :]
    mask_a = np.where(np.abs(q - k) <= 128, 0.0, NEG).reshape(2, P, T).transpose(1, 0, 2)
    qc, kc = np.arange(P)[:, None] % GRID, np.arange(T)[None, :] % GRID
    cs = np.clip(qc - 8, 0, GRID - 16)
    mask_b = np.where((kc >= cs) & (kc < cs + 16), 0.0, NEG)
    t, i = np.arange(P)[:, None], np.arange(P)[None, :]
    tri = np.stack([t <= i, t >= i, t > i, t < i], 1)
    levels = []
    for s in LEVELS:
        levels.append((t // (2 * s) == i // (2 * s)) & (t % (2 * s) < s) & (i % (2 * s) >= s))
    levels += [m.T for m in levels] + [t == i]
    levels = np.stack(levels, 1)
    c = lambda a: np.ascontiguousarray(a, dtype=np.float32)
    return {"t_ident": c(np.eye(P)), "t_cos": c(cos2), "t_sin": c(sin2), "t_mask_a": c(mask_a),
            "t_mask_b": c(mask_b), "t_tri": c(tri), "t_levels": c(levels)}


def build(nc, a, out):
    with ExitStack() as ctx:
        def sb(name, words):
            return ctx.enter_context(nc.sbuf_tensor(name, [P, words], F32))

        def sem(name):
            return ctx.enter_context(nc.semaphore(name))

        ring = ctx.enter_context(nc.sbuf_tensor("ring", [P, SLOTS, CK, CN], F32))
        x_tok = ctx.enter_context(nc.sbuf_tensor("x_tok", [P, 2, D], F32))
        act_t = ctx.enter_context(nc.sbuf_tensor("act_t", [P, KD, T], F32))
        big = sb("big", KF * T)
        mid = sb("mid", 15360)
        ident = sb("ident", P)
        ones = sb("ones", P)
        small = sb("small", 880)
        PS = ctx.enter_context(nc.psum_tensor("PS", [P, 8, 512], F32))

        def cut(tile, at, *shape):
            n = int(np.prod(shape))
            v = tile[:, at:at + n]
            if len(shape) == 2:
                return v.rearrange("p (a b) -> p a b", b=shape[1])
            if len(shape) == 3:
                return v.rearrange("p (a b c) -> p a b c", b=shape[1], c=shape[2])
            if len(shape) == 4:
                return v.rearrange("p (a b c d) -> p a b c d", b=shape[1], c=shape[2], d=shape[3])
            return v

        at = [0]

        def little(n):
            at[0] += n
            return small[:, at[0] - n:at[0]]

        g_mix, g_ffn = little(16), little(16)
        g_pre1, g_post1, g_pre2, g_post2 = little(16), little(16), little(16), little(16)
        b_mod = little(96)
        mod = little(128)
        c_vec = little(32)
        sink = little(8)
        bq_norm, bk_norm = little(1), little(1)
        conv = little(4 * 88).rearrange("p (f k) -> p f k", k=4)
        out_g, ln_g, ln_b = little(8), little(8), little(8)
        ss, rs = little(16), little(16)
        norm_ss, norm_rs = little(2), little(2)
        gate_col = little(16)
        mx = little(8)
        den = little(8)
        mean = little(8)
        decay = little(8)
        zero_col = little(1)
        eps_col = little(1)
        one_col = little(1)
        scale_c, scale_x1, scale_x2 = little(16), little(16), little(16)
        assert at[0] <= 880

        qa_t, ka_t, va = cut(big, 0, 8, T), cut(big, 2048, 2, T), cut(big, 2560, 2, T)
        qb_t, kb_t, vb = cut(big, 3072, 8, T), cut(big, 5120, 8, T), cut(big, 7168, 2, 1024)
        mask_a, mask_b = cut(big, 9216, 2, T), cut(big, 9728, T)
        cos, sin = cut(big, 9984, 2, P), cut(big, 10240, 2, P)
        aq_bc, ak_bc = cut(big, 10496, P), cut(big, 10624, P)
        bias = cut(big, 10752, 2, T)
        gates = cut(mid, 0, 32, T)
        oa_t, ob_t = cut(mid, 8192, 8, T), cut(mid, 10240, 8, T)
        tmp = [cut(mid, 12288 + 1024 * n, 1024) for n in range(3)]
        score_a, score_b = cut(mid, 12288, 2, T), cut(mid, 12800, 2, T)
        pt_a, pt_b = cut(mid, 13312, 2, T), cut(mid, 13824, 2, T)
        q_head = [cut(mid, 14336, T), cut(mid, 14592, T)]
        v_head = [cut(mid, 14848, 2, P), cut(mid, 15104, 2, P)]
        hidden = cut(big, 0, KF, T)
        wmod = cut(mid, 0, 4, CK, CN)
        acc = cut(mid, 8192, CN)
        conv_g, conv_v = cut(mid, 9216, 4, T), cut(mid, 10240, 4, T)
        ctx_tok = cut(mid, 11264, 2, D)
        hx_t = cut(big, 0, KD, T)
        cat_t = cut(big, 4096, KD, T)
        vv, k_tok = cut(big, 8192, 2, 1024), cut(big, 10240, 2, 512)
        q_t, k_t = cut(mid, 0, GH, T), cut(mid, 1024, GH, T)
        la = cut(mid, 2048, 2, 2, 512)
        state = cut(mid, 4096, 2, 2, 1024)
        level_mask = cut(mid, 8192, 15, P)
        tri = cut(mid, 10112, 4, P)
        s_t = cut(mid, 10624, GH, P)
        b_t = cut(mid, 11136, 2, 2, 512)
        e_buf = cut(mid, 13184, 2, 512)
        qe = cut(mid, 14208, 2, 512)
        y_tok = cut(mid, 14208, 1024)
        ql, kl = cut(mid, 2048, 2, 512), cut(mid, 3072, 2, 512)
        kc_tok, vvc = cut(mid, 0, 2, 512), cut(mid, 11136, 2, 1024)
        act_words = act_t[:].rearrange("p a b -> p (a b)")
        ws_t = act_words[:, 0:1024].rearrange("p (h i) -> p h i", i=P)
        bs_bc = act_words[:, 1024:2048].rearrange("p (h i) -> p h i", i=P)
        v_sgu = act_words[:, 2048:3072]
        v_tmp = act_words[:, 3072:4096]
        mix_out = cut(mid, 0, 2, D)
        gate_bc = cut(mid, 4096, D)
        gate_w = cut(mid, 6144, 4, P)
        norm_tmp = cut(mid, 12288, 4, 2, T)
        norm_tmp_c = cut(mid, 9216, 4, 2, T)
        norm_tmp2 = cut(big, 4096, 8, 2, T)
        d_t = ctx.enter_context(nc.sbuf_tensor("d_t", [33, T], F32))
        wd2 = mid[0:33, 1024:2048]
        w_d = sb("w_d", KD * 2 * RANK).rearrange("p (k n) -> p k n", n=2 * RANK)
        rpb = bias.rearrange("p a b -> p (a b)")[0:56, 0:P]
        skew = nc.dram_tensor("skew", (56, 64 * P), F32, kind="Internal").ap()

        weight_loaded = [sem(f"weight_loaded{n}") for n in range(SLOTS)]
        weight_used = sem("weight_used")
        names = [
            "attn_done", "attn_kept", "bias_loaded", "bias_used", "bs_loaded", "c_ready", "consts_loaded",
            "ctx_kept", "ctx_loaded", "cum_done", "cum_kept", "d_done", "d_kept", "decay_ready",
            "down2_kept", "down_added", "exps_done", "gate_kept", "gates_squashed", "grp_free",
            "head_staged", "hidden2_ready", "hidden_ready", "job_acc", "job_kept", "job_summed", "kdec_ready",
            "kt_done", "kt_kept", "la_done", "la_exp", "la_ready", "lv_diff", "lv_done", "lv_exp", "lv_k",
            "lv_q", "lv_taken", "masks_loaded", "max_ready", "merged", "mixer_loaded",
            "mod_ready", "o_done", "o_rs", "o_sq", "o_sum", "out_stored", "post_added", "post_bc",
            "post_bc_kept", "post_rs", "post_w", "probs_ready", "probs_t_ready", "probs_turned", "proj_free",
            "qe_exp", "qe_ready", "qkv_kept", "rem_done", "rem_exp", "rpb_loaded", "rstd_ready", "scores_done",
            "setup_done", "sgu_centred", "sgu_kept", "sgu_mixed", "sgu_ready", "sgu_rs", "sgu_sq", "sgu_var",
            "skew_written", "squared", "state_done", "state_ready", "summed", "turned", "up2_g_free",
            "up_g_act", "up_g_based", "up_g_free", "up_v_based", "up_v_free", "wd2_loaded", "wmod_loaded0",
            "wmod_loaded1", "wmod_loaded2", "wmod_loaded3", "wmod_used", "wout2_kept", "wout_added", "ws_kept",
            "ws_turned", "x_loaded", "y_kept", "y_ready", "y_turned",
        ]
        s = {n: sem(n) for n in names}
        norm_sems = {}
        for key in ("mix", "ffn", "ctx", "mix2", "ffn2"):
            norm_sems[key] = {n: sem(f"norm_{key}_{n}") for n in ("rstd", "tok", "turned", "kept")}

        block = ctx.enter_context(nc.Block())

        def ktiles(w):
            return w.rearrange("(k p) n -> p k n", p=P)

        w_in, w_up, w_down = ktiles(a["w_in"]), ktiles(a["w_up"]), ktiles(a["w_down"])
        w_ba, w_bb, w_out = ktiles(a["w_branch_a"]), ktiles(a["w_branch_b"]), ktiles(a["w_out"])
        w_mod, w_in2 = ktiles(a["w_mod_2"]), ktiles(a["w_in_2"])
        w_out2, w_up2, w_down2 = ktiles(a["w_out_2"]), ktiles(a["w_ffn_in_2"]), ktiles(a["w_ffn_out_2"])

        wide = lambda name, n: bass.AP(a[name].tensor, 0, [[0, P], [1, n]])
        consts = [(ident[:], a["t_ident"]), (g_mix, a["norm_mix"]), (cos[:], a["t_cos"]), (sin[:], a["t_sin"]),
                  (aq_bc, wide("a_q_norm", HD)), (ak_bc, wide("a_k_norm", HD)), (bq_norm, a["b_q_norm"]),
                  (bk_norm, a["b_k_norm"]), (mask_a[:], a["t_mask_a"]), (mask_b, a["t_mask_b"]),
                  (sink, wide("a_sink", 8)), (g_ffn, a["norm_ffn"]), (conv[:], a["conv"]),
                  (c_vec[:, 0:16], a["c_ctx_2"]), (c_vec[:, 16:32], a["c_2"]), (b_mod, a["b_mod_2"]),
                  (g_pre1, a["g_pre_mix_2"]), (g_post1, a["g_post_mix_2"]), (g_pre2, a["g_pre_ffn_2"]),
                  (g_post2, a["g_post_ffn_2"]), (out_g, a["gla_out_g_2"]), (ln_g, a["gmlp_ln_g_2"]),
                  (ln_b, a["gmlp_ln_b_2"]), (w_d[:], a["w_decay"])]
        N_CONSTS = len(consts)

        MIX_GROUPS = [("k", 2560), ("q", 2048), ("vv0", 3072), ("vv1", 3584), ("g0", 4096), ("g1", 4608),
                      ("u0", 0), ("u1", 512), ("v0", 1024), ("v1", 1536)]
        PROJ = ["qa0", "qa1", "kv", "qb0", "qb1", "kb0", "kb1", "vb0", "vb1"]
        NORMED = PROJ[:7]

        sched = []
        for c in range(4):
            sched.append(("mm", 0, c))
        sched.append(("post", 0))
        sched += [("d",), ("la",)]
        for c in range(4):
            sched.append(("mm", 1, c))
            if c == 1:
                sched.append(("kt",))
            if c == 2:
                sched.append(("cum",))
        sched.append(("post", 1))
        for c in range(4):
            sched.append(("mm", 2, c))
            if c == 0:
                sched.append(("wst",))
            if c == 1:
                sched += [("rem", 0), ("rem", 1)]
        sched.append(("post", 2))
        for c in range(4):
            sched.append(("mm", 3, c))
        sched.append(("post", 3))
        todo = []
        for n in range(2):
            todo += [("qe", n)] + [("level", n, l) for l in range(15)] + [("o", n), ("y", n)]
        slot = 0
        for g in range(4, 10):
            for c in range(4):
                sched.append(("mm", g, c))
                if slot == 0:
                    sched += [("upd", 0), ("upd", 1)]
                if c == 0 and g > 4:
                    sched.append(("post", g - 1))
                if (g, c) == (9, 2):
                    sched.append(("sgu", 0))
                if slot >= 1:
                    sched += todo[2 * slot - 2:2 * slot]
                slot += 1
        assert 2 * slot - 2 >= len(todo)
        sched += [("post", 9), ("sgu", 1)]

        def down_jobs(g, c):
            at_ = {3: 0, 6: 1, 10: 2}.get(c)
            j = None if at_ is None else 11 * LOOP_JOBS + 3 * g + at_
            return [j] if j is not None and j < JOBS else []

        def group_done(eng, n_last):
            eng.wait_ge(weight_used, n_last + 1)

        def loaded(eng, n):
            eng.wait_ge(weight_loaded[n % SLOTS], 16 * (n // SLOTS + 1))

        def loaded_in(eng, n, i):
            eng.wait_ge(weight_loaded[n % SLOTS], i * 16 + 16 * (n // SLOTS + 1))

        @block.sync
        def _(sp):
            def load(n, src):
                if n >= SLOTS:
                    sp.wait_ge(weight_used, n - SLOTS + 1)
                sp.dma_start(ring[:, n % SLOTS, :, :], src).then_inc(weight_loaded[n % SLOTS], 16)

            def load_in(n, i, src):
                sp.wait_ge(weight_used, i * 8 + (n - SLOTS + 1))
                sp.dma_start(ring[:, n % SLOTS, :, :], src).then_inc(weight_loaded[n % SLOTS], 16)

            def cols(w, c, at):
                return w[:, CK * c:CK * c + CK, at:at + CN]

            sp.dma_start(x_tok[:, 0, :], a["x"][0:P, :]).then_inc(s["x_loaded"], 16)
            sp.dma_start(x_tok[:, 1, :], a["x"][P:T, :]).then_inc(s["x_loaded"], 16)
            for g in range(9):
                for c in range(4):
                    load(N_PROJ + 4 * g + c, cols(w_in, c, CN * g))
            with sp.Fori(0, 4) as i:
                for j in range(8):
                    load_in(N_GATE + j, i, w_in[:, CK * (j % 4):CK * (j % 4) + CK,
                                                bass.ds(i * 1024 + (4608 + CN * (j // 4)), CN)])
            for g in range(4):
                for c in range(4):
                    load(N_BRANCH + 4 * g + c, cols(w_ba if c < 2 else w_bb, c % 2, CN * g))
            for g in range(4):
                for c in range(4):
                    load(N_WOUT + 4 * g + c, cols(w_out, c, CN * g))

            def ffn(n_up, n_down, up, down):
                with sp.Fori(0, 11) as i:
                    for j in range(8):
                        load_in(n_up + j, i, up[:, CK * (j % 4):CK * (j % 4) + CK,
                                                bass.ds(i * CN + FF * (j // 4), CN)])
                for g in range(4):
                    for c in range(11):
                        load(n_down + 11 * g + c, cols(down, c, CN * g))

            ffn(N_UP, N_DOWN, w_up, w_down)
            for g, at_ in enumerate((2560, 3072, 3584)):
                for c in range(4):
                    load(N_CTX + 4 * g + c, cols(w_in2, c, at_))
            for g, (_, at_) in enumerate(MIX_GROUPS):
                for c in range(4):
                    load(N_MIX + 4 * g + c, cols(w_in2, c, at_))
            for g in range(4):
                for c in range(4):
                    load(N_WOUT2 + 4 * g + c, cols(w_out2, c, CN * g))
            ffn(N_UP2, N_DOWN2, w_up2, w_down2)
            for h in range(2):
                sp.wait_ge(s["post_added"], 3 + h)
                sp.dma_start(out[h * P:(h + 1) * P, :], x_tok[:, h, :]).then_inc(s["out_stored"], 16)
            sp.wait_ge(s["out_stored"], 32)


        def bc(ap, shape):
            return ap.broadcast_to(shape)

        @block.tensor
        def _(pe):
            def chunk_tok(n, c, chunks, stat, bank):
                loaded(pe, n)
                for k in range(CK):
                    kt = CK * c + k
                    for h in range(2):
                        mm = pe.matmul(PS[:, bank + h, :], stat[:, kt, h * P:(h + 1) * P],
                                       ring[:, n % SLOTS, k, :], start=kt == 0, stop=kt == CK * chunks - 1)
                mm.then_inc(weight_used, 1)

            def chunk_feat(n, c, chunks, mov, bank, i=None):
                loaded(pe, n) if i is None else loaded_in(pe, n, i)
                for k in range(CK):
                    kt = CK * c + k
                    for f in range(4):
                        mm = pe.matmul(PS[:, bank + f // 2, (f % 2) * T:(f % 2) * T + T],
                                       ring[:, n % SLOTS, k, f * P:(f + 1) * P], mov[:, kt, :],
                                       start=kt == 0 and f % 2 == 0, stop=kt == CK * chunks - 1,
                                       skip_group_check=True)
                mm.then_inc(weight_used, 1)

            def norm_piece(key, j, src):
                n = norm_sems[key]
                pe.wait_ge(n["tok"], j + 1)
                if j >= 2:
                    pe.wait_ge(n["kept"], j - 1)
                for m in range(2):
                    for h in range(2):
                        mm = pe.transpose(PS[:, 4 + j % 2, m * T + h * P:m * T + (h + 1) * P],
                                          src[:, j % src.shape[1], h, m * P:(m + 1) * P], ident[:])
                mm.then_inc(n["turned"], 1)

            def turn(n):
                pe.wait_ge(s["proj_free"], n + 1)
                if n >= 1:
                    pe.wait_ge(s["qkv_kept"], n)
                heads = 2 if NORMED[n] == "kv" else 4
                for hd in range(heads):
                    for h in range(2):
                        at_ = (h * heads + hd) * P
                        mm = pe.transpose(PS[:, 4 + hd // 2, (hd % 2) * T + h * P:(hd % 2) * T + (h + 1) * P],
                                          tmp[1][:, at_:at_ + P], ident[:])
                mm.then_inc(s["turned"], 1)

            def mod_sum(done):
                pe.wait_ge(s["job_acc"], done + 1)
                pe.wait_ge(s["job_kept"], done + 1)
                for q in range(4):
                    mm = pe.matmul(PS[:, 6, q:q + 1], acc[:, q * P:(q + 1) * P], ones[:, 0:1],
                                   start=True, stop=True)
                mm.then_inc(s["job_summed"], 1)

            pe.wait_ge(s["consts_loaded"], 16 * N_CONSTS)
            pe.wait_ge(s["setup_done"], 1)
            for j in range(8):
                norm_piece("mix", j, norm_tmp)

            for g in range(9):
                for c in range(4):
                    if g == 0:
                        pe.wait_ge(norm_sems["mix"]["kept"], 2 * c + 2)
                    elif g >= 2 and c == 0:
                        pe.wait_ge(s["proj_free"], g - 1)
                    chunk_tok(N_PROJ + 4 * g + c, c, 4, act_t, 2 * (g % 2))
                    if c == 2 and 1 <= g <= len(NORMED):
                        turn(g - 1)

            pe.wait_ge(s["proj_free"], 9)
            pe.wait_ge(s["qkv_kept"], 7)
            pe.sem_inc(s["attn_done"], 1)
            pe.sem_inc(s["job_summed"], 1)
            with pe.Fori(0, 4) as i:
                for u in range(2):
                    done = i * 2 + u
                    pe.wait_ge(s["head_staged"], done + 1)
                    for n, keys in ((0, ka_t[:, i // 2, :]), (1, kb_t[:, done, :])):
                        for b in range(2):
                            mm = pe.matmul(PS[:, 4 + n, b * T:(b + 1) * T], q_head[n][:, b * P:(b + 1) * P],
                                           keys, start=True, stop=True)
                    mm.then_inc(s["scores_done"], 1)
                    pe.wait_ge(s["gate_kept"], done + 1)
                    for c in range(4):
                        chunk_feat(N_GATE + 4 * u + c, c, 4, act_t, 0, i)
                        if c == 1:
                            pe.wait_ge(s["probs_ready"], done + 1)
                            for n, probs in ((0, score_a), (1, score_b)):
                                for b in range(2):
                                    for k in range(2):
                                        mm = pe.transpose(PS[:, 6 + n, k * T + b * P:k * T + (b + 1) * P],
                                                          probs[:, b, k * P:(k + 1) * P], ident[:])
                            mm.then_inc(s["probs_turned"], 1)
                        if c == 2:
                            pe.wait_ge(s["probs_t_ready"], done + 1)
                            for n, probs in ((0, pt_a), (1, pt_b)):
                                for k in range(2):
                                    mm = pe.matmul(PS[:, 2 + n, 0:T], v_head[n][:, k, :], probs[:, k, :],
                                                   start=k == 0, stop=k == 1)
                            mm.then_inc(s["attn_done"], 1)

            pe.wait_ge(s["attn_kept"], 8)
            pe.wait_ge(s["gate_kept"], 9)
            for g in range(4):
                if g >= 2:
                    pe.wait_ge(s["merged"], g - 1)
                for c in range(4):
                    chunk_feat(N_BRANCH + 4 * g + c, c % 2, 2, oa_t if c < 2 else ob_t, 4 * (g % 2) + 2 * (c // 2))

            for g in range(4):
                pe.wait_ge(s["merged"], 3 + g // 2)
                for c in range(4):
                    pe.wait_ge(s["merged"], max(c + 1, 3 + g // 2))
                    chunk_tok(N_WOUT + 4 * g + c, c, 4, gates, 2 * g)

            for j in range(8):
                norm_piece("ffn", j, norm_tmp)

            pe.wait_ge(norm_sems["ffn"]["kept"], 8)
            with pe.Fori(0, 11) as i:
                pe.wait_ge(s["up_g_free"], i + 1)
                for c in range(4):
                    chunk_feat(N_UP + c, c, 4, act_t, 0, i)
                pe.wait_ge(s["up_v_free"], i + 1)
                for c in range(4):
                    chunk_feat(N_UP + 4 + c, c, 4, act_t, 2, i)
                    if c == 1:
                        mod_sum(i * LOOP_JOBS)
                mod_sum(i * LOOP_JOBS + 1)
            pe.wait_ge(s["hidden_ready"], 11)
            for g in range(4):
                if g >= 2:
                    pe.wait_ge(s["down_added"], g - 1)
                for c in range(11):
                    chunk_tok(N_DOWN + 11 * g + c, c, 11, hidden, 2 * (g % 2))
                    for j in down_jobs(g, c):
                        mod_sum(j)
                    if g == 3 and c >= 3:
                        norm_piece("ctx", c - 3, norm_tmp_c)

            def decay_proj(src, m):
                for k in range(KD):
                    mm = pe.matmul(PS[0:2 * RANK, 7, 0:T], w_d[:, k, :], src[:, k, :], start=k == 0,
                                   stop=k == KD - 1)
                mm.then_inc(s["d_done"], 1)

            def log_decay(m):
                pe.wait_ge(s["d_kept"], m + 1)
                pe.wait_ge(s["wd2_loaded"], 64)
                for h in range(2):
                    for r in range(2):
                        mm = pe.matmul(PS[:, 4 + 2 * h + r, :], d_t[:, h * P:(h + 1) * P],
                                       wd2[:, r * 512:(r + 1) * 512], start=True, stop=True)
                mm.then_inc(s["la_done"], 1)

            pe.wait_ge(norm_sems["ctx"]["kept"], 8)
            decay_proj(act_t, 0)
            for g in range(3):
                if g == 0:
                    pe.wait_ge(s["down_added"], 3)
                if g == 1:
                    pe.wait_ge(s["down_added"], 4)
                if g == 2:
                    pe.wait_ge(s["ctx_kept"], 1)
                for c in range(4):
                    chunk_tok(N_CTX + 4 * g + c, c, 4, act_t, 2 * (g % 2))
                    if g == 0 and c == 1:
                        log_decay(0)
                    if g == 1 and c == 0:
                        pe.wait_ge(s["masks_loaded"], 32)
                        pe.wait_ge(s["la_ready"], 1)
                        for r in range(2):
                            for h in range(2):
                                other = 1 - h
                                whole = (h == 0) if r == 0 else (h == 1)
                                mm = pe.matmul(PS[:, 4 + 2 * r + h, :], tri[:, 2 + r, :], la[:, h, r, :],
                                               start=True, stop=not whole)
                                if whole:
                                    mm = pe.matmul(PS[:, 4 + 2 * r + h, :], ones[:], la[:, other, r, :],
                                                   start=False, stop=True)
                        mm.then_inc(s["rem_done"], 1)
                    if (g, c) in ((1, 2), (1, 3), (2, 0), (2, 1)):
                        pe.wait_ge(s["rem_exp"], 1)
                        at_ = 2 * (4 * (g - 1) + c - 2)
                        norm_piece("mix2", at_, norm_tmp2)
                        norm_piece("mix2", at_ + 1, norm_tmp2)
            pe.wait_ge(s["ctx_kept"], 3)
            for r in range(2):
                pe.wait_ge(s["kdec_ready"], r + 1)
                for hd in range(GH):
                    for h in range(2):
                        mm = pe.matmul(PS[:, 4 + 2 * r + hd // 2, (hd % 2) * T:(hd % 2) * T + T],
                                       e_buf[:, h, hd * P:(hd + 1) * P] if r == 0 else qe[:, h, hd * P:(hd + 1) * P],
                                       vvc[:, h, hd * T:(hd + 1) * T], start=h == 0 and hd % 2 == 0, stop=h == 1,
                                       skip_group_check=True)
                mm.then_inc(s["state_done"], 1)

            def mix_bank(g):
                return 2 * (g % 2)

            lv = 0
            for item in sched:
                if item[0] == "mm":
                    _, g, c = item
                    if c == 0:
                        if g == 0:
                            pe.wait_ge(norm_sems["mix2"]["kept"], 8)
                        if g >= 2:
                            pe.wait_ge(s["grp_free"], g - 1)
                    kind = MIX_GROUPS[g][0]
                    if kind[0] in "kv":
                        chunk_tok(N_MIX + 4 * g + c, c, 4, hx_t, mix_bank(g))
                    else:
                        chunk_feat(N_MIX + 4 * g + c, c, 4, hx_t, mix_bank(g))
                elif item[0] == "d":
                    pe.wait_ge(s["state_ready"], 2)
                    decay_proj(hx_t, 1)
                elif item[0] == "la":
                    pe.wait_ge(norm_sems["mix2"]["kept"], 8)
                    log_decay(1)
                elif item[0] == "kt":
                    pe.wait_ge(s["grp_free"], 1)
                    pe.wait_ge(s["la_ready"], 2)
                    for hd in range(GH):
                        for h in range(2):
                            mm = pe.transpose(PS[:, 4 + hd // 2, (hd % 2) * T + h * P:(hd % 2) * T + (h + 1) * P],
                                              k_tok[:, h, hd * P:(hd + 1) * P], ident[:])
                    mm.then_inc(s["kt_done"], 1)
                elif item[0] == "cum":
                    pe.wait_ge(s["kt_kept"], 1)
                    for n in range(2):
                        for r in range(2):
                            for hd in range(GH):
                                mm = pe.matmul(PS[:, 4 + 2 * n + r, hd * P:(hd + 1) * P],
                                               la[:, n, r, hd * P:(hd + 1) * P], tri[:, r, :], start=True, stop=True)
                    mm.then_inc(s["cum_done"], 1)
                elif item[0] == "wst":
                    pe.wait_ge(s["cum_kept"], 1)
                    pe.wait_ge(s["mixer_loaded"], 16)
                    for hd in range(8):
                        mm = pe.transpose(PS[:, 4 + hd // 4, (hd % 4) * P:(hd % 4 + 1) * P],
                                          v_sgu[:, hd * P:(hd + 1) * P], ident[:])
                    mm.then_inc(s["ws_turned"], 1)
                elif item[0] == "rem":
                    r = item[1]
                    mm = pe.matmul(PS[:, 6 + r, :], tri[:, 2 + r, :], la[:, r, r, :], start=True, stop=True)
                    mm.then_inc(s["rem_done"], 1)
                elif item[0] == "upd":
                    r = item[1]
                    pe.wait_ge(s["kdec_ready"], 3 + r)
                    pe.wait_ge(s["grp_free"], 4)
                    pe.wait_ge(s["ws_kept"], 1)
                    for hd in range(GH):
                        mm = pe.matmul(PS[:, 4 + 2 * r + hd // 2, (hd % 2) * T:(hd % 2) * T + T],
                                       e_buf[:, r, hd * P:(hd + 1) * P], vv[:, r, hd * T:(hd + 1) * T],
                                       start=True, stop=True)
                    mm.then_inc(s["state_done"], 1)
                elif item[0] == "level":
                    pe.wait_ge(s["lv_q"], lv + 1)
                    pe.wait_ge(s["lv_k"], lv + 1)
                    if lv >= 2:
                        pe.wait_ge(s["lv_taken"], lv - 1)
                    elif lv == 0:
                        pe.wait_ge(s["state_ready"], 4)
                    for hd in range(GH):
                        mm = pe.matmul(PS[:, 4 + lv % 2, hd * P:(hd + 1) * P], kl[:, lv % 2, hd * P:(hd + 1) * P],
                                       ql[:, lv % 2, hd * P:(hd + 1) * P], start=True, stop=True)
                    mm.then_inc(s["lv_done"], 1)
                    lv += 1
                elif item[0] == "o":
                    n = item[1]
                    pe.wait_ge(s["lv_taken"], 15 * (n + 1))
                    pe.wait_ge(s["qe_ready"], n + 1)
                    if n == 1:
                        pe.wait_ge(s["y_ready"], 1)
                    for hd in range(GH):
                        o = PS[:, 6 + hd // 2, (hd % 2) * T:(hd % 2) * T + T]
                        pe.matmul(o, s_t[:, hd, :], vv[:, n, hd * T:(hd + 1) * T], start=True, stop=False)
                        for r in range(2):
                            mm = pe.matmul(o, qe[:, r, hd * P:(hd + 1) * P],
                                           state[:, r, n if r == 0 else 1 - n, hd * T:(hd + 1) * T],
                                           start=False, stop=r == 1)
                    mm.then_inc(s["o_done"], 1)
                elif item[0] == "y":
                    n = item[1]
                    pe.wait_ge(s["y_ready"], n + 1)
                    if n == 1:
                        pe.wait_ge(s["y_kept"], 1)
                    for f in range(8):
                        mm = pe.transpose(PS[:, 6 + f // 4, (f % 4) * P:(f % 4 + 1) * P],
                                          y_tok[:, f * P:(f + 1) * P], ident[:])
                    mm.then_inc(s["y_turned"], 1)
                elif item[0] == "sgu":
                    m = item[1]
                    pe.wait_ge(s["sgu_ready"], m + 1)
                    pe.wait_ge(s["ws_kept"], 1)
                    pe.wait_ge(s["lv_taken"], 30)
                    pe.wait_ge(s["y_kept"], 2)
                    if m == 1:
                        pe.wait_ge(s["sgu_kept"], 1)
                    for n in range(2):
                        for hd in range(4):
                            mm = pe.matmul(PS[:, 4 + n, hd * P:(hd + 1) * P],
                                           v_sgu[:, n * 512 + hd * P:n * 512 + (hd + 1) * P],
                                           ws_t[:, 4 * m + hd, :], start=True, stop=True)
                    for hd in range(4):
                        mm = pe.matmul(PS[:, 6, hd * P:(hd + 1) * P], ones[:], ws_t[:, 4 * m + hd, :],
                                       start=True, stop=True)
                    mm.then_inc(s["sgu_mixed"], 1)

            for g in range(4):
                if g == 0:
                    pe.wait_ge(s["grp_free"], 10)
                    pe.wait_ge(s["sgu_kept"], 2)
                for c in range(4):
                    chunk_tok(N_WOUT2 + 4 * g + c, c, 4, cat_t, 2 * g)

            def spread_gate(m):
                for j in range(4):
                    pe.wait_ge(s["post_w"], 4 * m + j + 1)
                    if m + j:
                        pe.wait_ge(s["post_bc_kept"], 4 * m + j)
                    for f in range(4):
                        mm = pe.matmul(PS[:, 0, f * P:(f + 1) * P], gate_w[:, f, :], ident[:], start=True, stop=True)
                    mm.then_inc(s["post_bc"], 1)

            pe.wait_ge(s["wout2_kept"], 1)
            spread_gate(0)
            for j in range(8):
                norm_piece("ffn2", j, norm_tmp)

            pe.wait_ge(norm_sems["ffn2"]["kept"], 8)
            with pe.Fori(0, 11) as i:
                pe.wait_ge(s["up2_g_free"], i + 1)
                for c in range(4):
                    chunk_feat(N_UP2 + c, c, 4, act_t, 0, i)
                pe.wait_ge(s["hidden2_ready"], i + 1)
                for c in range(4):
                    chunk_feat(N_UP2 + 4 + c, c, 4, act_t, 2, i)
            pe.wait_ge(s["hidden2_ready"], 12)
            for g in range(4):
                for c in range(11):
                    chunk_tok(N_DOWN2 + 11 * g + c, c, 11, hidden, 2 * g)
            pe.wait_ge(s["down2_kept"], 1)
            spread_gate(1)

        @block.vector
        def _(ve):
            def norm(key, src, dst):
                n = norm_sems[key]
                ve.wait_ge(n["rstd"], 1)
                for j in range(8):
                    if j >= dst.shape[1]:
                        ve.wait_ge(n["turned"], j - 3)
                    for h in range(2):
                        op = ve.tensor_scalar(dst[:, j % dst.shape[1], h, :], src[:, h, j * T:(j + 1) * T],
                                              norm_rs[:, h:h + 1], None, ALU.mult)
                    op.then_inc(n["tok"], 1)

            def pair(bank, width=512):
                return PS[:, bank:bank + 2, 0:width]

            ve.memset(d_t[2 * RANK:2 * RANK + 1, :], 1.0)
            ve.wait_ge(s["x_loaded"], 32)
            norm("mix", x_tok, norm_tmp)

            for g, kind in enumerate(PROJ):
                if g >= len(NORMED):
                    group_done(ve, N_PROJ + 4 * g + 3)
                    at_ = 512 * (g - len(NORMED))
                    ve.tensor_copy(vb[:, :, at_:at_ + 512], pair(2 * (g % 2))).then_inc(s["proj_free"], 1)
                    continue
                heads = 2 if kind == "kv" else 4
                w = heads * HD
                sq, tok, rot = (t[:, 0:2 * w].rearrange("p (h n d) -> p h n d", h=2, d=HD) for t in tmp)
                ve.wait_ge(s["squared"], g + 1)
                ve.tensor_reduce(ss[:, 0:2 * heads], tmp[0][:, 0:2 * w].rearrange("p (n d) -> p n d", d=HD),
                                 AX, ALU.add).then_inc(s["summed"], 1)
                ve.wait_ge(s["rstd_ready"], g + 1)
                if g:
                    ve.wait_ge(s["turned"], g)
                ps = pair(2 * (g % 2), w).rearrange("p h (n d) -> p h n d", d=HD)
                rstd = rs[:, 0:2 * heads].rearrange("p (h n) -> p h n", h=2).unsqueeze(3)
                op = ve.tensor_tensor(tok, ps, bc(rstd, [P, 2, heads, HD]), ALU.mult)
                if g < 3:
                    if kind == "kv":
                        ve.tensor_copy(va[:], PS[:, 2 * (g % 2):2 * (g % 2) + 2, 256:512])
                    ve.drain()
                    flat = tmp[1][:, 0:2 * w].rearrange("p (n d) -> p n d", d=HD)
                    weight = (ak_bc if kind == "kv" else aq_bc).unsqueeze(1)
                    ve.tensor_tensor(flat, flat, bc(weight, [P, 2 * heads, HD]), ALU.mult)
                    ve.drain()
                    ve.tensor_tensor(sq, tok, bc(cos.unsqueeze(2), [P, 2, heads, HD]), ALU.mult)
                    half = HD // 2
                    lo = bc(sin[:, :, 0:half].unsqueeze(2), [P, 2, heads, half])
                    hi = bc(sin[:, :, half:HD].unsqueeze(2), [P, 2, heads, half])
                    ve.tensor_tensor(rot[:, :, :, 0:half], tok[:, :, :, half:HD], lo, ALU.mult)
                    ve.tensor_tensor(rot[:, :, :, half:HD], tok[:, :, :, 0:half], hi, ALU.mult)
                    ve.drain()
                    op = ve.tensor_tensor(tmp[1][:, 0:2 * w], tmp[0][:, 0:2 * w], tmp[2][:, 0:2 * w], ALU.add)
                op.then_inc(s["proj_free"], 1)

            scale = 1.0 / math.sqrt(HD)
            ve.sem_inc(s["bias_used"], 1)
            with ve.Fori(0, 4) as i:
                for u in range(2):
                    done = i * 2 + u
                    sink_col = sink[:, bass.ds(i * 2 + u, 1)]
                    ve.wait_ge(s["bias_loaded"], done * 64 + 64)
                    ve.wait_ge(s["scores_done"], done + 1)
                    ps = PS[:, 4:6, :].rearrange("p a (b t) -> p a b t", t=T)
                    ve.scalar_tensor_tensor(score_a[:], ps[:, 0], scale, mask_a[:], ALU.mult, ALU.add)
                    ve.scalar_tensor_tensor(score_b[:], ps[:, 1], scale, bias[:], ALU.mult, ALU.add)\
                        .then_inc(s["bias_used"], 1)
                    ve.drain()
                    ve.tensor_tensor(score_b[:], score_b[:], bc(mask_b.unsqueeze(1), [P, 2, T]), ALU.add)
                    ve.tensor_reduce(mx[:, 0:2], score_a[:], AX, ALU.max)
                    ve.drain()
                    ve.tensor_reduce(mx[:, 2:4], score_b[:], AX, ALU.max)
                    ve.tensor_scalar(mx[:, 0:2], mx[:, 0:2], sink_col, None, ALU.max)
                    ve.drain()
                    ve.tensor_scalar(mx[:, 4:8], mx[:, 0:4], -1.0, None, ALU.mult).then_inc(s["max_ready"], 1)
                    ve.wait_ge(s["exps_done"], done + 1)
                    ve.tensor_tensor(den[:, 0:2], den[:, 0:2], den[:, 4:6], ALU.add)
                    ve.drain()
                    ve.reciprocal(den[:, 4:8], den[:, 0:4])
                    ve.drain()
                    for n, probs in ((0, score_a), (1, score_b)):
                        for b in range(2):
                            op = ve.tensor_scalar(probs[:, b, :], probs[:, b, :],
                                                  den[:, 4 + 2 * n + b:5 + 2 * n + b], None, ALU.mult)
                    op.then_inc(s["probs_ready"], 1)

            for g in range(4):
                banks = 4 * (g % 2)
                ga = gates[:, 4 * g:4 * g + 4, :].rearrange("p (a b) t -> p a (b t)", a=2)
                gb = gates[:, 16 + 4 * g:20 + 4 * g, :].rearrange("p (a b) t -> p a (b t)", a=2)
                ve.wait_ge(s["gates_squashed"], g + 1)
                group_done(ve, N_BRANCH + 4 * g + 3)
                ve.tensor_tensor(ga, ga, pair(banks), ALU.mult)
                ve.tensor_tensor(gb, gb, pair(banks + 2), ALU.mult)
                ve.drain()
                ve.tensor_tensor(ga, ga, gb, ALU.add).then_inc(s["merged"], 1)

            for g in range(4):
                group_done(ve, N_WOUT + 4 * g + 3)
                part = x_tok[:, :, CN * g:CN * (g + 1)]
                ve.tensor_tensor(part, part, pair(2 * g), ALU.add).then_inc(s["wout_added"], 1)
            norm("ffn", x_tok, norm_tmp)

            def job(j, c_at):
                for c in range(4):
                    if c:
                        ve.drain()
                    ve.wait_ge(s[f"wmod_loaded{c}"], j * 16 + 16)
                    if c == 0:
                        ve.wait_ge(s["job_summed"], j + 1)
                    for k in range(CK):
                        col = c_vec[:, c_at + CK * c + k:c_at + CK * c + k + 1]
                        if c + k == 0:
                            op = ve.tensor_scalar(acc, wmod[:, c, k, :], col, None, ALU.mult)
                        else:
                            if k:
                                ve.drain()
                            op = ve.scalar_tensor_tensor(acc, wmod[:, c, k, :], col, acc, ALU.mult, ALU.add)
                    op.then_inc(s["wmod_used"], 1)
                ve.drain().then_inc(s["job_acc"], 1)

            def conv_sides(dst, bank, i, at_):
                for side in range(2):
                    for f in range(4):
                        ps = PS[:, bank + f // 2, (f % 2) * T:(f % 2) * T + T]
                        w = conv[:, bass.ds(i * 4 + (at_ + f), 1), 2 * side]
                        if side == 0:
                            o, src = dst[:, f, 1:T], ps[:, 0:T - 1]
                        else:
                            o, src = dst[:, f, 0:T - 1], ps[:, 1:T]
                        op = ve.scalar_tensor_tensor(o, src, w, o, ALU.mult, ALU.add)
                    if side == 0:
                        ve.drain()
                return op

            ve.wait_ge(s["c_ready"], 1)
            for name in ("up_g_free", "up_v_free", "hidden_ready"):
                ve.sem_inc(s[name], 1)
            for first, last, c_at in ((0, 4, 0), (4, 11, 16)):
                with ve.Fori(first, last) as i:
                    job(i * LOOP_JOBS, c_at)
                    ve.wait_ge(s["up_g_based"], i + 1)
                    conv_sides(conv_g, 0, i, 0).then_inc(s["up_g_free"], 1)
                    job(i * LOOP_JOBS + 1, c_at)
                    ve.wait_ge(s["up_v_based"], i + 1)
                    conv_sides(conv_v, 2, i, KF).then_inc(s["up_v_free"], 1)
                    ve.drain()
                    ve.wait_ge(s["up_g_act"], i + 1)
                    ve.tensor_tensor(hidden[:, bass.ds(i * 4, 4), :], conv_g[:], conv_v[:], ALU.mult)\
                        .then_inc(s["hidden_ready"], 1)

            ve.wait_ge(s["job_kept"], 1 + 11 * LOOP_JOBS)
            ve.tensor_tensor(mod[:, 0:32], mod[:, 0:32], b_mod[:, 0:32], ALU.add)
            ve.drain()
            ve.scalar_tensor_tensor(scale_c, mod[:, 16:32], 1.0, g_pre1, ALU.add, ALU.mult)\
                .then_inc(s["mod_ready"], 1)
            for g in range(4):
                for c in range(11):
                    for j in down_jobs(g, c):
                        job(j, 16)
                if g == 3:
                    norm("ctx", ctx_tok, norm_tmp_c)
                group_done(ve, N_DOWN + 11 * g + 10)
                part = x_tok[:, :, CN * g:CN * (g + 1)]
                ve.tensor_tensor(part, part, pair(2 * (g % 2)), ALU.add).then_inc(s["down_added"], 1)
            ve.wait_ge(s["job_kept"], 1 + JOBS)
            ve.tensor_tensor(mod[:, 32:128], mod[:, 32:128], b_mod[:, 0:96], ALU.add)
            ve.drain()
            ve.scalar_tensor_tensor(scale_x1, mod[:, 48:64], 1.0, g_pre1, ALU.add, ALU.mult)
            ve.scalar_tensor_tensor(scale_x2, mod[:, 96:112], 1.0, g_pre2, ALU.add, ALU.mult)\
                .then_inc(s["mod_ready"], 1)
            norm("mix2", x_tok, norm_tmp2)

            def log_decay(m):
                ve.wait_ge(s["la_exp"], m + 1)
                flat = la.rearrange("p a b c -> p (a b) c")
                ve.scalar_tensor_tensor(flat, PS[:, 4:8, :], 0.0, flat, ALU.min, ALU.subtract)
                ve.drain()
                ve.tensor_scalar(flat, flat, 1.0 / TAU, None, ALU.mult).then_inc(s["la_ready"], 1)

            log_decay(0)
            ve.wait_ge(s["rem_exp"], 1)
            ve.wait_ge(s["ctx_kept"], 1)
            for r, k in ((0, e_buf), (1, qe)):
                ve.tensor_tensor(k[:], k[:], kc_tok[:], ALU.mult).then_inc(s["kdec_ready"], 1)

            lv, taken, diffs, levels = 0, 0, 0, []
            ve.wait_ge(s["masks_loaded"], 32)

            def take(upto):
                nonlocal taken
                while taken < upto:
                    ve.wait_ge(s["lv_done"], taken + 1)
                    l = levels[taken]
                    mask = bc(level_mask[:, l, :].unsqueeze(1), [P, GH, P]).bitcast(I32)
                    ps = PS[:, 4 + taken % 2, :].rearrange("p (h i) -> p h i", i=P)
                    ve.copy_predicated(s_t[:], mask, ps).then_inc(s["lv_taken"], 1)
                    ve.drain()
                    taken += 1

            for item in sched:
                if item[0] == "la":
                    log_decay(1)
                elif item[0] == "rem":
                    r = item[1]
                    ve.wait_ge(s["rem_exp"], 2 + r)
                    ve.tensor_tensor(e_buf[:, r, :], e_buf[:, r, :], k_tok[:, r, :], ALU.mult)\
                        .then_inc(s["kdec_ready"], 1)
                elif item[0] == "upd":
                    r = item[1]
                    ve.wait_ge(s["state_done"], 3 + r)
                    ve.wait_ge(s["decay_ready"], r + 1)
                    for hd in range(GH):
                        op = ve.scalar_tensor_tensor(state[:, r, 1, hd * T:(hd + 1) * T],
                                                     state[:, r, 0, hd * T:(hd + 1) * T],
                                                     decay[:, 4 * r + hd:4 * r + hd + 1],
                                                     PS[:, 4 + 2 * r + hd // 2, (hd % 2) * T:(hd % 2) * T + T],
                                                     ALU.mult, ALU.add)
                    op.then_inc(s["state_ready"], 1)
                    if r == 1:
                        ve.memset(s_t[:], 0.0)
                elif item[0] == "qe":
                    n = item[1]
                    ve.wait_ge(s["qe_exp"], n + 1)
                    ve.wait_ge(s["grp_free"], 2)
                    qe4 = qe.rearrange("p r (h i) -> p r h i", i=P)
                    for r in range(2):
                        op = ve.tensor_tensor(qe4[:, r], qe4[:, r], q_t[:, :, n * P:(n + 1) * P], ALU.mult)
                    op.then_inc(s["qe_ready"], 1)
                elif item[0] == "level":
                    _, n, l = item
                    q = q_t[:, :, n * P:(n + 1) * P]
                    e = e_buf[:, lv % 2, :]
                    ql3 = ql[:, lv % 2, :].rearrange("p (h i) -> p h i", i=P)
                    if l < 14:
                        r, size = l // 7, LEVELS[l % 7]
                        if lv >= 2:
                            ve.wait_ge(s["lv_k"], lv - 1)
                        else:
                            ve.wait_ge(s["cum_kept"], 1)
                        b = b_t[:, n, r, :].rearrange("p (m t) -> p m t", t=2 * size)
                        ref = b[:, :, size - 1 + r:size + r]
                        ve.tensor_tensor(e.rearrange("p (m t) -> p m t", t=2 * size), b,
                                         bc(ref, [P, 256 // size, 2 * size]), ALU.subtract).then_inc(s["lv_diff"], 1)
                        diffs += 1
                        ve.wait_ge(s["lv_exp"], diffs)
                        if lv >= 2:
                            ve.wait_ge(s["lv_done"], lv - 1)
                        ve.tensor_tensor(ql3, e.rearrange("p (h i) -> p h i", i=P), q, ALU.mult)\
                            .then_inc(s["lv_q"], 1)
                    else:
                        ve.wait_ge(s["lv_done"], lv - 1)
                        ve.tensor_scalar(ql3, q, 2.0, None, ALU.mult).then_inc(s["lv_q"], 1)
                    levels.append(l)
                    lv += 1
                    if n == 1 and l == 0:
                        ve.wait_ge(s["o_done"], 1)
                    take(lv - 2 if l >= 2 else lv - l)
                elif item[0] == "o":
                    n = item[1]
                    take(15 * (n + 1))
                    ve.wait_ge(s["o_sq"], n + 1)
                    ve.tensor_reduce(ss[:, 0:4], y_tok.rearrange("p (h e) -> p h e", e=T), AX, ALU.add)\
                        .then_inc(s["o_sum"], 1)
                    ve.wait_ge(s["o_rs"], n + 1)
                    ve.tensor_tensor(y_tok.rearrange("p (h e) -> p h e", e=T),
                                     PS[:, 6:8, :].rearrange("p a (b e) -> p (a b) e", e=T),
                                     bc(rs[:, 0:4].unsqueeze(2), [P, 4, T]), ALU.mult).then_inc(s["y_ready"], 1)
                elif item[0] == "y":
                    n = item[1]
                    ve.wait_ge(s["y_turned"], n + 1)
                    ve.wait_ge(s["grp_free"], 6)
                    for f in range(8):
                        c = cat_t[:, 8 + f, n * P:(n + 1) * P]
                        op = ve.scalar_tensor_tensor(c, PS[:, 6 + f // 4, (f % 4) * P:(f % 4 + 1) * P],
                                                     out_g[:, f:f + 1], c, ALU.mult, ALU.mult)
                    op.then_inc(s["y_kept"], 1)
                elif item[0] == "post" and item[1] >= 8:
                    m = item[1] - 8
                    v3 = v_sgu.rearrange("p (n d) -> p n d", d=HD)
                    ve.wait_ge(s["grp_free"], 9 + m)
                    ve.tensor_reduce(mean[:, 0:8], v3, AX, ALU.add)
                    ve.drain()
                    ve.tensor_scalar(mean[:, 0:8], mean[:, 0:8], -1.0 / HD, None, ALU.mult)
                    ve.drain()
                    ve.tensor_tensor(v3, v3, bc(mean[:, 0:8].unsqueeze(2), [P, 8, HD]), ALU.add)\
                        .then_inc(s["sgu_centred"], 1)
                    ve.wait_ge(s["sgu_sq"], m + 1)
                    ve.tensor_reduce(ss[:, 8:16], v_tmp.rearrange("p (n d) -> p n d", d=HD), AX, ALU.add)\
                        .then_inc(s["sgu_var"], 1)
                    ve.wait_ge(s["sgu_rs"], m + 1)
                    ve.tensor_tensor(v3, v3, bc(rs[:, 8:16].unsqueeze(2), [P, 8, HD]), ALU.mult)\
                        .then_inc(s["sgu_ready"], 1)
                elif item[0] == "sgu":
                    m = item[1]
                    ve.wait_ge(s["sgu_mixed"], m + 1)
                    ve.wait_ge(s["bs_loaded"], 16)
                    for hd in range(4):
                        hh = 4 * m + hd
                        ve.scalar_tensor_tensor(s_t[:, hd, :], PS[:, 6, hd * P:(hd + 1) * P], ln_b[:, hh:hh + 1],
                                                bs_bc[:, hh, :], ALU.mult, ALU.add)
                    ve.drain()
                    mixed = v_tmp.rearrange("p (h n i) -> p h n i", n=2, i=P)
                    for n in range(2):
                        for hd in range(4):
                            hh = 4 * m + hd
                            ve.scalar_tensor_tensor(mixed[:, hd, n, :], PS[:, 4 + n, hd * P:(hd + 1) * P],
                                                    ln_g[:, hh:hh + 1], s_t[:, hd, :], ALU.mult, ALU.add)
                    ve.drain()
                    u_part = cat_t[:, 4 * m:4 * m + 4, :].rearrange("p h t -> p (h t)")
                    ve.tensor_tensor(u_part, u_part, v_tmp, ALU.mult).then_inc(s["sgu_kept"], 1)

            def post(m, gate, g_post):
                ve.tensor_tensor(gate_col, gate, g_post, ALU.mult)
                ve.drain()
                for j in range(4):
                    if m == 0 and j == 0:
                        group_done(ve, N_WOUT2 + 3)
                    if j or m:
                        ve.wait_ge(s["post_bc"], 4 * m + j)
                    for f in range(4):
                        op = ve.tensor_scalar(gate_w[:, f, :], ones[:], gate_col[:, 4 * j + f:4 * j + f + 1], None,
                                              ALU.mult)
                    op.then_inc(s["post_w"], 1)
                ve.wait_ge(s["post_bc_kept"], 4 * m + 4)
                ve.wait_ge(s["post_rs"], m + 1)
                for h in range(2):
                    ve.scalar_tensor_tensor(mix_out[:, h, :], mix_out[:, h, :], norm_rs[:, h:h + 1], gate_bc,
                                            ALU.mult, ALU.mult)
                    ve.drain()
                    ve.tensor_tensor(x_tok[:, h, :], x_tok[:, h, :], mix_out[:, h, :], ALU.add)\
                        .then_inc(s["post_added"], 1)

            post(0, mod[:, 64:80], g_post1)
            norm("ffn2", x_tok, norm_tmp)

            ve.sem_inc(s["hidden2_ready"], 1)
            with ve.Fori(0, 11) as i:
                ve.wait_ge(s["up2_g_free"], i + 2)
                group_done(ve, i * 8 + (N_UP2 + 7))
                ve.tensor_tensor(hidden[:, bass.ds(i * 4, 4), :].rearrange("p (a b) t -> p a (b t)", a=2),
                                 conv_g.rearrange("p (a b) t -> p a (b t)", a=2), pair(2), ALU.mult)\
                    .then_inc(s["hidden2_ready"], 1)
            post(1, mod[:, 112:128], g_post2)

        @block.scalar
        def _(act):
            def norm_stats(src, junk):
                for h in range(2):
                    act.activation(junk, src[:, h, :], ACT.Square, accum_out=norm_ss[:, h:h + 1])
                    act.drain()
                act.activation(norm_rs, norm_ss, ACT.Ln, scale=1.0 / D, bias=eps_col)
                act.drain()
                return act.activation(norm_rs, norm_rs, ACT.Exp, scale=-0.5)

            def norm(key, src, tmp_, dst, gain, shift):
                n = norm_sems[key]
                norm_stats(src, tmp_.rearrange("p a b c -> p (a b c)")).then_inc(n["rstd"], 1)
                norm_keep(key, dst, gain, shift)

            def norm_keep(key, dst, gain, shift):
                n = norm_sems[key]
                for j in range(8):
                    act.wait_ge(n["turned"], j + 1)
                    for m in range(2):
                        kt = 2 * j + m
                        bias_ = 0.0 if shift is None else shift[:, kt:kt + 1]
                        op = act.activation(dst[:, kt, :], PS[:, 4 + j % 2, m * T:(m + 1) * T], ACT.Identity,
                                            scale=gain[:, kt:kt + 1], bias=bias_)
                    op.then_inc(n["kept"], 1)

            for dst, src in consts:
                act.dma_start(dst, src).then_inc(s["consts_loaded"], 16)
            act.wait_ge(s["consts_loaded"], 16 * N_CONSTS)
            act.wait_ge(s["setup_done"], 1)
            act.activation(c_vec, c_vec, ACT.Silu).then_inc(s["c_ready"], 1)
            act.wait_ge(s["x_loaded"], 32)
            norm("mix", x_tok, norm_tmp, act_t, g_mix, None)

            def pair(bank, width=512):
                return PS[:, bank:bank + 2, 0:width]

            for g, kind in enumerate(NORMED):
                heads = 2 if kind == "kv" else 4
                w = heads * HD
                group_done(act, N_PROJ + 4 * g + 3)
                if g:
                    act.wait_ge(s["proj_free"], g)
                act.activation(tmp[0][:, 0:2 * w].rearrange("p (h w) -> p h w", h=2), pair(2 * (g % 2), w),
                               ACT.Square).then_inc(s["squared"], 1)
                act.wait_ge(s["summed"], g + 1)
                act.activation(rs[:, 0:2 * heads], ss[:, 0:2 * heads], ACT.Ln, scale=1.0 / HD, bias=eps_col)
                act.drain()
                act.activation(rs[:, 0:2 * heads], rs[:, 0:2 * heads], ACT.Exp, scale=-0.5)\
                    .then_inc(s["rstd_ready"], 1)
                act.wait_ge(s["turned"], g + 1)
                dst = {"qa0": qa_t[:, 0:4], "qa1": qa_t[:, 4:8], "kv": ka_t[:], "qb0": qb_t[:, 0:4],
                       "qb1": qb_t[:, 4:8], "kb0": kb_t[:, 0:4], "kb1": kb_t[:, 4:8]}[kind]
                dst = dst.rearrange("p n t -> p (n t)")
                src = PS[:, 4:6, :].rearrange("p a b -> p (a b)")[:, 0:heads * T]
                if kind[1] == "b":
                    op = act.activation(dst, src, ACT.Copy, scale=bq_norm if kind[0] == "q" else bk_norm)
                else:
                    op = act.copy(dst, src)
                op.then_inc(s["qkv_kept"], 1)

            act.wait_ge(s["proj_free"], 9)
            act.sem_inc(s["gate_kept"], 1)
            with act.Fori(0, 4) as i:
                for u in range(2):
                    done = i * 2 + u
                    act.wait_ge(s["max_ready"], done + 1)
                    for n, sc in ((0, score_a), (1, score_b)):
                        for b in range(2):
                            at_ = 2 * n + b
                            act.activation(sc[:, b, :], sc[:, b, :], ACT.Exp, bias=mx[:, 4 + at_:5 + at_],
                                           accum_out=den[:, at_:at_ + 1])
                    for b in range(2):
                        op = act.activation(den[:, 4 + b:5 + b], sink[:, bass.ds(i * 2 + u, 1)], ACT.Exp,
                                            bias=mx[:, 4 + b:5 + b])
                    op.then_inc(s["exps_done"], 1)
                    act.wait_ge(s["probs_turned"], done + 1)
                    act.copy(pt_a[:], PS[:, 6, :].rearrange("p (k t) -> p k t", t=T))
                    act.copy(pt_b[:], PS[:, 7, :].rearrange("p (k t) -> p k t", t=T)).then_inc(s["probs_t_ready"], 1)
                    act.wait_ge(s["attn_done"], done + 2)
                    act.copy(oa_t[:, done, :], PS[:, 2, 0:T])
                    act.copy(ob_t[:, done, :], PS[:, 3, 0:T]).then_inc(s["attn_kept"], 1)
                    group_done(act, i * 8 + (N_GATE + 4 * u + 3))
                    act.copy(gates[:, bass.ds(i * 8 + 4 * u, 4), :].rearrange("p (a b) t -> p a (b t)", a=2),
                             pair(0)).then_inc(s["gate_kept"], 1)
            act.drain()
            for g in range(4):
                for first in (0, 16):
                    ga = gates[:, first + 4 * g:first + 4 * g + 4, :]
                    op = act.activation(ga, ga, ACT.Sigmoid)
                op.then_inc(s["gates_squashed"], 1)

            act.wait_ge(s["wout_added"], 4)
            norm("ffn", x_tok, norm_tmp, act_t, g_ffn, None)

            def conv_base(dst, bank, i, at_):
                for f in range(4):
                    w = conv[:, bass.ds(i * 4 + (at_ + f), 1), :]
                    op = act.activation(dst[:, f, :], PS[:, bank + f // 2, (f % 2) * T:(f % 2) * T + T],
                                        ACT.Identity, scale=w[:, 0, 1:2], bias=w[:, 0, 3:4])
                return op

            def keep_job(j):
                act.wait_ge(s["job_summed"], j + 2)
                act.copy(mod[:, bass.ds(j * 4, 4)] if not isinstance(j, int) else mod[:, 4 * j:4 * j + 4],
                         PS[:, 6, 0:4]).then_inc(s["job_kept"], 1)

            act.sem_inc(s["job_kept"], 1)
            with act.Fori(0, 11) as i:
                act.wait_ge(s["hidden_ready"], i + 1)
                group_done(act, i * 8 + (N_UP + 3))
                conv_base(conv_g, 0, i, 0).then_inc(s["up_g_based"], 1)
                act.wait_ge(s["up_g_free"], i + 2)
                act.activation(conv_g[:], conv_g[:], ACT.Silu).then_inc(s["up_g_act"], 1)
                keep_job(i * LOOP_JOBS)
                group_done(act, i * 8 + (N_UP + 7))
                conv_base(conv_v, 2, i, KF).then_inc(s["up_v_based"], 1)
                keep_job(i * LOOP_JOBS + 1)

            act.wait_ge(s["hidden_ready"], 12)
            for g in range(4):
                if g == 2:
                    act.wait_ge(s["mod_ready"], 1)
                    act.wait_ge(s["ctx_loaded"], 32)
                    norm_stats(ctx_tok, norm_tmp_c.rearrange("p a b c -> p (a b c)"))\
                        .then_inc(norm_sems["ctx"]["rstd"], 1)
                for c in range(11):
                    for j in down_jobs(g, c):
                        keep_job(j)
                    if g == 3 and c == 3:
                        norm_keep("ctx", act_t, scale_c, mod[:, 0:16])
            act.wait_ge(s["down_added"], 4)
            act.wait_ge(s["mod_ready"], 2)
            norm_stats(x_tok, norm_tmp2[:, 0:4].rearrange("p a b c -> p (a b c)"))\
                .then_inc(norm_sems["mix2"]["rstd"], 1)

            def keep_d(m):
                act.wait_ge(s["d_done"], m + 1)
                act.copy(d_t[0:2 * RANK, :], PS[0:2 * RANK, 7, 0:T]).then_inc(s["d_kept"], 1)

            def log_decay(m):
                flat = la.rearrange("p a b c -> p (a b) c")
                act.wait_ge(s["la_done"], m + 1)
                act.activation(flat, PS[:, 4:8, :], ACT.Abs)
                act.drain()
                act.activation(flat, flat, ACT.Exp, scale=-1.0)
                act.drain()
                act.activation(flat, flat, ACT.Ln, bias=one_col).then_inc(s["la_exp"], 1)

            keep_d(0)
            log_decay(0)
            group_done(act, N_CTX + 3)
            act.copy(kc_tok[:], pair(0)).then_inc(s["ctx_kept"], 1)
            act.wait_ge(s["rem_done"], 1)
            act.activation(e_buf[:], PS[:, 4:6, :], ACT.Exp)
            act.activation(qe[:], PS[:, 6:8, :], ACT.Exp).then_inc(s["rem_exp"], 1)
            norm_keep("mix2", hx_t, scale_x1, mod[:, 32:48])
            for m in range(2):
                group_done(act, N_CTX + 4 * m + 7)
                act.copy(vvc[:, :, 512 * m:512 * (m + 1)], pair(2 - 2 * m)).then_inc(s["ctx_kept"], 1)
            for r in range(2):
                act.wait_ge(s["state_done"], r + 1)
                act.copy(state[:, r, 0, :].rearrange("p (a b) -> p a b", a=2), pair(4 + 2 * r))\
                    .then_inc(s["state_ready"], 1)

            lv = 0
            for item in sched:
                if item[0] == "post":
                    g = item[1]
                    kind = MIX_GROUPS[g][0]
                    bank = 2 * (g % 2)
                    group_done(act, N_MIX + 4 * g + 3)
                    feat = lambda n: cat_t[:, n:n + 4, :].rearrange("p (a b) t -> p a (b t)", a=2)
                    if kind == "k":
                        op = act.copy(k_tok[:], pair(bank))
                    elif kind == "q":
                        op = act.activation(q_t.rearrange("p (a b) t -> p a (b t)", a=2), pair(bank), ACT.Copy,
                                            scale=float(HD) ** -0.5)
                    elif kind[:2] == "vv":
                        m = int(kind[2])
                        op = act.copy(vv[:, :, 512 * m:512 * (m + 1)], pair(bank))
                    elif kind[0] == "u":
                        op = act.activation(feat(4 * int(kind[1])), pair(bank), ACT.Gelu_apprx_tanh)
                    elif kind[0] == "g":
                        op = act.activation(feat(8 + 4 * int(kind[1])), pair(bank), ACT.Silu)
                    else:
                        if kind == "v1":
                            act.wait_ge(s["sgu_kept"], 1)
                        op = act.activation(v_sgu.rearrange("p (a b) -> p a b", a=2), pair(bank),
                                            ACT.Gelu_apprx_tanh)
                    op.then_inc(s["grp_free"], 1)
                    if kind in ("v0", "v1"):
                        m = int(kind[1])
                        act.wait_ge(s["sgu_centred"], m + 1)
                        act.activation(v_tmp, v_sgu, ACT.Square).then_inc(s["sgu_sq"], 1)
                        act.wait_ge(s["sgu_var"], m + 1)
                        act.activation(rs[:, 8:16], ss[:, 8:16], ACT.Ln, scale=1.0 / HD, bias=eps_col)
                        act.drain()
                        act.activation(rs[:, 8:16], rs[:, 8:16], ACT.Exp, scale=-0.5).then_inc(s["sgu_rs"], 1)
                elif item[0] == "d":
                    keep_d(1)
                elif item[0] == "la":
                    log_decay(1)
                elif item[0] == "kt":
                    act.wait_ge(s["kt_done"], 1)
                    act.copy(k_t.rearrange("p (a b) t -> p a (b t)", a=2), pair(4)).then_inc(s["kt_kept"], 1)
                elif item[0] == "cum":
                    act.wait_ge(s["cum_done"], 1)
                    act.copy(b_t.rearrange("p a b c -> p (a b) c"), PS[:, 4:8, :]).then_inc(s["cum_kept"], 1)
                elif item[0] == "wst":
                    act.wait_ge(s["ws_turned"], 1)
                    act.copy(ws_t.rearrange("p (a b) i -> p a (b i)", a=2), pair(4)).then_inc(s["ws_kept"], 1)
                elif item[0] == "rem":
                    r = item[1]
                    act.wait_ge(s["rem_done"], 2 + r)
                    act.activation(e_buf[:, r, :], PS[:, 6 + r, :], ACT.Exp).then_inc(s["rem_exp"], 1)
                elif item[0] == "upd":
                    r = item[1]
                    edge = HD - 1 if r == 0 else 0
                    act.activation(decay[:, 4 * r:4 * r + 4], b_t[:, r, r, edge:512:HD], ACT.Exp)\
                        .then_inc(s["decay_ready"], 1)
                elif item[0] == "qe":
                    n = item[1]
                    if n:
                        act.wait_ge(s["y_turned"], 1)
                    act.activation(qe[:], b_t[:, n], ACT.Exp).then_inc(s["qe_exp"], 1)
                elif item[0] == "level" and item[2] < 14:
                    lv += 1
                    act.wait_ge(s["lv_diff"], lv)
                    e = e_buf[:, (lv - 1 + (item[1])) % 2, :]
                    act.activation(e, e, ACT.Abs)
                    act.drain()
                    act.activation(e, e, ACT.Exp, scale=-1.0).then_inc(s["lv_exp"], 1)
                elif item[0] == "o":
                    n = item[1]
                    act.wait_ge(s["o_done"], n + 1)
                    act.activation(y_tok.rearrange("p (a b) -> p a b", a=2), PS[:, 6:8, :], ACT.Square)\
                        .then_inc(s["o_sq"], 1)
                    act.wait_ge(s["o_sum"], n + 1)
                    act.activation(rs[:, 0:4], ss[:, 0:4], ACT.Ln, scale=1.0 / T, bias=eps_col)
                    act.drain()
                    act.activation(rs[:, 0:4], rs[:, 0:4], ACT.Exp, scale=-0.5).then_inc(s["o_rs"], 1)

            def post(m, n0, chunks, kept):
                for g in range(4):
                    group_done(act, n0 + chunks * (g + 1) - 1)
                    op = act.copy(mix_out[:, :, CN * g:CN * (g + 1)], pair(2 * g))
                op.then_inc(s[kept], 1)
                act.drain()
                norm_stats(mix_out, norm_tmp.rearrange("p a b c -> p (a b c)")).then_inc(s["post_rs"], 1)
                for j in range(4):
                    act.wait_ge(s["post_bc"], 4 * m + j + 1)
                    act.copy(gate_bc[:, CN * j:CN * (j + 1)], PS[:, 0, :]).then_inc(s["post_bc_kept"], 1)

            post(0, N_WOUT2, 4, "wout2_kept")
            act.wait_ge(s["post_added"], 2)
            norm("ffn2", x_tok, norm_tmp, act_t, scale_x2, mod[:, 80:96])
            act.sem_inc(s["up2_g_free"], 1)
            with act.Fori(0, 11) as i:
                act.wait_ge(s["hidden2_ready"], i + 1)
                group_done(act, i * 8 + (N_UP2 + 3))
                act.activation(conv_g.rearrange("p (a b) t -> p a (b t)", a=2), pair(0), ACT.Silu)\
                    .then_inc(s["up2_g_free"], 1)
            post(1, N_DOWN2, 11, "down2_kept")

        @block.gpsimd
        def _(pool):
            pool.memset(ones[:], 1.0)
            pool.memset(eps_col, EPS)
            pool.memset(one_col, 1.0)
            pool.memset(rpb, 0.0)
            pool.drain().then_inc(s["setup_done"], 1)
            pool.wait_ge(s["setup_done"], 1)
            for h in range(8):
                pool.dma_start(rpb[7 * h:7 * h + 7, 48:79], a["b_rpb"][h, 4:11, :]).then_inc(s["rpb_loaded"], 16)
            pool.wait_ge(s["rpb_loaded"], 128)
            src = bc(rpb[:, 0:P - 1].unsqueeze(1), [56, GRID, P - 1])
            pool.dma_start(skew.rearrange("r (q c) -> r q c", c=P)[:, :, 0:P - 1], src).then_inc(s["skew_written"], 16)
            pool.wait_ge(s["skew_written"], 16)
            pool.wait_ge(s["consts_loaded"], 16 * N_CONSTS)
            pool.wait_ge(s["proj_free"], 9)
            pool.wait_ge(s["qkv_kept"], 7)
            with pool.Fori(0, 4) as i:
                for u in range(2):
                    done = i * 2 + u
                    pool.wait_ge(s["bias_used"], done + 1)
                    for qr in range(4):
                        src = bass.AP(skew.tensor, i * (2 * 7 * 64 * P) + (u * 7 + 3 - qr) * 64 * P + GRID - 1,
                                      [[P - 1, GRID], [64 * P, 4], [1, GRID]])
                        dst = bias[(qr % 2) * GRID:(qr % 2 + 1) * GRID, qr // 2, :]
                        pool.dma_start(dst.rearrange("p (r c) -> p r c", c=GRID), src).then_inc(s["bias_loaded"], 16)
                    pool.wait_ge(s["attn_done"], done + 1)
                    pool.tensor_copy(q_head[0], qa_t[:, done, :])
                    pool.tensor_copy(q_head[1], qb_t[:, done, :])
                    pool.tensor_copy(v_head[0][:], va[:, :, bass.ds(i // 2 * P, P)])
                    pool.tensor_copy(v_head[1][:], vb[:, :, bass.ds(i * (2 * P) + u * P, P)])
                    pool.drain().then_inc(s["head_staged"], 1)

            def load_job(j, cols):
                for c in range(4):
                    pool.wait_ge(s["wmod_used"], j * 4 + (c + 1))
                    pool.dma_start(wmod[:, c, :, :], w_mod[:, CK * c:CK * c + CK, cols])\
                        .then_inc(s[f"wmod_loaded{c}"], 16)

            pool.wait_ge(norm_sems["ffn"]["kept"], 8)
            for h in range(2):
                pool.dma_start(ctx_tok[:, h, :], a["ctx_2"][h * P:(h + 1) * P, :]).then_inc(s["ctx_loaded"], 16)
            pool.sem_inc(s["wmod_used"], 4)
            with pool.Fori(0, 4) as i:
                for u in range(2):
                    load_job(i * 2 + u, bass.ds(i * (2 * CN) + u * CN, CN))
            with pool.Fori(4, 11) as i:
                for u in range(2):
                    load_job(i * 2 + u, bass.ds(i * (2 * CN) + (u - 8) * CN, CN))
            for j in range(22, JOBS):
                load_job(j, slice((j - 8) * CN, (j - 7) * CN))
            pool.wait_ge(norm_sems["ctx"]["turned"], 8)
            pool.wait_ge(s["job_kept"], 1 + JOBS)
            pool.memset(wd2, 0.0)
            pool.drain().then_inc(s["setup_done"], 1)
            pool.wait_ge(s["setup_done"], 2)
            for row, n, col, name in ((0, RANK, 0, "gla_wd2_fwd_2"), (RANK, RANK, 512, "gla_wd2_bwd_2"),
                                      (2 * RANK, 1, 0, "gla_bd_fwd_2"), (2 * RANK, 1, 512, "gla_bd_bwd_2")):
                pool.dma_start(wd2[row:row + n, col:col + 512], a[name]).then_inc(s["wd2_loaded"], 16)
            pool.dma_start(tri[:], a["t_tri"]).then_inc(s["masks_loaded"], 16)
            pool.dma_start(level_mask[:], a["t_levels"]).then_inc(s["masks_loaded"], 16)
            group_done(pool, N_CTX + 11)
            pool.dma_start(v_sgu.rearrange("p (h j) -> p h j", j=P), a["gmlp_ws_2"].rearrange("h i j -> i h j"))\
                .then_inc(s["mixer_loaded"], 16)
            pool.dma_start(bs_bc.rearrange("p h i -> p (h i)"),
                           bass.AP(a["gmlp_bs_2"].tensor, 0, [[0, P], [1, 1024]])).then_inc(s["bs_loaded"], 16)
            lv = 0
            pool.wait_ge(s["kt_kept"], 1)
            for item in sched:
                if item[0] != "level":
                    continue
                _, n, l = item
                keys = k_t[:, :, n * P:(n + 1) * P]
                dst = kl[:, lv % 2, :].rearrange("p (h i) -> p h i", i=P)
                if lv >= 2:
                    pool.wait_ge(s["lv_done"], lv - 1)
                if l < 14:
                    pool.wait_ge(s["lv_exp"], lv + 1 - n)
                    pool.tensor_tensor(dst, keys, e_buf[:, lv % 2, :].rearrange("p (h i) -> p h i", i=P), ALU.mult)\
                        .then_inc(s["lv_k"], 1)
                else:
                    pool.tensor_copy(dst, keys).then_inc(s["lv_k"], 1)
                lv += 1


WEIGHTS = ["w_in", "w_branch_a", "w_branch_b", "w_out", "w_up", "w_down", "w_mod_2", "w_in_2", "w_out_2",
           "w_ffn_in_2", "w_ffn_out_2"]
FEATURE_MAJOR = {"norm_mix": 16, "norm_ffn": 16, "g_pre_mix_2": 16, "g_post_mix_2": 16, "g_pre_ffn_2": 16,
                 "g_post_ffn_2": 16, "b_mod_2": 96, "c_2": 16, "c_ctx_2": 16, "b_q_norm": 1, "b_k_norm": 1,
                 "gla_out_g_2": 8, "gmlp_ln_g_2": 8, "gmlp_ln_b_2": 8}
ROWS = ["gla_wd2_fwd_2", "gla_wd2_bwd_2", "gla_bd_fwd_2", "gla_bd_bwd_2", "a_q_norm", "a_k_norm", "a_sink"]


def kernel(**inputs):
    import numpy as _np
    import concourse.bacc as _bacc
    from concourse import mybir as _mybir
    from concourse.bass_utils import run_bass_kernel_spmd as _run

    get = lambda n: _np.asarray(inputs[n])
    laid = {n: get(n)[0] for n in WEIGHTS}
    laid["x"], laid["ctx_2"] = get("x")[0], get("ctx_2")[0]
    for n, cols in FEATURE_MAJOR.items():
        laid[n] = get(n).reshape(cols, P).T
    for n in ROWS:
        laid[n] = get(n).reshape(-1, get(n).shape[-1])
    laid["b_rpb"], laid["gmlp_ws_2"], laid["gmlp_bs_2"] = get("b_rpb")[0], get("gmlp_ws_2")[0], get("gmlp_bs_2")[0]
    conv = _np.concatenate([get("conv_w")[0], get("conv_b")], 0)
    laid["conv"] = conv.reshape(4, 2 * KF, P).transpose(2, 1, 0)
    decay_cols = laid["w_in_2"][:, -2 * RANK:]
    laid["w_decay"] = decay_cols.reshape(KD, P, 2 * RANK).transpose(1, 0, 2)
    laid.update(host_tables())

    nc = _bacc.Bacc("TRN2", target_bir_lowering=False, num_devices=1)
    arrays, args = {}, {}
    for name, arr in laid.items():
        arr = _np.ascontiguousarray(arr)
        arrays[f"in_{name}"] = arr
        args[name] = nc.dram_tensor(f"in_{name}", arr.shape, _mybir.dt.from_np(arr.dtype), kind="ExternalInput").ap()
    out = nc.dram_tensor("out", (T, D), F32, kind="ExternalOutput").ap()
    build(nc, args, out)
    r = _run(nc, [arrays], core_ids=[0])
    return r.results[0]["out"].reshape(1, T, D)
```

```python
import math
from contextlib import ExitStack

import numpy as np

import concourse.bass as bass
from concourse import mybir

F32 = mybir.dt.float32
I32 = mybir.dt.int32
ALU = mybir.AluOpType
ACT = mybir.ActivationFunctionType
AX = mybir.AxisListType.X

P = 128
T = 256
D = 2048
KD = D // P
HD = 128
FF = 5632
KF = FF // P
EPS = 1e-6
NEG = -1e30
GRID = 64
TAU = 16.0
GH = 4
RANK = 16

CK, CN = 4, 512
CHUNK = CK * CN
SLOTS = 8
LEVELS = [64, 32, 16, 8, 4, 2, 1]

N_PROJ = 0
N_GATE = N_PROJ + 9 * 4
N_BRANCH = N_GATE + 8 * 4
N_WOUT = N_BRANCH + 4 * 4
N_UP = N_WOUT + 4 * 4
N_DOWN = N_UP + 22 * 4
N_CTX = N_DOWN + 4 * 11
N_MIX = N_CTX + 3 * 4
N_WOUT2 = N_MIX + 10 * 4
N_UP2 = N_WOUT2 + 4 * 4
N_DOWN2 = N_UP2 + 22 * 4

JOBS = 32
LOOP_JOBS = 2


def host_tables():
    half = HD // 2
    inv = np.float32(10000.0) ** (-np.arange(half, dtype=np.float32) * np.float32(2.0 / HD))
    ang = np.arange(T, dtype=np.float32)[:, None] * inv[None, :].astype(np.float32)
    cos, sin = np.cos(ang), np.sin(ang)
    cos2 = np.concatenate([cos, cos], 1).reshape(2, P, HD).transpose(1, 0, 2)
    sin2 = np.concatenate([-sin, sin], 1).reshape(2, P, HD).transpose(1, 0, 2)
    q, k = np.arange(T)[:, None], np.arange(T)[None, :]
    mask_a = np.where(np.abs(q - k) <= 128, 0.0, NEG).reshape(2, P, T).transpose(1, 0, 2)
    qc, kc = np.arange(P)[:, None] % GRID, np.arange(T)[None, :] % GRID
    cs = np.clip(qc - 8, 0, GRID - 16)
    mask_b = np.where((kc >= cs) & (kc < cs + 16), 0.0, NEG)
    t, i = np.arange(P)[:, None], np.arange(P)[None, :]
    tri = np.stack([t <= i, t >= i, t > i, t < i], 1)
    levels = []
    for s in LEVELS:
        levels.append((t // (2 * s) == i // (2 * s)) & ((t % (2 * s) < s) != (i % (2 * s) < s)))
    levels += [t == i]
    levels = np.stack(levels, 1)
    c = lambda a: np.ascontiguousarray(a, dtype=np.float32)
    return {"t_ident": c(np.eye(P)), "t_cos": c(cos2), "t_sin": c(sin2), "t_mask_a": c(mask_a),
            "t_mask_b": c(mask_b), "t_tri": c(tri), "t_levels": c(levels)}


def build(nc, a, out):
    with ExitStack() as ctx:
        def sb(name, words):
            return ctx.enter_context(nc.sbuf_tensor(name, [P, words], F32))

        def sem(name):
            return ctx.enter_context(nc.semaphore(name))

        ring = ctx.enter_context(nc.sbuf_tensor("ring", [P, SLOTS, CK, CN], F32))
        x_tok = ctx.enter_context(nc.sbuf_tensor("x_tok", [P, 2, D], F32))
        act_t = ctx.enter_context(nc.sbuf_tensor("act_t", [P, KD, T], F32))
        big = sb("big", KF * T)
        mid = sb("mid", 15360)
        ident = sb("ident", P)
        ones = sb("ones", P)
        small = sb("small", 888)
        PS = ctx.enter_context(nc.psum_tensor("PS", [P, 8, 512], F32))

        def cut(tile, at, *shape):
            n = int(np.prod(shape))
            v = tile[:, at:at + n]
            if len(shape) == 2:
                return v.rearrange("p (a b) -> p a b", b=shape[1])
            if len(shape) == 3:
                return v.rearrange("p (a b c) -> p a b c", b=shape[1], c=shape[2])
            if len(shape) == 4:
                return v.rearrange("p (a b c d) -> p a b c d", b=shape[1], c=shape[2], d=shape[3])
            return v

        at = [0]

        def little(n):
            at[0] += n
            return small[:, at[0] - n:at[0]]

        g_mix, g_ffn = little(16), little(16)
        g_pre1, g_post1, g_pre2, g_post2 = little(16), little(16), little(16), little(16)
        b_mod = little(96)
        mod = little(128)
        c_vec = little(32)
        sink = little(8)
        bq_norm, bk_norm = little(1), little(1)
        conv = little(4 * 88).rearrange("p (f k) -> p f k", k=4)
        out_g, ln_g, ln_b = little(8), little(8), little(8)
        ss, rs = little(16), little(16)
        norm_ss, norm_rs = little(2), little(2)
        gate_col = little(16)
        part_ss = little(8)
        mx = little(8)
        den = little(8)
        mean = little(8)
        decay = little(8)
        zero_col = little(1)
        eps_col = little(1)
        one_col = little(1)
        scale_c, scale_x1, scale_x2 = little(16), little(16), little(16)
        assert at[0] <= 888

        qa_t, ka_t, va = cut(big, 0, 8, T), cut(big, 2048, 2, T), cut(big, 2560, 2, T)
        qb_t, kb_t, vb = cut(big, 3072, 8, T), cut(big, 5120, 8, T), cut(big, 7168, 2, 1024)
        mask_a, mask_b = cut(big, 9216, 2, T), cut(big, 9728, T)
        cos, sin = cut(big, 9984, 2, P), cut(big, 10240, 2, P)
        aq_bc, ak_bc = cut(big, 10496, P), cut(big, 10624, P)
        bias = cut(big, 10752, 2, T)
        gates = cut(mid, 0, 32, T)
        oa_t, ob_t = cut(mid, 8192, 8, T), cut(mid, 10240, 8, T)
        tmp = [cut(mid, 12288 + 1024 * n, 1024) for n in range(3)]
        score_a, score_b = cut(mid, 12288, 2, T), cut(mid, 12800, 2, T)
        pt_a, pt_b = cut(mid, 13312, 2, T), cut(mid, 13824, 2, T)
        q_head = [cut(mid, 14336, T), cut(mid, 14592, T)]
        v_head = [cut(mid, 14848, 2, P), cut(mid, 15104, 2, P)]
        hidden = cut(big, 0, KF, T)
        wmod = cut(mid, 0, 4, CK, CN)
        acc = cut(mid, 8192, CN)
        conv_g, conv_v = cut(mid, 9216, 4, T), cut(mid, 10240, 4, T)
        ctx_tok = cut(mid, 11264, 2, D)
        hx_t = cut(big, 0, KD, T)
        cat_t = cut(big, 4096, KD, T)
        vv, k_tok = cut(big, 8192, 2, 1024), cut(big, 10240, 2, 512)
        q_t, k_t = cut(mid, 0, GH, T), cut(mid, 1024, GH, T)
        la = cut(mid, 2048, 2, 2, 512)
        state = cut(mid, 4096, 2, 2, 1024)
        level_mask = cut(mid, 8192, 8, P)
        tri = cut(mid, 10112, 4, P)
        s_t = cut(mid, 10624, GH, P)
        b_t = cut(mid, 11136, 2, 2, 512)
        e_buf = cut(mid, 13184, 2, 512)
        qe = cut(mid, 14208, 2, 512)
        y_tok = cut(mid, 14208, 1024)
        ql, kl = cut(mid, 2048, 2, 512), cut(mid, 3072, 2, 512)
        kc_tok, vvc = cut(mid, 0, 2, 512), cut(mid, 11136, 2, 1024)
        act_words = act_t[:].rearrange("p a b -> p (a b)")
        ws_t = act_words[:, 0:1024].rearrange("p (h i) -> p h i", i=P)
        bs_bc = act_words[:, 1024:2048].rearrange("p (h i) -> p h i", i=P)
        v_sgu = act_words[:, 2048:3072]
        v_tmp = act_words[:, 3072:4096]
        mix_out = cut(mid, 0, 2, D)
        gate_bc = cut(mid, 4096, D)
        gate_w = cut(mid, 6144, 2, 4, P)
        norm_tmp = cut(mid, 12288, 4, 2, T)
        norm_tmp_c = cut(mid, 9216, 4, 2, T)
        norm_tmp2 = cut(big, 4096, 8, 2, T)
        d_t = ctx.enter_context(nc.sbuf_tensor("d_t", [33, T], F32))
        wd2 = mid[0:33, 1024:2048]
        w_d = sb("w_d", KD * 2 * RANK).rearrange("p (k n) -> p k n", n=2 * RANK)
        rpb = bias.rearrange("p a b -> p (a b)")[0:56, 0:P]
        skew = nc.dram_tensor("skew", (56, 64 * P), F32, kind="Internal").ap()

        weight_loaded = [sem(f"weight_loaded{n}") for n in range(SLOTS)]
        weight_used = sem("weight_used")
        names = [
            "attn_done", "attn_kept", "bias_loaded", "bias_used", "bs_added", "bs_loaded", "c_ready",
            "cat_ready", "consts_loaded", "ctx_kept", "ctx_loaded", "cum_done", "cum_kept", "d_done", "d_kept",
            "decay_ready", "down_added", "exps_done", "first_loaded", "gate_kept", "gates_squashed", "grp_free",
            "head_staged", "hidden2_ready", "hidden_ready", "job_acc", "job_kept", "job_summed", "kdec_ready",
            "kt_done", "kt_kept", "la_done", "la_exp", "la_ready", "lv_diff", "lv_done", "lv_exp", "lv_k",
            "lv_q", "lv_taken", "masks_loaded", "max_ready", "merged", "mixer_loaded", "mod_ready", "o_done",
            "o_rs", "o_sq", "o_sum", "out_stored", "post_added", "post_bc", "post_bc_kept", "post_rs",
            "post_scaled", "post_squared", "post_ss", "post_w", "probs_ready", "probs_t_ready", "probs_turned",
            "proj_free", "qe_exp", "qe_ready", "qkv_kept", "rem_done", "rem_exp", "rpb_loaded", "rstd_ready",
            "scores_done", "setup_done", "sgu_centred", "sgu_mixed", "sgu_ready", "sgu_rs", "sgu_sq",
            "sgu_taken", "sgu_var", "skew_written", "squared", "state_done", "state_ready", "summed", "turned",
            "up2_g_free", "up_g_act", "up_g_based", "up_g_free", "up_v_based", "up_v_free", "wd2_loaded",
            "wmod_loaded0", "wmod_loaded1", "wmod_loaded2", "wmod_loaded3", "wmod_used", "wout_added",
            "ws_kept", "ws_summed", "ws_turned", "x0_loaded", "x1_loaded", "y_kept", "y_ready", "y_turned",
        ]
        s = {n: sem(n) for n in names}
        norm_sems = {}
        for key in ("mix", "ffn", "ctx", "mix2", "ffn2"):
            norm_sems[key] = {n: sem(f"norm_{key}_{n}") for n in ("rstd", "tok", "turned", "kept")}
            if key in ("mix", "ffn", "ffn2"):
                norm_sems[key]["kept_odd"] = sem(f"norm_{key}_kept_odd")

        block = ctx.enter_context(nc.Block())

        def ktiles(w):
            return w.rearrange("(k p) n -> p k n", p=P)

        w_in, w_up, w_down = ktiles(a["w_in"]), ktiles(a["w_up"]), ktiles(a["w_down"])
        w_ba, w_bb, w_out = ktiles(a["w_branch_a"]), ktiles(a["w_branch_b"]), ktiles(a["w_out"])
        w_mod, w_in2 = ktiles(a["w_mod_2"]), ktiles(a["w_in_2"])
        w_out2, w_up2, w_down2 = ktiles(a["w_out_2"]), ktiles(a["w_ffn_in_2"]), ktiles(a["w_ffn_out_2"])

        wide = lambda name, n: bass.AP(a[name].tensor, 0, [[0, P], [1, n]])
        first = [(ident[:], a["t_ident"]), (g_mix, a["norm_mix"])]
        consts = [(cos[:], a["t_cos"]), (sin[:], a["t_sin"]),
                  (aq_bc, wide("a_q_norm", HD)), (ak_bc, wide("a_k_norm", HD)), (bq_norm, a["b_q_norm"]),
                  (bk_norm, a["b_k_norm"]), (mask_a[:], a["t_mask_a"]), (mask_b, a["t_mask_b"]),
                  (sink, wide("a_sink", 8)), (g_ffn, a["norm_ffn"]), (conv[:], a["conv"]),
                  (c_vec[:, 0:16], a["c_ctx_2"]), (c_vec[:, 16:32], a["c_2"]), (b_mod, a["b_mod_2"]),
                  (g_pre1, a["g_pre_mix_2"]), (g_post1, a["g_post_mix_2"]), (g_pre2, a["g_pre_ffn_2"]),
                  (g_post2, a["g_post_ffn_2"]), (out_g, a["gla_out_g_2"]), (ln_g, a["gmlp_ln_g_2"]),
                  (ln_b, a["gmlp_ln_b_2"]), (w_d[:], a["w_decay"])]
        N_CONSTS = len(consts)

        MIX_GROUPS = [("k", 2560), ("q", 2048), ("vv0", 3072), ("vv1", 3584), ("g0", 4096), ("g1", 4608),
                      ("v0", 1024), ("u0", 0), ("v1", 1536), ("u1", 512)]
        WOUT2_ORDER = [2, 3, 0, 1]
        PROJ = ["qa0", "qa1", "kv", "qb0", "qb1", "kb0", "kb1", "vb0", "vb1"]
        NORMED = PROJ[:7]

        sched = []
        for c in range(4):
            sched.append(("mm", 0, c))
        sched.append(("post", 0))
        sched += [("d",), ("la",)]
        for c in range(4):
            sched.append(("mm", 1, c))
            if c == 1:
                sched.append(("kt",))
            if c == 2:
                sched.append(("cum",))
        sched.append(("post", 1))
        for c in range(4):
            sched.append(("mm", 2, c))
            if c == 0:
                sched.append(("wst",))
            if c == 1:
                sched += [("rem", 0), ("rem", 1), ("wsum",)]
        sched.append(("post", 2))
        for c in range(4):
            sched.append(("mm", 3, c))
        sched.append(("post", 3))
        steps = []
        for n in range(2):
            steps.append(([("y", 0)] if n else []) + [("qe", n), ("level", n, 0)])
            steps += [[("level", n, l)] for l in range(1, 8)] + [[("o", n)]]
        steps.append([("y", 1)])
        slot = 0
        for g in range(4, 10):
            for c in range(4):
                sched.append(("mm", g, c))
                if slot == 0:
                    sched += [("upd", 0), ("upd", 1)]
                if c == 0 and g > 4:
                    sched.append(("post", g - 1))
                if g in (7, 9) and c in (1, 2):
                    sched.append(("sgu", (g - 7) // 2, c - 1))
                if 1 <= slot <= len(steps):
                    sched += steps[slot - 1]
                slot += 1
        assert slot > len(steps)
        sched += [("post", 9)]

        def down_jobs(g, c):
            at_ = {3: 0, 6: 1, 10: 2}.get(c)
            j = None if at_ is None else 11 * LOOP_JOBS + 3 * g + at_
            return [j] if j is not None and j < JOBS else []

        def group_done(eng, n_last):
            eng.wait_ge(weight_used, n_last + 1)

        def loaded(eng, n):
            eng.wait_ge(weight_loaded[n % SLOTS], 16 * (n // SLOTS + 1))

        def loaded_in(eng, n, i):
            eng.wait_ge(weight_loaded[n % SLOTS], i * 16 + 16 * (n // SLOTS + 1))

        @block.sync
        def _(sp):
            def load(n, src):
                if n >= SLOTS:
                    sp.wait_ge(weight_used, n - SLOTS + 1)
                sp.dma_start(ring[:, n % SLOTS, :, :], src).then_inc(weight_loaded[n % SLOTS], 16)

            def load_in(n, i, src):
                sp.wait_ge(weight_used, i * 8 + (n - SLOTS + 1))
                sp.dma_start(ring[:, n % SLOTS, :, :], src).then_inc(weight_loaded[n % SLOTS], 16)

            def cols(w, c, at):
                return w[:, CK * c:CK * c + CK, at:at + CN]

            sp.dma_start(x_tok[:, 0, :], a["x"][0:P, :]).then_inc(s["x0_loaded"], 16)
            sp.wait_ge(s["x1_loaded"], 16)
            for g in range(9):
                for c in range(4):
                    load(N_PROJ + 4 * g + c, cols(w_in, c, CN * g))
            with sp.Fori(0, 4) as i:
                for j in range(8):
                    load_in(N_GATE + j, i, w_in[:, CK * (j % 4):CK * (j % 4) + CK,
                                                bass.ds(i * 1024 + (4608 + CN * (j // 4)), CN)])
            for g in range(4):
                for c in range(4):
                    load(N_BRANCH + 4 * g + c, cols(w_ba if c < 2 else w_bb, c % 2, CN * g))
            for g in range(4):
                for c in range(4):
                    load(N_WOUT + 4 * g + c, cols(w_out, c, CN * g))

            def ffn(n_up, n_down, up, down):
                with sp.Fori(0, 11) as i:
                    for j in range(8):
                        load_in(n_up + j, i, up[:, CK * (j % 4):CK * (j % 4) + CK,
                                                bass.ds(i * CN + FF * (j // 4), CN)])
                for g in range(4):
                    for c in range(11):
                        load(n_down + 11 * g + c, cols(down, c, CN * g))

            ffn(N_UP, N_DOWN, w_up, w_down)
            for g, at_ in enumerate((2560, 3072, 3584)):
                for c in range(4):
                    load(N_CTX + 4 * g + c, cols(w_in2, c, at_))
            for g, (_, at_) in enumerate(MIX_GROUPS):
                for c in range(4):
                    load(N_MIX + 4 * g + c, cols(w_in2, c, at_))
            for g in range(4):
                for c in range(4):
                    load(N_WOUT2 + 4 * g + c, cols(w_out2, WOUT2_ORDER[c], CN * g))
            ffn(N_UP2, N_DOWN2, w_up2, w_down2)
            for h in range(2):
                sp.wait_ge(s["post_added"], 3 + h)
                sp.dma_start(out[h * P:(h + 1) * P, :], x_tok[:, h, :]).then_inc(s["out_stored"], 16)
            sp.wait_ge(s["out_stored"], 32)


        def keepers(key):
            return 2 if "kept_odd" in norm_sems[key] else 1

        def norm_kept(eng, key, pieces=8):
            eng.wait_ge(norm_sems[key]["kept"], pieces)
            if keepers(key) == 2:
                eng.wait_ge(norm_sems[key]["kept_odd"], pieces)

        def norm_bank(key, j, m):
            bank, at_ = (4 + j % 2, m * T) if keepers(key) == 1 else (4 + 2 * (j % 2) + m, 0)
            return PS[:, bank, at_:at_ + T]

        def block_half(v, size, half):
            v = v.rearrange("p (h m t) -> p h m t", h=GH, t=2 * size)
            return v[:, :, :, half * size:(half + 1) * size]

        def token_half(v, n, size, half):
            v = v[:, :, n * P:(n + 1) * P].rearrange("p h (m t) -> p h m t", t=2 * size)
            return v[:, :, :, half * size:(half + 1) * size]

        def bc(ap, shape):
            return ap.broadcast_to(shape)

        @block.tensor
        def _(pe):
            def chunk_tok(n, c, chunks, stat, bank, part=None):
                loaded(pe, n)
                for k in range(CK):
                    kt = CK * (c if part is None else part) + k
                    for h in range(2):
                        mm = pe.matmul(PS[:, bank + h, :], stat[:, kt, h * P:(h + 1) * P],
                                       ring[:, n % SLOTS, k, :], start=c + k == 0,
                                       stop=CK * c + k == CK * chunks - 1)
                mm.then_inc(weight_used, 1)

            def chunk_feat(n, c, chunks, mov, bank, i=None):
                loaded(pe, n) if i is None else loaded_in(pe, n, i)
                for k in range(CK):
                    kt = CK * c + k
                    for f in range(4):
                        mm = pe.matmul(PS[:, bank + f // 2, (f % 2) * T:(f % 2) * T + T],
                                       ring[:, n % SLOTS, k, f * P:(f + 1) * P], mov[:, kt, :],
                                       start=kt == 0 and f % 2 == 0, stop=kt == CK * chunks - 1,
                                       skip_group_check=True)
                mm.then_inc(weight_used, 1)

            def norm_piece(key, j, src):
                n = norm_sems[key]
                pe.wait_ge(n["tok"], j + 1)
                if j >= 2:
                    norm_kept(pe, key, j - 1)
                for m in range(2):
                    for h in range(2):
                        mm = pe.transpose(norm_bank(key, j, m)[:, h * P:(h + 1) * P],
                                          src[:, j % src.shape[1], h, m * P:(m + 1) * P], ident[:])
                mm.then_inc(n["turned"], 1)

            def turn(n):
                pe.wait_ge(s["proj_free"], n + 1)
                if n >= 1:
                    pe.wait_ge(s["qkv_kept"], n)
                heads = 2 if NORMED[n] == "kv" else 4
                for hd in range(heads):
                    for h in range(2):
                        at_ = (h * heads + hd) * P
                        mm = pe.transpose(PS[:, 4 + hd // 2, (hd % 2) * T + h * P:(hd % 2) * T + (h + 1) * P],
                                          tmp[1][:, at_:at_ + P], ident[:])
                mm.then_inc(s["turned"], 1)

            def mod_sum(done):
                pe.wait_ge(s["job_acc"], done + 1)
                pe.wait_ge(s["job_kept"], done + 1)
                for q in range(4):
                    mm = pe.transpose(PS[:, 6, q * P:(q + 1) * P], acc[:, q * P:(q + 1) * P], ident[:])
                mm.then_inc(s["job_summed"], 1)

            pe.wait_ge(s["first_loaded"], 32)

            for g in range(9):
                for c in range(4):
                    if g == 0:
                        for j in range(8) if c == 0 else ():
                            norm_piece("mix", j, norm_tmp)
                        norm_kept(pe, "mix", 2 * c + 2)
                    elif g >= 2 and c == 0:
                        pe.wait_ge(s["proj_free"], g - 1)
                    chunk_tok(N_PROJ + 4 * g + c, c, 4, act_t, 2 * (g % 2))
                    if c == 2 and 1 <= g <= len(NORMED):
                        turn(g - 1)

            pe.wait_ge(s["qkv_kept"], 7)
            pe.wait_ge(s["proj_free"], 8)
            pe.sem_inc(s["attn_done"], 1)
            pe.sem_inc(s["job_summed"], 1)
            with pe.Fori(0, 4) as i:
                for u in range(2):
                    done = i * 2 + u
                    pe.wait_ge(s["head_staged"], done + 1)
                    for n, keys in ((0, ka_t[:, i // 2, :]), (1, kb_t[:, done, :])):
                        for b in range(2):
                            mm = pe.matmul(PS[:, 4 + n, b * T:(b + 1) * T], q_head[n][:, b * P:(b + 1) * P],
                                           keys, start=True, stop=True)
                    mm.then_inc(s["scores_done"], 1)
                    pe.wait_ge(s["gate_kept"], done + 1)
                    for c in range(4):
                        chunk_feat(N_GATE + 4 * u + c, c, 4, act_t, 2, i)
                        if c == 1:
                            pe.wait_ge(s["probs_ready"], done + 1)
                            for n, probs in ((0, score_a), (1, score_b)):
                                for b in range(2):
                                    for k in range(2):
                                        mm = pe.transpose(PS[:, 6 + n, k * T + b * P:k * T + (b + 1) * P],
                                                          probs[:, b, k * P:(k + 1) * P], ident[:])
                            mm.then_inc(s["probs_turned"], 1)
                        if c == 2:
                            pe.wait_ge(s["probs_t_ready"], done + 1)
                            pe.wait_ge(s["proj_free"], 9)
                            for n, probs in ((0, pt_a), (1, pt_b)):
                                for k in range(2):
                                    mm = pe.matmul(PS[:, n, 0:T], v_head[n][:, k, :], probs[:, k, :],
                                                   start=k == 0, stop=k == 1)
                            mm.then_inc(s["attn_done"], 1)

            pe.wait_ge(s["attn_kept"], 8)
            pe.wait_ge(s["gate_kept"], 9)
            for g in range(4):
                if g >= 2:
                    pe.wait_ge(s["merged"], g - 1)
                for c in range(4):
                    chunk_feat(N_BRANCH + 4 * g + c, c % 2, 2, oa_t if c < 2 else ob_t, 4 * (g % 2) + 2 * (c // 2))

            for g in range(4):
                pe.wait_ge(s["merged"], 3 + g // 2)
                for c in range(4):
                    pe.wait_ge(s["merged"], max(c + 1, 3 + g // 2))
                    chunk_tok(N_WOUT + 4 * g + c, c, 4, gates, 2 * g)

            for j in range(8):
                norm_piece("ffn", j, norm_tmp)

            norm_kept(pe, "ffn")
            with pe.Fori(0, 11) as i:
                pe.wait_ge(s["up_g_free"], i + 1)
                for c in range(4):
                    chunk_feat(N_UP + c, c, 4, act_t, 0, i)
                pe.wait_ge(s["up_v_free"], i + 1)
                for c in range(4):
                    chunk_feat(N_UP + 4 + c, c, 4, act_t, 2, i)
                    if c == 1:
                        mod_sum(i * LOOP_JOBS)
                mod_sum(i * LOOP_JOBS + 1)
            pe.wait_ge(s["hidden_ready"], 11)
            for g in range(4):
                if g >= 2:
                    pe.wait_ge(s["down_added"], g - 1)
                for c in range(11):
                    chunk_tok(N_DOWN + 11 * g + c, c, 11, hidden, 2 * (g % 2))
                    for j in down_jobs(g, c):
                        mod_sum(j)
                    if g == 3 and c >= 3:
                        norm_piece("ctx", c - 3, norm_tmp_c)

            def decay_proj(src, m):
                for k in range(KD):
                    mm = pe.matmul(PS[0:2 * RANK, 7, 0:T], w_d[:, k, :], src[:, k, :], start=k == 0,
                                   stop=k == KD - 1)
                mm.then_inc(s["d_done"], 1)

            def log_decay(m):
                pe.wait_ge(s["d_kept"], m + 1)
                pe.wait_ge(s["wd2_loaded"], 64)
                for h in range(2):
                    for r in range(2):
                        mm = pe.matmul(PS[:, 4 + 2 * h + r, :], d_t[:, h * P:(h + 1) * P],
                                       wd2[:, r * 512:(r + 1) * 512], start=True, stop=True)
                mm.then_inc(s["la_done"], 1)

            norm_kept(pe, "ctx")
            decay_proj(act_t, 0)
            for g in range(3):
                if g == 0:
                    pe.wait_ge(s["down_added"], 3)
                if g == 1:
                    pe.wait_ge(s["down_added"], 4)
                if g == 2:
                    pe.wait_ge(s["ctx_kept"], 1)
                for c in range(4):
                    chunk_tok(N_CTX + 4 * g + c, c, 4, act_t, 2 * (g % 2))
                    if g == 0 and c == 1:
                        log_decay(0)
                    if g == 1 and c == 0:
                        pe.wait_ge(s["masks_loaded"], 32)
                        pe.wait_ge(s["la_ready"], 1)
                        for r in range(2):
                            for h in range(2):
                                other = 1 - h
                                whole = (h == 0) if r == 0 else (h == 1)
                                mm = pe.matmul(PS[:, 4 + 2 * r + h, :], tri[:, 2 + r, :], la[:, h, r, :],
                                               start=True, stop=not whole)
                                if whole:
                                    mm = pe.matmul(PS[:, 4 + 2 * r + h, :], ones[:], la[:, other, r, :],
                                                   start=False, stop=True)
                        mm.then_inc(s["rem_done"], 1)
                    if (g, c) in ((1, 2), (1, 3), (2, 0), (2, 1)):
                        pe.wait_ge(s["rem_exp"], 1)
                        at_ = 2 * (4 * (g - 1) + c - 2)
                        norm_piece("mix2", at_, norm_tmp2)
                        norm_piece("mix2", at_ + 1, norm_tmp2)
            pe.wait_ge(s["ctx_kept"], 3)
            for r in range(2):
                pe.wait_ge(s["kdec_ready"], r + 1)
                for hd in range(GH):
                    for h in range(2):
                        mm = pe.matmul(PS[:, 4 + 2 * r + hd // 2, (hd % 2) * T:(hd % 2) * T + T],
                                       e_buf[:, h, hd * P:(hd + 1) * P] if r == 0 else qe[:, h, hd * P:(hd + 1) * P],
                                       vvc[:, h, hd * T:(hd + 1) * T], start=h == 0 and hd % 2 == 0, stop=h == 1,
                                       skip_group_check=True)
                mm.then_inc(s["state_done"], 1)

            def mix_bank(g):
                return 2 * (g % 2)

            lv = 0
            for item in sched:
                if item[0] == "mm":
                    _, g, c = item
                    if c == 0:
                        if g == 0:
                            norm_kept(pe, "mix2")
                        if g >= 2:
                            pe.wait_ge(s["grp_free"], g - 1)
                    kind = MIX_GROUPS[g][0]
                    if kind[0] in "kv":
                        chunk_tok(N_MIX + 4 * g + c, c, 4, hx_t, mix_bank(g))
                    else:
                        chunk_feat(N_MIX + 4 * g + c, c, 4, hx_t, mix_bank(g))
                elif item[0] == "d":
                    pe.wait_ge(s["state_ready"], 2)
                    decay_proj(hx_t, 1)
                elif item[0] == "la":
                    norm_kept(pe, "mix2")
                    log_decay(1)
                elif item[0] == "kt":
                    pe.wait_ge(s["grp_free"], 1)
                    pe.wait_ge(s["la_ready"], 2)
                    for hd in range(GH):
                        for h in range(2):
                            mm = pe.transpose(PS[:, 4 + hd // 2, (hd % 2) * T + h * P:(hd % 2) * T + (h + 1) * P],
                                              k_tok[:, h, hd * P:(hd + 1) * P], ident[:])
                    mm.then_inc(s["kt_done"], 1)
                elif item[0] == "cum":
                    pe.wait_ge(s["kt_kept"], 1)
                    for n in range(2):
                        for r in range(2):
                            for hd in range(GH):
                                mm = pe.matmul(PS[:, 4 + 2 * n + r, hd * P:(hd + 1) * P],
                                               la[:, n, r, hd * P:(hd + 1) * P], tri[:, r, :], start=True, stop=True)
                    mm.then_inc(s["cum_done"], 1)
                elif item[0] == "wst":
                    pe.wait_ge(s["cum_kept"], 1)
                    pe.wait_ge(s["mixer_loaded"], 16)
                    for hd in range(8):
                        mm = pe.transpose(PS[:, 4 + hd // 4, (hd % 4) * P:(hd % 4 + 1) * P],
                                          v_sgu[:, hd * P:(hd + 1) * P], ident[:])
                    mm.then_inc(s["ws_turned"], 1)
                elif item[0] == "wsum":
                    pe.wait_ge(s["ws_kept"], 1)
                    for hd in range(8):
                        mm = pe.matmul(PS[:, 4 + hd // 4, (hd % 4) * P:(hd % 4 + 1) * P], ones[:], ws_t[:, hd, :],
                                       start=True, stop=True)
                    mm.then_inc(s["ws_summed"], 1)
                elif item[0] == "rem":
                    r = item[1]
                    mm = pe.matmul(PS[:, 6 + r, :], tri[:, 2 + r, :], la[:, r, r, :], start=True, stop=True)
                    mm.then_inc(s["rem_done"], 1)
                elif item[0] == "upd":
                    r = item[1]
                    pe.wait_ge(s["kdec_ready"], 3 + r)
                    pe.wait_ge(s["grp_free"], 4)
                    pe.wait_ge(s["bs_added"], 1)
                    for hd in range(GH):
                        mm = pe.matmul(PS[:, 4 + 2 * r + hd // 2, (hd % 2) * T:(hd % 2) * T + T],
                                       e_buf[:, r, hd * P:(hd + 1) * P], vv[:, r, hd * T:(hd + 1) * T],
                                       start=True, stop=True)
                    mm.then_inc(s["state_done"], 1)
                elif item[0] == "level":
                    pe.wait_ge(s["lv_q"], lv + 1)
                    pe.wait_ge(s["lv_k"], lv + 1)
                    if lv:
                        pe.wait_ge(s["lv_taken"], lv)
                    else:
                        pe.wait_ge(s["state_ready"], 4)
                    for hd in range(GH):
                        mm = pe.matmul(PS[:, 4, hd * P:(hd + 1) * P], kl[:, lv % 2, hd * P:(hd + 1) * P],
                                       ql[:, lv % 2, hd * P:(hd + 1) * P], start=True, stop=True)
                    mm.then_inc(s["lv_done"], 1)
                    lv += 1
                elif item[0] == "o":
                    n = item[1]
                    pe.wait_ge(s["lv_taken"], 8 * (n + 1))
                    pe.wait_ge(s["qe_ready"], n + 1)
                    if n == 1:
                        pe.wait_ge(s["y_ready"], 1)
                    for hd in range(GH):
                        o = PS[:, 6 + hd // 2, (hd % 2) * T:(hd % 2) * T + T]
                        pe.matmul(o, s_t[:, hd, :], vv[:, n, hd * T:(hd + 1) * T], start=True, stop=False)
                        for r in range(2):
                            mm = pe.matmul(o, qe[:, r, hd * P:(hd + 1) * P],
                                           state[:, r, n if r == 0 else 1 - n, hd * T:(hd + 1) * T],
                                           start=False, stop=r == 1)
                    mm.then_inc(s["o_done"], 1)
                elif item[0] == "y":
                    n = item[1]
                    pe.wait_ge(s["y_ready"], n + 1)
                    if n == 1:
                        pe.wait_ge(s["y_kept"], 1)
                    for f in range(8):
                        mm = pe.transpose(PS[:, 6 + f // 4, (f % 4) * P:(f % 4 + 1) * P],
                                          y_tok[:, f * P:(f + 1) * P], ident[:])
                    mm.then_inc(s["y_turned"], 1)
                elif item[0] == "sgu":
                    _, m, n = item
                    pe.wait_ge(s["sgu_ready"], m + 1)
                    if m + n:
                        pe.wait_ge(s["sgu_taken"], 2 * m + n)
                    for hd in range(4):
                        mm = pe.matmul(PS[:, 5, hd * P:(hd + 1) * P],
                                       v_sgu[:, n * 512 + hd * P:n * 512 + (hd + 1) * P],
                                       ws_t[:, 4 * m + hd, :], start=True, stop=True)
                    mm.then_inc(s["sgu_mixed"], 1)

            def spread_gate(m, j):
                pe.wait_ge(s["post_w"], 4 * m + j + 1)
                if m + j:
                    pe.wait_ge(s["post_bc_kept"], 4 * m + j)
                for f in range(4):
                    mm = pe.matmul(PS[:, 7, f * P:(f + 1) * P], gate_w[:, j % 2, f, :], ident[:],
                                   start=True, stop=True)
                mm.then_inc(s["post_bc"], 1)

            for g in range(4):
                if g == 0:
                    pe.wait_ge(s["y_kept"], 2)
                elif g == 1:
                    pe.wait_ge(s["grp_free"], 10)
                else:
                    pe.wait_ge(s["post_scaled"], g - 1)
                for c in range(4):
                    if c == 3:
                        pe.wait_ge(s["cat_ready"], 2)
                    chunk_tok(N_WOUT2 + 4 * g + c, c, 4, cat_t, 2 * (g % 2), WOUT2_ORDER[c])
                    if g == 0:
                        spread_gate(0, c)

            for j in range(8):
                norm_piece("ffn2", j, norm_tmp)

            norm_kept(pe, "ffn2")
            with pe.Fori(0, 11) as i:
                pe.wait_ge(s["up2_g_free"], i + 1)
                for c in range(4):
                    chunk_feat(N_UP2 + c, c, 4, act_t, 0, i)
                pe.wait_ge(s["hidden2_ready"], i + 1)
                for c in range(4):
                    chunk_feat(N_UP2 + 4 + c, c, 4, act_t, 2, i)
            pe.wait_ge(s["hidden2_ready"], 12)
            for g in range(4):
                if g >= 2:
                    pe.wait_ge(s["post_scaled"], 4 + g - 1)
                for c in range(11):
                    chunk_tok(N_DOWN2 + 11 * g + c, c, 11, hidden, 2 * (g % 2))
                    if g == 0 and c < 4:
                        spread_gate(1, c)

        @block.vector
        def _(ve):
            def norm(key, src, dst, kept=None, gain=None, shift=None):
                n = norm_sems[key]
                ve.wait_ge(n["rstd"], 1)

                def keep(j):
                    kt = 2 * j + 1
                    ve.wait_ge(n["turned"], j + 1)
                    ps = norm_bank(key, j, 1)
                    if shift is None:
                        op = ve.tensor_scalar(kept[:, kt, :], ps, gain[:, kt:kt + 1], None, ALU.mult)
                    else:
                        op = ve.tensor_scalar(kept[:, kt, :], ps, gain[:, kt:kt + 1], shift[:, kt:kt + 1],
                                              ALU.mult, ALU.add)
                    op.then_inc(n["kept_odd"], 1)

                for j in range(8):
                    if kept is not None and j >= 2:
                        keep(j - 2)
                    if j >= dst.shape[1]:
                        ve.wait_ge(n["turned"], j - 3)
                    for h in range(2):
                        op = ve.tensor_scalar(dst[:, j % dst.shape[1], h, :], src[:, h, j * T:(j + 1) * T],
                                              norm_rs[:, h:h + 1], None, ALU.mult)
                    op.then_inc(n["tok"], 1)
                if kept is not None:
                    keep(6)
                    keep(7)

            def pair(bank, width=512):
                return PS[:, bank:bank + 2, 0:width]

            ve.memset(d_t[2 * RANK:2 * RANK + 1, :], 1.0)
            ve.wait_ge(s["x0_loaded"], 16)
            ve.wait_ge(s["x1_loaded"], 16)
            ve.wait_ge(s["first_loaded"], 32)
            norm("mix", x_tok, norm_tmp, act_t, g_mix)
            ve.wait_ge(s["consts_loaded"], 16 * N_CONSTS)

            for g, kind in enumerate(PROJ):
                if g >= len(NORMED):
                    group_done(ve, N_PROJ + 4 * g + 3)
                    at_ = 512 * (g - len(NORMED))
                    ve.tensor_copy(vb[:, :, at_:at_ + 512], pair(2 * (g % 2))).then_inc(s["proj_free"], 1)
                    continue
                heads = 2 if kind == "kv" else 4
                w = heads * HD
                sq, tok, rot = (t[:, 0:2 * w].rearrange("p (h n d) -> p h n d", h=2, d=HD) for t in tmp)
                ve.wait_ge(s["squared"], g + 1)
                ve.tensor_reduce(ss[:, 0:2 * heads], tmp[0][:, 0:2 * w].rearrange("p (n d) -> p n d", d=HD),
                                 AX, ALU.add).then_inc(s["summed"], 1)
                ve.wait_ge(s["rstd_ready"], g + 1)
                if g:
                    ve.wait_ge(s["turned"], g)
                ps = pair(2 * (g % 2), w).rearrange("p h (n d) -> p h n d", d=HD)
                rstd = rs[:, 0:2 * heads].rearrange("p (h n) -> p h n", h=2).unsqueeze(3)
                op = ve.tensor_tensor(tok, ps, bc(rstd, [P, 2, heads, HD]), ALU.mult)
                if g < 3:
                    if kind == "kv":
                        ve.tensor_copy(va[:], PS[:, 2 * (g % 2):2 * (g % 2) + 2, 256:512])
                    ve.drain()
                    flat = tmp[1][:, 0:2 * w].rearrange("p (n d) -> p n d", d=HD)
                    weight = (ak_bc if kind == "kv" else aq_bc).unsqueeze(1)
                    ve.tensor_tensor(flat, flat, bc(weight, [P, 2 * heads, HD]), ALU.mult)
                    ve.drain()
                    ve.tensor_tensor(sq, tok, bc(cos.unsqueeze(2), [P, 2, heads, HD]), ALU.mult)
                    half = HD // 2
                    lo = bc(sin[:, :, 0:half].unsqueeze(2), [P, 2, heads, half])
                    hi = bc(sin[:, :, half:HD].unsqueeze(2), [P, 2, heads, half])
                    ve.tensor_tensor(rot[:, :, :, 0:half], tok[:, :, :, half:HD], lo, ALU.mult)
                    ve.tensor_tensor(rot[:, :, :, half:HD], tok[:, :, :, 0:half], hi, ALU.mult)
                    ve.drain()
                    op = ve.tensor_tensor(tmp[1][:, 0:2 * w], tmp[0][:, 0:2 * w], tmp[2][:, 0:2 * w], ALU.add)
                op.then_inc(s["proj_free"], 1)

            scale = 1.0 / math.sqrt(HD)
            ve.sem_inc(s["bias_used"], 1)
            with ve.Fori(0, 4) as i:
                for u in range(2):
                    done = i * 2 + u
                    sink_col = sink[:, bass.ds(i * 2 + u, 1)]
                    ve.wait_ge(s["bias_loaded"], done * 64 + 64)
                    ve.wait_ge(s["scores_done"], done + 1)
                    ps = PS[:, 4:6, :].rearrange("p a (b t) -> p a b t", t=T)
                    ve.scalar_tensor_tensor(score_a[:], ps[:, 0], scale, mask_a[:], ALU.mult, ALU.add)
                    ve.scalar_tensor_tensor(score_b[:], ps[:, 1], scale, bias[:], ALU.mult, ALU.add)\
                        .then_inc(s["bias_used"], 1)
                    ve.drain()
                    ve.tensor_tensor(score_b[:], score_b[:], bc(mask_b.unsqueeze(1), [P, 2, T]), ALU.add)
                    ve.tensor_reduce(mx[:, 0:2], score_a[:], AX, ALU.max)
                    ve.drain()
                    ve.tensor_reduce(mx[:, 2:4], score_b[:], AX, ALU.max)
                    ve.tensor_scalar(mx[:, 0:2], mx[:, 0:2], sink_col, None, ALU.max)
                    ve.drain()
                    ve.tensor_scalar(mx[:, 4:8], mx[:, 0:4], -1.0, None, ALU.mult).then_inc(s["max_ready"], 1)
                    ve.wait_ge(s["exps_done"], done + 1)
                    ve.tensor_tensor(den[:, 0:2], den[:, 0:2], den[:, 4:6], ALU.add)
                    ve.drain()
                    ve.reciprocal(den[:, 4:8], den[:, 0:4])
                    ve.drain()
                    for n, probs in ((0, score_a), (1, score_b)):
                        for b in range(2):
                            op = ve.tensor_scalar(probs[:, b, :], probs[:, b, :],
                                                  den[:, 4 + 2 * n + b:5 + 2 * n + b], None, ALU.mult)
                    op.then_inc(s["probs_ready"], 1)

            for g in range(4):
                banks = 4 * (g % 2)
                ga = gates[:, 4 * g:4 * g + 4, :].rearrange("p (a b) t -> p a (b t)", a=2)
                gb = gates[:, 16 + 4 * g:20 + 4 * g, :].rearrange("p (a b) t -> p a (b t)", a=2)
                ve.wait_ge(s["gates_squashed"], g + 1)
                group_done(ve, N_BRANCH + 4 * g + 3)
                ve.tensor_tensor(ga, ga, pair(banks), ALU.mult)
                ve.tensor_tensor(gb, gb, pair(banks + 2), ALU.mult)
                ve.drain()
                ve.tensor_tensor(ga, ga, gb, ALU.add).then_inc(s["merged"], 1)

            for g in range(4):
                group_done(ve, N_WOUT + 4 * g + 3)
                part = x_tok[:, :, CN * g:CN * (g + 1)]
                ve.tensor_tensor(part, part, pair(2 * g), ALU.add).then_inc(s["wout_added"], 1)
            norm("ffn", x_tok, norm_tmp, act_t, g_ffn)

            def job(j, c_at):
                for c in range(4):
                    if c:
                        ve.drain()
                    ve.wait_ge(s[f"wmod_loaded{c}"], j * 16 + 16)
                    if c == 0:
                        ve.wait_ge(s["job_summed"], j + 1)
                    for k in range(CK):
                        col = c_vec[:, c_at + CK * c + k:c_at + CK * c + k + 1]
                        if c + k == 0:
                            op = ve.tensor_scalar(acc, wmod[:, c, k, :], col, None, ALU.mult)
                        else:
                            if k:
                                ve.drain()
                            op = ve.scalar_tensor_tensor(acc, wmod[:, c, k, :], col, acc, ALU.mult, ALU.add)
                    op.then_inc(s["wmod_used"], 1)
                ve.drain().then_inc(s["job_acc"], 1)

            def keep_job(j):
                ve.wait_ge(s["job_summed"], j + 2)
                ve.tensor_reduce(mod[:, bass.ds(j * 4, 4)], PS[:, 6, :].rearrange("p (q r) -> p q r", r=P), AX,
                                 ALU.add).then_inc(s["job_kept"], 1)

            def conv_sides(dst, bank, i, at_):
                for side in range(2):
                    for f in range(4):
                        ps = PS[:, bank + f // 2, (f % 2) * T:(f % 2) * T + T]
                        w = conv[:, bass.ds(i * 4 + (at_ + f), 1), 2 * side]
                        if side == 0:
                            o, src = dst[:, f, 1:T], ps[:, 0:T - 1]
                        else:
                            o, src = dst[:, f, 0:T - 1], ps[:, 1:T]
                        op = ve.scalar_tensor_tensor(o, src, w, o, ALU.mult, ALU.add)
                    if side == 0:
                        ve.drain()
                return op

            ve.wait_ge(s["c_ready"], 1)
            for name in ("up_g_free", "up_v_free", "hidden_ready", "job_kept"):
                ve.sem_inc(s[name], 1)
            for first, last, c_at in ((0, 4, 0), (4, 11, 16)):
                with ve.Fori(first, last) as i:
                    job(i * LOOP_JOBS, c_at)
                    ve.wait_ge(s["up_g_based"], i + 1)
                    conv_sides(conv_g, 0, i, 0).then_inc(s["up_g_free"], 1)
                    keep_job(i * LOOP_JOBS)
                    job(i * LOOP_JOBS + 1, c_at)
                    ve.wait_ge(s["up_v_based"], i + 1)
                    conv_sides(conv_v, 2, i, KF).then_inc(s["up_v_free"], 1)
                    ve.drain()
                    ve.wait_ge(s["up_g_act"], i + 1)
                    ve.tensor_tensor(hidden[:, bass.ds(i * 4, 4), :], conv_g[:], conv_v[:], ALU.mult)\
                        .then_inc(s["hidden_ready"], 1)
                    keep_job(i * LOOP_JOBS + 1)

            ve.drain()
            ve.tensor_tensor(mod[:, 0:32], mod[:, 0:32], b_mod[:, 0:32], ALU.add)
            ve.drain()
            ve.scalar_tensor_tensor(scale_c, mod[:, 16:32], 1.0, g_pre1, ALU.add, ALU.mult)\
                .then_inc(s["mod_ready"], 1)
            for g in range(4):
                for c in range(11):
                    for j in down_jobs(g, c):
                        job(j, 16)
                        keep_job(j)
                if g == 3:
                    norm("ctx", ctx_tok, norm_tmp_c)
                group_done(ve, N_DOWN + 11 * g + 10)
                part = x_tok[:, :, CN * g:CN * (g + 1)]
                ve.tensor_tensor(part, part, pair(2 * (g % 2)), ALU.add).then_inc(s["down_added"], 1)
            ve.drain()
            ve.tensor_tensor(mod[:, 32:128], mod[:, 32:128], b_mod[:, 0:96], ALU.add)
            ve.drain()
            ve.scalar_tensor_tensor(scale_x1, mod[:, 48:64], 1.0, g_pre1, ALU.add, ALU.mult)
            ve.scalar_tensor_tensor(scale_x2, mod[:, 96:112], 1.0, g_pre2, ALU.add, ALU.mult)\
                .then_inc(s["mod_ready"], 1)
            norm("mix2", x_tok, norm_tmp2)

            def log_decay(m):
                ve.wait_ge(s["la_exp"], m + 1)
                flat = la.rearrange("p a b c -> p (a b) c")
                ve.scalar_tensor_tensor(flat, PS[:, 4:8, :], 0.0, flat, ALU.min, ALU.subtract)
                ve.drain()
                ve.tensor_scalar(flat, flat, 1.0 / TAU, None, ALU.mult).then_inc(s["la_ready"], 1)

            log_decay(0)
            ve.wait_ge(s["rem_exp"], 1)
            ve.wait_ge(s["ctx_kept"], 1)
            for r, k in ((0, e_buf), (1, qe)):
                ve.tensor_tensor(k[:], k[:], kc_tok[:], ALU.mult).then_inc(s["kdec_ready"], 1)

            lv, taken = 0, 0
            ve.wait_ge(s["masks_loaded"], 32)

            def take(upto):
                nonlocal taken
                while taken < upto:
                    ve.wait_ge(s["lv_done"], taken + 1)
                    mask = bc(level_mask[:, taken % 8, :].unsqueeze(1), [P, GH, P]).bitcast(I32)
                    ve.copy_predicated(s_t[:], mask, PS[:, 4, :].rearrange("p (h i) -> p h i", i=P))\
                        .then_inc(s["lv_taken"], 1)
                    ve.drain()
                    taken += 1

            for item in sched:
                if item[0] == "la":
                    log_decay(1)
                elif item[0] == "rem":
                    r = item[1]
                    ve.wait_ge(s["rem_exp"], 2 + r)
                    ve.tensor_tensor(e_buf[:, r, :], e_buf[:, r, :], k_tok[:, r, :], ALU.mult)\
                        .then_inc(s["kdec_ready"], 1)
                elif item[0] == "upd":
                    r = item[1]
                    ve.wait_ge(s["state_done"], 3 + r)
                    ve.wait_ge(s["decay_ready"], r + 1)
                    for hd in range(GH):
                        op = ve.scalar_tensor_tensor(state[:, r, 1, hd * T:(hd + 1) * T],
                                                     state[:, r, 0, hd * T:(hd + 1) * T],
                                                     decay[:, 4 * r + hd:4 * r + hd + 1],
                                                     PS[:, 4 + 2 * r + hd // 2, (hd % 2) * T:(hd % 2) * T + T],
                                                     ALU.mult, ALU.add)
                    op.then_inc(s["state_ready"], 1)
                    if r == 1:
                        ve.memset(s_t[:], 0.0)
                elif item[0] == "qe":
                    n = item[1]
                    ve.wait_ge(s["qe_exp"], n + 1)
                    ve.wait_ge(s["grp_free"], 2)
                    qe4 = qe.rearrange("p r (h i) -> p r h i", i=P)
                    for r in range(2):
                        op = ve.tensor_tensor(qe4[:, r], qe4[:, r], q_t[:, :, n * P:(n + 1) * P], ALU.mult)
                    op.then_inc(s["qe_ready"], 1)
                elif item[0] == "level":
                    _, n, l = item
                    if n and l == 0:
                        ve.wait_ge(s["o_done"], 1)
                    if l < 7:
                        size = LEVELS[l]
                        if lv:
                            ve.drain()
                            ve.wait_ge(s["lv_k"], lv)
                        for r in range(2):
                            b = b_t[:, n, r, :].rearrange("p (m t) -> p m t", t=2 * size)
                            ref = bc(b[:, :, size - 1 + r:size + r], [P, 256 // size, 2 * size])
                            op = ve.tensor_tensor(e_buf[:, r, :].rearrange("p (m t) -> p m t", t=2 * size), b, ref,
                                                  ALU.subtract)
                        op.then_inc(s["lv_diff"], 1)
                        take(lv)
                        ve.wait_ge(s["lv_exp"], lv + 1 - n)
                        if lv >= 2:
                            ve.wait_ge(s["lv_done"], lv - 1)
                        for half in range(2):
                            op = ve.tensor_tensor(block_half(ql[:, lv % 2, :], size, half),
                                                  token_half(q_t, n, size, half),
                                                  block_half(e_buf[:, 1 - half, :], size, half), ALU.mult)
                        op.then_inc(s["lv_q"], 1)
                    else:
                        take(lv)
                        ve.tensor_scalar(ql[:, lv % 2, :].rearrange("p (h i) -> p h i", i=P),
                                         q_t[:, :, n * P:(n + 1) * P], 2.0, None, ALU.mult).then_inc(s["lv_q"], 1)
                    lv += 1
                elif item[0] == "o":
                    n = item[1]
                    take(8 * (n + 1))
                    ve.wait_ge(s["o_sq"], n + 1)
                    ve.tensor_reduce(ss[:, 0:4], y_tok.rearrange("p (h e) -> p h e", e=T), AX, ALU.add)\
                        .then_inc(s["o_sum"], 1)
                    ve.wait_ge(s["o_rs"], n + 1)
                    ve.tensor_tensor(y_tok.rearrange("p (h e) -> p h e", e=T),
                                     PS[:, 6:8, :].rearrange("p a (b e) -> p (a b) e", e=T),
                                     bc(rs[:, 0:4].unsqueeze(2), [P, 4, T]), ALU.mult).then_inc(s["y_ready"], 1)
                elif item[0] == "y":
                    n = item[1]
                    ve.wait_ge(s["y_turned"], n + 1)
                    ve.wait_ge(s["grp_free"], 6)
                    for f in range(8):
                        c = cat_t[:, 8 + f, n * P:(n + 1) * P]
                        op = ve.scalar_tensor_tensor(c, PS[:, 6 + f // 4, (f % 4) * P:(f % 4 + 1) * P],
                                                     out_g[:, f:f + 1], c, ALU.mult, ALU.mult)
                    op.then_inc(s["y_kept"], 1)
                elif item[0] == "wsum":
                    ve.wait_ge(s["ws_summed"], 1)
                    ve.wait_ge(s["bs_loaded"], 16)
                    for hd in range(8):
                        op = ve.scalar_tensor_tensor(bs_bc[:, hd, :], PS[:, 4 + hd // 4, (hd % 4) * P:(hd % 4 + 1) * P],
                                                     ln_b[:, hd:hd + 1], bs_bc[:, hd, :], ALU.mult, ALU.add)
                    op.then_inc(s["bs_added"], 1)
                elif item[0] == "post" and MIX_GROUPS[item[1]][0] in ("u0", "u1"):
                    m = int(MIX_GROUPS[item[1]][0][1])
                    ve.wait_ge(s["grp_free"], item[1] + 1)
                    ve.drain()
                    u_part = cat_t[:, 4 * m:4 * m + 4, :].rearrange("p h t -> p (h t)")
                    ve.tensor_tensor(u_part, u_part, v_tmp, ALU.mult).then_inc(s["cat_ready"], 1)
                elif item[0] == "post" and MIX_GROUPS[item[1]][0] in ("v0", "v1"):
                    m = int(MIX_GROUPS[item[1]][0][1])
                    v3 = v_sgu.rearrange("p (n d) -> p n d", d=HD)
                    ve.wait_ge(s["grp_free"], item[1] + 1)
                    ve.tensor_reduce(mean[:, 0:8], v3, AX, ALU.add)
                    ve.drain()
                    ve.tensor_scalar(mean[:, 0:8], mean[:, 0:8], -1.0 / HD, None, ALU.mult)
                    ve.drain()
                    ve.tensor_tensor(v3, v3, bc(mean[:, 0:8].unsqueeze(2), [P, 8, HD]), ALU.add)\
                        .then_inc(s["sgu_centred"], 1)
                    ve.wait_ge(s["sgu_sq"], m + 1)
                    ve.tensor_reduce(ss[:, 8:16], v_tmp.rearrange("p (n d) -> p n d", d=HD), AX, ALU.add)\
                        .then_inc(s["sgu_var"], 1)
                    ve.wait_ge(s["sgu_rs"], m + 1)
                    ve.tensor_tensor(v3, v3, bc(rs[:, 8:16].unsqueeze(2), [P, 8, HD]), ALU.mult)\
                        .then_inc(s["sgu_ready"], 1)
                elif item[0] == "sgu":
                    _, m, n = item
                    ve.wait_ge(s["sgu_mixed"], 2 * m + n + 1)
                    mixed = v_tmp.rearrange("p (h n i) -> p h n i", n=2, i=P)
                    for hd in range(4):
                        hh = 4 * m + hd
                        op = ve.scalar_tensor_tensor(mixed[:, hd, n, :], PS[:, 5, hd * P:(hd + 1) * P],
                                                     ln_g[:, hh:hh + 1], bs_bc[:, hh, :], ALU.mult, ALU.add)
                    op.then_inc(s["sgu_taken"], 1)

            def post(m, gate, g_post):
                ve.tensor_tensor(gate_col, gate, g_post, ALU.mult)
                ve.drain()
                for j in range(4):
                    if m or j >= 2:
                        ve.wait_ge(s["post_bc"], 4 * m + j - 1)
                    for f in range(4):
                        op = ve.tensor_scalar(gate_w[:, j % 2, f, :], ones[:], gate_col[:, 4 * j + f:4 * j + f + 1],
                                              None, ALU.mult)
                    op.then_inc(s["post_w"], 1)
                for g in range(4):
                    ve.wait_ge(s["post_bc_kept"], 4 * m + g + 1)
                    ve.wait_ge(s["post_squared"], 4 * m + g + 1)
                    if g == 3:
                        ve.tensor_reduce(norm_ss, part_ss.rearrange("p (g h) -> p h g", h=2), AX, ALU.add)\
                            .then_inc(s["post_ss"], 1)
                    gate_part = bc(gate_bc[:, CN * g:CN * (g + 1)].unsqueeze(1), [P, 2, CN])
                    ve.tensor_tensor(mix_out[:, :, CN * g:CN * (g + 1)], pair(2 * (g % 2)), gate_part, ALU.mult)\
                        .then_inc(s["post_scaled"], 1)
                ve.drain()
                ve.wait_ge(s["post_rs"], m + 1)
                for h in range(2):
                    ve.scalar_tensor_tensor(x_tok[:, h, :], mix_out[:, h, :], norm_rs[:, h:h + 1], x_tok[:, h, :],
                                            ALU.mult, ALU.add).then_inc(s["post_added"], 1)

            post(0, mod[:, 64:80], g_post1)
            norm("ffn2", x_tok, norm_tmp, act_t, scale_x2, mod[:, 80:96])

            ve.sem_inc(s["hidden2_ready"], 1)
            with ve.Fori(0, 11) as i:
                ve.wait_ge(s["up2_g_free"], i + 2)
                group_done(ve, i * 8 + (N_UP2 + 7))
                ve.tensor_tensor(hidden[:, bass.ds(i * 4, 4), :].rearrange("p (a b) t -> p a (b t)", a=2),
                                 conv_g.rearrange("p (a b) t -> p a (b t)", a=2), pair(2), ALU.mult)\
                    .then_inc(s["hidden2_ready"], 1)
            post(1, mod[:, 112:128], g_post2)

        @block.scalar
        def _(act):
            def rstd_of(n_):
                act.activation(norm_rs, norm_ss, ACT.Ln, scale=1.0 / n_, bias=eps_col)
                act.drain()
                return act.activation(norm_rs, norm_rs, ACT.Exp, scale=-0.5)

            def norm_stats(src, junk, ready=None):
                for h in range(2):
                    if ready:
                        ready(h)
                    act.activation(junk, src[:, h, :], ACT.Square, accum_out=norm_ss[:, h:h + 1])
                    act.drain()
                return rstd_of(D)

            def norm(key, src, tmp_, dst, gain, shift, ready=None):
                n = norm_sems[key]
                norm_stats(src, tmp_.rearrange("p a b c -> p (a b c)"), ready).then_inc(n["rstd"], 1)
                norm_keep(key, dst, gain, shift)

            def norm_keep(key, dst, gain, shift):
                n = norm_sems[key]
                for j in range(8):
                    act.wait_ge(n["turned"], j + 1)
                    for m in range(3 - keepers(key)):
                        kt = 2 * j + m
                        bias_ = 0.0 if shift is None else shift[:, kt:kt + 1]
                        op = act.activation(dst[:, kt, :], norm_bank(key, j, m), ACT.Identity,
                                            scale=gain[:, kt:kt + 1], bias=bias_)
                    op.then_inc(n["kept"], 1)

            act.dma_start(x_tok[:, 1, :], a["x"][P:T, :]).then_inc(s["x1_loaded"], 16)
            for dst, src in first:
                act.dma_start(dst, src).then_inc(s["first_loaded"], 16)
            act.wait_ge(s["setup_done"], 1)
            norm("mix", x_tok, norm_tmp, act_t, g_mix, None,
                 lambda h: act.wait_ge(s[f"x{h}_loaded"], 16))
            for dst, src in consts:
                act.dma_start(dst, src).then_inc(s["consts_loaded"], 16)
            act.wait_ge(s["consts_loaded"], 16 * N_CONSTS)
            act.activation(c_vec, c_vec, ACT.Silu).then_inc(s["c_ready"], 1)

            def pair(bank, width=512):
                return PS[:, bank:bank + 2, 0:width]

            for g, kind in enumerate(NORMED):
                heads = 2 if kind == "kv" else 4
                w = heads * HD
                group_done(act, N_PROJ + 4 * g + 3)
                if g:
                    act.wait_ge(s["proj_free"], g)
                act.activation(tmp[0][:, 0:2 * w].rearrange("p (h w) -> p h w", h=2), pair(2 * (g % 2), w),
                               ACT.Square).then_inc(s["squared"], 1)
                act.wait_ge(s["summed"], g + 1)
                act.activation(rs[:, 0:2 * heads], ss[:, 0:2 * heads], ACT.Ln, scale=1.0 / HD, bias=eps_col)
                act.drain()
                act.activation(rs[:, 0:2 * heads], rs[:, 0:2 * heads], ACT.Exp, scale=-0.5)\
                    .then_inc(s["rstd_ready"], 1)
                act.wait_ge(s["turned"], g + 1)
                dst = {"qa0": qa_t[:, 0:4], "qa1": qa_t[:, 4:8], "kv": ka_t[:], "qb0": qb_t[:, 0:4],
                       "qb1": qb_t[:, 4:8], "kb0": kb_t[:, 0:4], "kb1": kb_t[:, 4:8]}[kind]
                dst = dst.rearrange("p n t -> p (n t)")
                src = PS[:, 4:6, :].rearrange("p a b -> p (a b)")[:, 0:heads * T]
                if kind[1] == "b":
                    op = act.activation(dst, src, ACT.Copy, scale=bq_norm if kind[0] == "q" else bk_norm)
                else:
                    op = act.copy(dst, src)
                op.then_inc(s["qkv_kept"], 1)

            act.sem_inc(s["gate_kept"], 1)
            with act.Fori(0, 4) as i:
                for u in range(2):
                    done = i * 2 + u
                    act.wait_ge(s["max_ready"], done + 1)
                    for n, sc in ((0, score_a), (1, score_b)):
                        for b in range(2):
                            at_ = 2 * n + b
                            act.activation(sc[:, b, :], sc[:, b, :], ACT.Exp, bias=mx[:, 4 + at_:5 + at_],
                                           accum_out=den[:, at_:at_ + 1])
                    for b in range(2):
                        op = act.activation(den[:, 4 + b:5 + b], sink[:, bass.ds(i * 2 + u, 1)], ACT.Exp,
                                            bias=mx[:, 4 + b:5 + b])
                    op.then_inc(s["exps_done"], 1)
                    act.wait_ge(s["probs_turned"], done + 1)
                    act.copy(pt_a[:], PS[:, 6, :].rearrange("p (k t) -> p k t", t=T))
                    act.copy(pt_b[:], PS[:, 7, :].rearrange("p (k t) -> p k t", t=T)).then_inc(s["probs_t_ready"], 1)
                    act.wait_ge(s["attn_done"], done + 2)
                    act.copy(oa_t[:, done, :], PS[:, 0, 0:T])
                    act.copy(ob_t[:, done, :], PS[:, 1, 0:T]).then_inc(s["attn_kept"], 1)
                    group_done(act, i * 8 + (N_GATE + 4 * u + 3))
                    act.copy(gates[:, bass.ds(i * 8 + 4 * u, 4), :].rearrange("p (a b) t -> p a (b t)", a=2),
                             pair(2)).then_inc(s["gate_kept"], 1)
            act.drain()
            for g in range(4):
                for at_ in (0, 16):
                    ga = gates[:, at_ + 4 * g:at_ + 4 * g + 4, :]
                    op = act.activation(ga, ga, ACT.Sigmoid)
                op.then_inc(s["gates_squashed"], 1)

            act.wait_ge(s["wout_added"], 4)
            norm("ffn", x_tok, norm_tmp, act_t, g_ffn, None)

            def conv_base(dst, bank, i, at_):
                for f in range(4):
                    w = conv[:, bass.ds(i * 4 + (at_ + f), 1), :]
                    op = act.activation(dst[:, f, :], PS[:, bank + f // 2, (f % 2) * T:(f % 2) * T + T],
                                        ACT.Identity, scale=w[:, 0, 1:2], bias=w[:, 0, 3:4])
                return op

            with act.Fori(0, 11) as i:
                act.wait_ge(s["hidden_ready"], i + 1)
                group_done(act, i * 8 + (N_UP + 3))
                conv_base(conv_g, 0, i, 0).then_inc(s["up_g_based"], 1)
                act.wait_ge(s["up_g_free"], i + 2)
                act.activation(conv_g[:], conv_g[:], ACT.Silu).then_inc(s["up_g_act"], 1)
                group_done(act, i * 8 + (N_UP + 7))
                conv_base(conv_v, 2, i, KF).then_inc(s["up_v_based"], 1)

            act.wait_ge(s["hidden_ready"], 12)
            act.wait_ge(s["mod_ready"], 1)
            act.wait_ge(s["ctx_loaded"], 32)
            norm_stats(ctx_tok, norm_tmp_c.rearrange("p a b c -> p (a b c)")).then_inc(norm_sems["ctx"]["rstd"], 1)
            norm_keep("ctx", act_t, scale_c, mod[:, 0:16])
            act.wait_ge(s["down_added"], 4)
            act.wait_ge(s["mod_ready"], 2)
            norm_stats(x_tok, norm_tmp2[:, 0:4].rearrange("p a b c -> p (a b c)"))\
                .then_inc(norm_sems["mix2"]["rstd"], 1)

            def keep_d(m):
                act.wait_ge(s["d_done"], m + 1)
                act.copy(d_t[0:2 * RANK, :], PS[0:2 * RANK, 7, 0:T]).then_inc(s["d_kept"], 1)

            def log_decay(m):
                flat = la.rearrange("p a b c -> p (a b) c")
                act.wait_ge(s["la_done"], m + 1)
                act.activation(flat, PS[:, 4:8, :], ACT.Abs)
                act.drain()
                act.activation(flat, flat, ACT.Exp, scale=-1.0)
                act.drain()
                act.activation(flat, flat, ACT.Ln, bias=one_col).then_inc(s["la_exp"], 1)

            keep_d(0)
            log_decay(0)
            group_done(act, N_CTX + 3)
            act.copy(kc_tok[:], pair(0)).then_inc(s["ctx_kept"], 1)
            act.wait_ge(s["rem_done"], 1)
            act.activation(e_buf[:], PS[:, 4:6, :], ACT.Exp)
            act.activation(qe[:], PS[:, 6:8, :], ACT.Exp).then_inc(s["rem_exp"], 1)
            norm_keep("mix2", hx_t, scale_x1, mod[:, 32:48])
            for m in range(2):
                group_done(act, N_CTX + 4 * m + 7)
                act.copy(vvc[:, :, 512 * m:512 * (m + 1)], pair(2 - 2 * m)).then_inc(s["ctx_kept"], 1)
            for r in range(2):
                act.wait_ge(s["state_done"], r + 1)
                act.copy(state[:, r, 0, :].rearrange("p (a b) -> p a b", a=2), pair(4 + 2 * r))\
                    .then_inc(s["state_ready"], 1)

            lv = 0
            for item in sched:
                if item[0] == "post":
                    g = item[1]
                    kind = MIX_GROUPS[g][0]
                    bank = 2 * (g % 2)
                    group_done(act, N_MIX + 4 * g + 3)
                    feat = lambda n: cat_t[:, n:n + 4, :].rearrange("p (a b) t -> p a (b t)", a=2)
                    if kind == "k":
                        op = act.copy(k_tok[:], pair(bank))
                    elif kind == "q":
                        op = act.activation(q_t.rearrange("p (a b) t -> p a (b t)", a=2), pair(bank), ACT.Copy,
                                            scale=float(HD) ** -0.5)
                    elif kind[:2] == "vv":
                        m = int(kind[2])
                        op = act.copy(vv[:, :, 512 * m:512 * (m + 1)], pair(bank))
                    elif kind[0] == "u":
                        op = act.activation(feat(4 * int(kind[1])), pair(bank), ACT.Gelu_apprx_tanh)
                    elif kind[0] == "g":
                        op = act.activation(feat(8 + 4 * int(kind[1])), pair(bank), ACT.Silu)
                    else:
                        if kind == "v1":
                            act.wait_ge(s["sgu_mixed"], 2)
                        op = act.activation(v_sgu.rearrange("p (a b) -> p a b", a=2), pair(bank),
                                            ACT.Gelu_apprx_tanh)
                    op.then_inc(s["grp_free"], 1)
                    if kind in ("v0", "v1"):
                        m = int(kind[1])
                        act.wait_ge(s["sgu_centred"], m + 1)
                        if m:
                            act.wait_ge(s["cat_ready"], 1)
                        act.activation(v_tmp, v_sgu, ACT.Square).then_inc(s["sgu_sq"], 1)
                        act.wait_ge(s["sgu_var"], m + 1)
                        act.activation(rs[:, 8:16], ss[:, 8:16], ACT.Ln, scale=1.0 / HD, bias=eps_col)
                        act.drain()
                        act.activation(rs[:, 8:16], rs[:, 8:16], ACT.Exp, scale=-0.5).then_inc(s["sgu_rs"], 1)
                elif item[0] == "d":
                    keep_d(1)
                elif item[0] == "la":
                    log_decay(1)
                elif item[0] == "kt":
                    act.wait_ge(s["kt_done"], 1)
                    act.copy(k_t.rearrange("p (a b) t -> p a (b t)", a=2), pair(4)).then_inc(s["kt_kept"], 1)
                elif item[0] == "cum":
                    act.wait_ge(s["cum_done"], 1)
                    act.copy(b_t.rearrange("p a b c -> p (a b) c"), PS[:, 4:8, :]).then_inc(s["cum_kept"], 1)
                elif item[0] == "wst":
                    act.wait_ge(s["ws_turned"], 1)
                    act.copy(ws_t.rearrange("p (a b) i -> p a (b i)", a=2), pair(4)).then_inc(s["ws_kept"], 1)
                elif item[0] == "rem":
                    r = item[1]
                    act.wait_ge(s["rem_done"], 2 + r)
                    act.activation(e_buf[:, r, :], PS[:, 6 + r, :], ACT.Exp).then_inc(s["rem_exp"], 1)
                elif item[0] == "upd":
                    r = item[1]
                    edge = HD - 1 if r == 0 else 0
                    act.activation(decay[:, 4 * r:4 * r + 4], b_t[:, r, r, edge:512:HD], ACT.Exp)\
                        .then_inc(s["decay_ready"], 1)
                elif item[0] == "qe":
                    n = item[1]
                    if n:
                        act.wait_ge(s["y_turned"], 1)
                    act.activation(qe[:], b_t[:, n], ACT.Exp).then_inc(s["qe_exp"], 1)
                elif item[0] == "level" and item[2] < 7:
                    lv += 1
                    act.wait_ge(s["lv_diff"], lv)
                    act.activation(e_buf[:], e_buf[:], ACT.Abs)
                    act.drain()
                    act.activation(e_buf[:], e_buf[:], ACT.Exp, scale=-1.0).then_inc(s["lv_exp"], 1)
                elif item[0] == "o":
                    n = item[1]
                    act.wait_ge(s["o_done"], n + 1)
                    act.activation(y_tok.rearrange("p (a b) -> p a b", a=2), PS[:, 6:8, :], ACT.Square)\
                        .then_inc(s["o_sq"], 1)
                    act.wait_ge(s["o_sum"], n + 1)
                    act.activation(rs[:, 0:4], ss[:, 0:4], ACT.Ln, scale=1.0 / T, bias=eps_col)
                    act.drain()
                    act.activation(rs[:, 0:4], rs[:, 0:4], ACT.Exp, scale=-0.5).then_inc(s["o_rs"], 1)

            def post(m, n0, chunks):
                def keep_gate(j):
                    act.wait_ge(s["post_bc"], 4 * m + j + 1)
                    act.copy(gate_bc[:, CN * j:CN * (j + 1)], PS[:, 7, :]).then_inc(s["post_bc_kept"], 1)

                for j in range(4):
                    keep_gate(j)
                for g in range(4):
                    group_done(act, n0 + chunks * (g + 1) - 1)
                    for h in range(2):
                        junk = norm_tmp.rearrange("p a b c -> p (a b c)")[:, 1024 * (g % 2) + CN * h:][:, 0:CN]
                        op = act.activation(junk, PS[:, 2 * (g % 2) + h, :], ACT.Square,
                                            accum_out=part_ss[:, 2 * g + h:2 * g + h + 1])
                        act.drain()
                    act.drain().then_inc(s["post_squared"], 1)
                act.wait_ge(s["post_ss"], m + 1)
                rstd_of(D).then_inc(s["post_rs"], 1)

            post(0, N_WOUT2, 4)
            norm("ffn2", x_tok, norm_tmp, act_t, scale_x2, mod[:, 80:96],
                 lambda h: act.wait_ge(s["post_added"], h + 1))
            act.sem_inc(s["up2_g_free"], 1)
            with act.Fori(0, 11) as i:
                act.wait_ge(s["hidden2_ready"], i + 1)
                group_done(act, i * 8 + (N_UP2 + 3))
                act.activation(conv_g.rearrange("p (a b) t -> p a (b t)", a=2), pair(0), ACT.Silu)\
                    .then_inc(s["up2_g_free"], 1)
            post(1, N_DOWN2, 11)

        @block.gpsimd
        def _(pool):
            pool.memset(ones[:], 1.0)
            pool.memset(eps_col, EPS)
            pool.memset(one_col, 1.0)
            pool.memset(rpb, 0.0)
            pool.drain().then_inc(s["setup_done"], 1)
            pool.wait_ge(s["setup_done"], 1)
            pool.wait_ge(weight_used, 4)
            for h in range(8):
                pool.dma_start(rpb[7 * h:7 * h + 7, 48:79], a["b_rpb"][h, 4:11, :]).then_inc(s["rpb_loaded"], 16)
            pool.wait_ge(s["rpb_loaded"], 128)
            src = bc(rpb[:, 0:P - 1].unsqueeze(1), [56, GRID, P - 1])
            pool.dma_start(skew.rearrange("r (q c) -> r q c", c=P)[:, :, 0:P - 1], src).then_inc(s["skew_written"], 16)
            pool.wait_ge(s["skew_written"], 16)
            pool.wait_ge(s["consts_loaded"], 16 * N_CONSTS)
            pool.wait_ge(s["proj_free"], 8)
            pool.wait_ge(s["qkv_kept"], 5)
            with pool.Fori(0, 4) as i:
                for u in range(2):
                    done = i * 2 + u
                    pool.wait_ge(s["bias_used"], done + 1)
                    for qr in range(4):
                        src = bass.AP(skew.tensor, i * (2 * 7 * 64 * P) + (u * 7 + 3 - qr) * 64 * P + GRID - 1,
                                      [[P - 1, GRID], [64 * P, 4], [1, GRID]])
                        dst = bias[(qr % 2) * GRID:(qr % 2 + 1) * GRID, qr // 2, :]
                        pool.dma_start(dst.rearrange("p (r c) -> p r c", c=GRID), src).then_inc(s["bias_loaded"], 16)
                    pool.wait_ge(s["attn_done"], done + 1)
                    if u:
                        pool.wait_ge(s["proj_free"], 9)
                    pool.tensor_copy(q_head[0], qa_t[:, done, :])
                    pool.tensor_copy(q_head[1], qb_t[:, done, :])
                    pool.tensor_copy(v_head[0][:], va[:, :, bass.ds(i // 2 * P, P)])
                    pool.tensor_copy(v_head[1][:], vb[:, :, bass.ds(i * (2 * P) + u * P, P)])
                    pool.drain().then_inc(s["head_staged"], 1)

            def load_job(j, cols):
                for c in range(4):
                    pool.wait_ge(s["wmod_used"], j * 4 + (c + 1))
                    pool.dma_start(wmod[:, c, :, :], w_mod[:, CK * c:CK * c + CK, cols])\
                        .then_inc(s[f"wmod_loaded{c}"], 16)

            norm_kept(pool, "ffn")
            for h in range(2):
                pool.dma_start(ctx_tok[:, h, :], a["ctx_2"][h * P:(h + 1) * P, :]).then_inc(s["ctx_loaded"], 16)
            pool.sem_inc(s["wmod_used"], 4)
            with pool.Fori(0, 4) as i:
                for u in range(2):
                    load_job(i * 2 + u, bass.ds(i * (2 * CN) + u * CN, CN))
            with pool.Fori(4, 11) as i:
                for u in range(2):
                    load_job(i * 2 + u, bass.ds(i * (2 * CN) + (u - 8) * CN, CN))
            for j in range(22, JOBS):
                load_job(j, slice((j - 8) * CN, (j - 7) * CN))
            pool.wait_ge(norm_sems["ctx"]["turned"], 8)
            pool.wait_ge(s["job_kept"], 1 + JOBS)
            pool.memset(wd2, 0.0)
            pool.drain().then_inc(s["setup_done"], 1)
            pool.wait_ge(s["setup_done"], 2)
            for row, n, col, name in ((0, RANK, 0, "gla_wd2_fwd_2"), (RANK, RANK, 512, "gla_wd2_bwd_2"),
                                      (2 * RANK, 1, 0, "gla_bd_fwd_2"), (2 * RANK, 1, 512, "gla_bd_bwd_2")):
                pool.dma_start(wd2[row:row + n, col:col + 512], a[name]).then_inc(s["wd2_loaded"], 16)
            pool.dma_start(tri[:], a["t_tri"]).then_inc(s["masks_loaded"], 16)
            pool.dma_start(level_mask[:], a["t_levels"]).then_inc(s["masks_loaded"], 16)
            group_done(pool, N_CTX + 11)
            pool.dma_start(v_sgu.rearrange("p (h j) -> p h j", j=P), a["gmlp_ws_2"].rearrange("h i j -> i h j"))\
                .then_inc(s["mixer_loaded"], 16)
            pool.dma_start(bs_bc.rearrange("p h i -> p (h i)"),
                           bass.AP(a["gmlp_bs_2"].tensor, 0, [[0, P], [1, 1024]])).then_inc(s["bs_loaded"], 16)
            lv = 0
            pool.wait_ge(s["kt_kept"], 1)
            for item in sched:
                if item[0] != "level":
                    continue
                _, n, l = item
                if lv >= 2:
                    pool.wait_ge(s["lv_done"], lv - 1)
                if l < 7:
                    size = LEVELS[l]
                    pool.wait_ge(s["lv_exp"], lv + 1 - n)
                    for half in range(2):
                        op = pool.tensor_tensor(block_half(kl[:, lv % 2, :], size, half),
                                                token_half(k_t, n, size, half),
                                                block_half(e_buf[:, half, :], size, half), ALU.mult)
                    op.then_inc(s["lv_k"], 1)
                else:
                    pool.tensor_copy(kl[:, lv % 2, :].rearrange("p (h i) -> p h i", i=P),
                                     k_t[:, :, n * P:(n + 1) * P]).then_inc(s["lv_k"], 1)
                lv += 1


WEIGHTS = ["w_in", "w_branch_a", "w_branch_b", "w_out", "w_up", "w_down", "w_mod_2", "w_in_2", "w_out_2",
           "w_ffn_in_2", "w_ffn_out_2"]
FEATURE_MAJOR = {"norm_mix": 16, "norm_ffn": 16, "g_pre_mix_2": 16, "g_post_mix_2": 16, "g_pre_ffn_2": 16,
                 "g_post_ffn_2": 16, "b_mod_2": 96, "c_2": 16, "c_ctx_2": 16, "b_q_norm": 1, "b_k_norm": 1,
                 "gla_out_g_2": 8, "gmlp_ln_g_2": 8, "gmlp_ln_b_2": 8}
ROWS = ["gla_wd2_fwd_2", "gla_wd2_bwd_2", "gla_bd_fwd_2", "gla_bd_bwd_2", "a_q_norm", "a_k_norm", "a_sink"]


def kernel(**inputs):
    import numpy as _np
    import concourse.bacc as _bacc
    from concourse import mybir as _mybir
    from concourse.bass_utils import run_bass_kernel_spmd as _run

    get = lambda n: _np.asarray(inputs[n])
    laid = {n: get(n)[0] for n in WEIGHTS}
    laid["x"], laid["ctx_2"] = get("x")[0], get("ctx_2")[0]
    for n, cols in FEATURE_MAJOR.items():
        laid[n] = get(n).reshape(cols, P).T
    for n in ROWS:
        laid[n] = get(n).reshape(-1, get(n).shape[-1])
    laid["b_rpb"], laid["gmlp_ws_2"], laid["gmlp_bs_2"] = get("b_rpb")[0], get("gmlp_ws_2")[0], get("gmlp_bs_2")[0]
    conv = _np.concatenate([get("conv_w")[0], get("conv_b")], 0)
    laid["conv"] = conv.reshape(4, 2 * KF, P).transpose(2, 1, 0)
    decay_cols = laid["w_in_2"][:, -2 * RANK:]
    laid["w_decay"] = decay_cols.reshape(KD, P, 2 * RANK).transpose(1, 0, 2)
    laid.update(host_tables())

    nc = _bacc.Bacc("TRN2", target_bir_lowering=False, num_devices=1)
    arrays, args = {}, {}
    for name, arr in laid.items():
        arr = _np.ascontiguousarray(arr)
        arrays[f"in_{name}"] = arr
        args[name] = nc.dram_tensor(f"in_{name}", arr.shape, _mybir.dt.from_np(arr.dtype), kind="ExternalInput").ap()
    out = nc.dram_tensor("out", (T, D), F32, kind="ExternalOutput").ap()
    build(nc, args, out)
    r = _run(nc, [arrays], core_ids=[0])
    return r.results[0]["out"].reshape(1, T, D)
```

```python
import math
from contextlib import ExitStack

import numpy as np

import concourse.bass as bass
from concourse import mybir

F32 = mybir.dt.float32
I32 = mybir.dt.int32
ALU = mybir.AluOpType
ACT = mybir.ActivationFunctionType
AX = mybir.AxisListType.X

P = 128
T = 256
D = 2048
KD = D // P
HD = 128
FF = 5632
KF = FF // P
EPS = 1e-6
NEG = -1e30
GRID = 64
TAU = 16.0
GH = 4
RANK = 16

CK, CN = 4, 512
CHUNK = CK * CN
SLOTS = 8
LEVELS = [64, 32, 16, 8, 4, 2, 1]

N_PROJ = 0
N_GATE = N_PROJ + 9 * 4
N_BRANCH = N_GATE + 8 * 4
N_WOUT = N_BRANCH + 4 * 4
N_UP = N_WOUT + 4 * 4
N_DOWN = N_UP + 22 * 4
N_CTX = N_DOWN + 4 * 11
N_MIX = N_CTX + 3 * 4
N_WOUT2 = N_MIX + 10 * 4
N_UP2 = N_WOUT2 + 4 * 4
N_DOWN2 = N_UP2 + 22 * 4

SHARED = 8
JOBS = 24 + SHARED
LOOP_JOBS = 2


def host_tables():
    half = HD // 2
    inv = np.float32(10000.0) ** (-np.arange(half, dtype=np.float32) * np.float32(2.0 / HD))
    ang = np.arange(T, dtype=np.float32)[:, None] * inv[None, :].astype(np.float32)
    cos, sin = np.cos(ang), np.sin(ang)
    cos2 = np.concatenate([cos, cos], 1).reshape(2, P, HD).transpose(1, 0, 2)
    sin2 = np.concatenate([-sin, sin], 1).reshape(2, P, HD).transpose(1, 0, 2)
    q, k = np.arange(T)[:, None], np.arange(T)[None, :]
    mask_a = np.where(np.abs(q - k) <= 128, 0.0, NEG).reshape(2, P, T).transpose(1, 0, 2)
    qc, kc = np.arange(P)[:, None] % GRID, np.arange(T)[None, :] % GRID
    cs = np.clip(qc - 8, 0, GRID - 16)
    mask_b = np.where((kc >= cs) & (kc < cs + 16), 0.0, NEG)
    t, i = np.arange(P)[:, None], np.arange(P)[None, :]
    tri = np.stack([t <= i, t >= i, t > i, t < i], 1)
    levels = []
    for s in LEVELS:
        levels.append((t // (2 * s) == i // (2 * s)) & ((t % (2 * s) < s) != (i % (2 * s) < s)))
    levels += [t == i]
    levels = np.stack(levels, 1)
    c = lambda a: np.ascontiguousarray(a, dtype=np.float32)
    return {"t_ident": c(np.eye(P)), "t_cos": c(cos2), "t_sin": c(sin2), "t_mask_a": c(mask_a),
            "t_mask_b": c(mask_b), "t_tri": c(tri), "t_levels": c(levels)}


def build(nc, a, out):
    with ExitStack() as ctx:
        def sb(name, words):
            return ctx.enter_context(nc.sbuf_tensor(name, [P, words], F32))

        def sem(name):
            return ctx.enter_context(nc.semaphore(name))

        ring = ctx.enter_context(nc.sbuf_tensor("ring", [P, SLOTS, CK, CN], F32))
        x_tok = ctx.enter_context(nc.sbuf_tensor("x_tok", [P, 2, D], F32))
        act_t = ctx.enter_context(nc.sbuf_tensor("act_t", [P, KD, T], F32))
        big = sb("big", KF * T)
        mid = sb("mid", 15360)
        ident = sb("ident", P)
        ones = sb("ones", P)
        small = sb("small", 896)
        PS = ctx.enter_context(nc.psum_tensor("PS", [P, 8, 512], F32))

        def cut(tile, at, *shape):
            n = int(np.prod(shape))
            v = tile[:, at:at + n]
            if len(shape) == 2:
                return v.rearrange("p (a b) -> p a b", b=shape[1])
            if len(shape) == 3:
                return v.rearrange("p (a b c) -> p a b c", b=shape[1], c=shape[2])
            if len(shape) == 4:
                return v.rearrange("p (a b c d) -> p a b c d", b=shape[1], c=shape[2], d=shape[3])
            return v

        at = [0]

        def little(n):
            at[0] += n
            return small[:, at[0] - n:at[0]]

        g_mix, g_ffn = little(16), little(16)
        g_pre1, g_post1, g_pre2, g_post2 = little(16), little(16), little(16), little(16)
        b_mod = little(96)
        mod = little(128)
        c_vec = little(32)
        sink = little(8)
        bq_norm, bk_norm = little(1), little(1)
        conv = little(4 * 88).rearrange("p (f k) -> p f k", k=4)
        out_g, ln_g, ln_b = little(8), little(8), little(8)
        ss, rs = little(16), little(16)
        norm_ss, norm_rs = little(2), little(2)
        gate_col = little(16)
        part_ss = little(8)
        mx = little(8)
        den = little(8)
        mean = little(8)
        decay = little(8)
        eps_col = little(1)
        one_col = little(1)
        minus_half = little(2)
        scale_c, scale_x1, scale_x2 = little(16), little(16), little(16)
        assert at[0] <= 896

        qa_t, ka_t, va = cut(big, 0, 8, T), cut(big, 2048, 2, T), cut(big, 2560, 2, T)
        qb_t, kb_t, vb = cut(big, 3072, 8, T), cut(big, 5120, 8, T), cut(big, 7168, 2, 1024)
        mask_a, mask_b = cut(big, 9216, 2, T), cut(big, 9728, T)
        cos, sin = cut(big, 9984, 2, P), cut(big, 10240, 2, P)
        aq_bc, ak_bc = cut(big, 10496, P), cut(big, 10624, P)
        bias = cut(big, 10752, 2, T)
        gates = cut(mid, 0, 32, T)
        oa_t, ob_t = cut(mid, 8192, 8, T), cut(mid, 10240, 8, T)
        tmp = [cut(mid, 12288 + 1024 * n, 1024) for n in range(3)]
        score_a, score_b = cut(mid, 12288, 2, T), cut(mid, 12800, 2, T)
        pt_a, pt_b = cut(mid, 13312, 2, T), cut(mid, 13824, 2, T)
        q_head = [cut(mid, 14336, T), cut(mid, 14592, T)]
        v_head = [cut(mid, 14848, 2, P), cut(mid, 15104, 2, P)]
        hidden = cut(big, 0, KF, T)
        wmod = cut(mid, 0, 4, CK, CN)
        acc = cut(mid, 8192, 2, CN)
        conv_g, conv_v = cut(mid, 9216, 4, T), cut(mid, 10240, 4, T)
        ctx_tok = cut(mid, 11264, 2, D)
        hx_t = cut(big, 0, KD, T)
        cat_t = cut(big, 4096, KD, T)
        vv, k_tok = cut(big, 8192, 2, 1024), cut(big, 10240, 2, 512)
        q_t, k_t = cut(mid, 0, GH, T), cut(mid, 1024, GH, T)
        la = cut(mid, 2048, 2, 2, 512)
        state = cut(mid, 4096, 2, 2, 1024)
        level_mask = cut(mid, 8192, 8, P)
        tri = cut(mid, 10112, 4, P)
        s_t = cut(mid, 10624, GH, P)
        b_t = cut(mid, 11136, 2, 2, 512)
        e_buf = cut(mid, 13184, 2, 512)
        qe = cut(mid, 14208, 2, 512)
        y_tok = cut(mid, 14208, 1024)
        ql, kl = cut(mid, 2048, 2, 512), cut(mid, 3072, 2, 512)
        kc_tok, vvc = cut(mid, 0, 2, 512), cut(mid, 11136, 2, 1024)
        act_words = act_t[:].rearrange("p a b -> p (a b)")
        ws_t = act_words[:, 0:1024].rearrange("p (h i) -> p h i", i=P)
        bs_bc = act_words[:, 1024:2048].rearrange("p (h i) -> p h i", i=P)
        v_sgu = act_words[:, 2048:3072]
        v_tmp = act_words[:, 3072:4096]
        mix_out = cut(mid, 0, 2, D)
        gate_bc = cut(mid, 4096, D)
        gate_w = cut(mid, 6144, 2, 4, P)
        norm_tmp = cut(mid, 12288, 4, 2, T)
        norm_tmp_c = cut(mid, 9216, 4, 2, T)
        norm_tmp2 = cut(big, 4096, 8, 2, T)
        d_t = ctx.enter_context(nc.sbuf_tensor("d_t", [33, T], F32))
        wd2 = mid[0:33, 1024:2048]
        w_d = sb("w_d", KD * 2 * RANK).rearrange("p (k n) -> p k n", n=2 * RANK)
        rpb = bias.rearrange("p a b -> p (a b)")[0:56, 0:P]
        skew = nc.dram_tensor("skew", (56, 64 * P), F32, kind="Internal").ap()

        weight_loaded = [sem(f"weight_loaded{n}") for n in range(SLOTS)]
        weight_used = sem("weight_used")
        names = [
            "attn_done", "attn_kept", "bias_loaded", "bias_used", "bs_added", "bs_loaded", "c_ready", "cat_ready",
            "consts_loaded", "ctx_kept", "ctx_loaded", "cum_done", "cum_kept", "d_done", "d_kept", "decay_ready",
            "down_added", "exps_done", "first_loaded", "gate_kept", "gates_squashed", "grp_free", "head_staged",
            "hidden2_ready", "hidden_ready", "job_acc", "job_kept", "job_summed", "kdec_ready", "kt_done",
            "kt_kept", "la_done", "la_exp", "la_ready", "lv_diff", "lv_done", "lv_exp", "lv_k", "lv_q", "lv_taken",
            "masks_loaded", "max_ready", "merged", "mixer_loaded", "mod_ready", "o_done", "o_rs", "o_sq", "o_sum",
            "out_stored", "post_added", "post_bc", "post_bc_kept", "post_rs", "post_scaled", "post_squared",
            "post_w", "probs_ready", "probs_t_ready", "probs_turned", "proj_free", "qe_exp", "qe_ready", "qkv_kept",
            "rem_done", "rem_exp", "rpb_loaded", "rstd_ready", "scores_done", "setup_done", "sgu_centred",
            "sgu_mixed", "sgu_ready", "sgu_rs", "sgu_sq", "sgu_taken", "sgu_var", "skew_written", "squared",
            "state_done", "state_ready", "summed", "turned", "up2_g_free", "up_g_act", "up_g_based", "up_g_free",
            "up_v_based", "up_v_free", "wd2_loaded", "wmod_loaded0", "wmod_loaded1", "wmod_loaded2", "wmod_loaded3",
            "wmod_used", "wout_added", "ws_kept", "ws_summed", "ws_turned", "x0_loaded", "x1_loaded", "y_kept",
            "y_ready", "y_turned",
        ]
        s = {n: sem(n) for n in names}
        norm_sems = {}
        for key in ("mix", "ffn", "ctx", "mix2", "ffn2"):
            norm_sems[key] = {n: sem(f"norm_{key}_{n}") for n in ("squared", "rstd", "tok", "turned", "kept")}
            if key in ("mix", "ffn", "ffn2"):
                norm_sems[key]["kept_odd"] = sem(f"norm_{key}_kept_odd")

        block = ctx.enter_context(nc.Block())

        def ktiles(w):
            return w.rearrange("(k p) n -> p k n", p=P)

        w_in, w_up, w_down = ktiles(a["w_in"]), ktiles(a["w_up"]), ktiles(a["w_down"])
        w_ba, w_bb, w_out = ktiles(a["w_branch_a"]), ktiles(a["w_branch_b"]), ktiles(a["w_out"])
        w_mod, w_in2 = ktiles(a["w_mod_2"]), ktiles(a["w_in_2"])
        w_out2, w_up2, w_down2 = ktiles(a["w_out_2"]), ktiles(a["w_ffn_in_2"]), ktiles(a["w_ffn_out_2"])

        wide = lambda name, n: bass.AP(a[name].tensor, 0, [[0, P], [1, n]])
        first = [(ident[:], a["t_ident"]), (g_mix, a["norm_mix"])]
        consts = [(cos[:], a["t_cos"]), (sin[:], a["t_sin"]),
                  (aq_bc, wide("a_q_norm", HD)), (ak_bc, wide("a_k_norm", HD)), (bq_norm, a["b_q_norm"]),
                  (bk_norm, a["b_k_norm"]), (mask_a[:], a["t_mask_a"]), (mask_b, a["t_mask_b"]),
                  (sink, wide("a_sink", 8)), (g_ffn, a["norm_ffn"]), (conv[:], a["conv"]),
                  (c_vec[:, 0:16], a["c_ctx_2"]), (c_vec[:, 16:32], a["c_2"]), (b_mod, a["b_mod_2"]),
                  (g_pre1, a["g_pre_mix_2"]), (g_post1, a["g_post_mix_2"]), (g_pre2, a["g_pre_ffn_2"]),
                  (g_post2, a["g_post_ffn_2"]), (out_g, a["gla_out_g_2"]), (ln_g, a["gmlp_ln_g_2"]),
                  (ln_b, a["gmlp_ln_b_2"]), (w_d[:], a["w_decay"])]
        N_CONSTS = len(consts)

        MIX_GROUPS = [("k", 2560), ("q", 2048), ("vv0", 3072), ("vv1", 3584), ("g0", 4096), ("g1", 4608),
                      ("v0", 1024), ("u0", 0), ("v1", 1536), ("u1", 512)]
        WOUT2_ORDER = [2, 3, 0, 1]
        PROJ = ["qa0", "qa1", "kv", "qb0", "qb1", "kb0", "kb1", "vb0", "vb1"]
        NORMED = PROJ[:7]

        sched = []
        for c in range(4):
            sched.append(("mm", 0, c))
        sched.append(("post", 0))
        sched += [("d",), ("la",)]
        for c in range(4):
            sched.append(("mm", 1, c))
            if c == 1:
                sched.append(("kt",))
            if c == 2:
                sched.append(("cum",))
        sched.append(("post", 1))
        for c in range(4):
            sched.append(("mm", 2, c))
            if c == 0:
                sched.append(("wst",))
            if c == 1:
                sched += [("rem", 0), ("rem", 1), ("wsum",)]
        sched.append(("post", 2))
        for c in range(4):
            sched.append(("mm", 3, c))
        sched.append(("post", 3))
        steps = []
        for n in range(2):
            steps.append([("level", n, 0), ("qe", n)])
            steps += [[("level", n, l)] for l in range(1, 8)] + [[("o", n)], [("y", n)]]
        slot = 0
        for g in range(4, 10):
            for c in range(4):
                sched.append(("mm", g, c))
                if slot == 0:
                    sched += [("upd", 0), ("upd", 1)]
                elif (g, c) not in ((7, 1), (9, 1)) and steps:
                    sched += steps.pop(0)
                if c == 0 and g > 4:
                    sched.append(("post", g - 1))
                if g in (7, 9) and c >= 2:
                    sched.append(("sgu", (g - 7) // 2, c - 2))
                slot += 1
        assert not steps
        sched += [("post", 9)]

        def down_jobs(g, c):
            at_ = {3: 0, 6: 1, 10: 2}.get(c)
            j = None if at_ is None else 11 * LOOP_JOBS + 3 * g + at_
            return [j] if j is not None and j < JOBS else []

        def group_done(eng, n_last):
            eng.wait_ge(weight_used, n_last + 1)

        def loaded(eng, n):
            eng.wait_ge(weight_loaded[n % SLOTS], 16 * (n // SLOTS + 1))

        def loaded_in(eng, n, i):
            eng.wait_ge(weight_loaded[n % SLOTS], i * 16 + 16 * (n // SLOTS + 1))

        @block.sync
        def _(sp):
            def load(n, src):
                if n >= SLOTS:
                    sp.wait_ge(weight_used, n - SLOTS + 1)
                sp.dma_start(ring[:, n % SLOTS, :, :], src).then_inc(weight_loaded[n % SLOTS], 16)

            def load_in(n, i, src):
                sp.wait_ge(weight_used, i * 8 + (n - SLOTS + 1))
                sp.dma_start(ring[:, n % SLOTS, :, :], src).then_inc(weight_loaded[n % SLOTS], 16)

            def cols(w, c, at):
                return w[:, CK * c:CK * c + CK, at:at + CN]

            sp.dma_start(x_tok[:, 0, :], a["x"][0:P, :]).then_inc(s["x0_loaded"], 16)
            sp.wait_ge(s["x1_loaded"], 16)
            for g in range(9):
                for c in range(4):
                    load(N_PROJ + 4 * g + c, cols(w_in, c, CN * g))
            with sp.Fori(0, 4) as i:
                for j in range(8):
                    load_in(N_GATE + j, i, w_in[:, CK * (j % 4):CK * (j % 4) + CK,
                                                bass.ds(i * 1024 + (4608 + CN * (j // 4)), CN)])
            for g in range(4):
                for c in range(4):
                    load(N_BRANCH + 4 * g + c, cols(w_ba if c < 2 else w_bb, c % 2, CN * g))
            for g in range(4):
                for c in range(4):
                    load(N_WOUT + 4 * g + c, cols(w_out, c, CN * g))

            def ffn(n_up, n_down, up, down):
                with sp.Fori(0, 11) as i:
                    for j in range(8):
                        load_in(n_up + j, i, up[:, CK * (j % 4):CK * (j % 4) + CK,
                                                bass.ds(i * CN + FF * (j // 4), CN)])
                for g in range(4):
                    for c in range(11):
                        load(n_down + 11 * g + c, cols(down, c, CN * g))

            ffn(N_UP, N_DOWN, w_up, w_down)
            for g, at_ in enumerate((2560, 3072, 3584)):
                for c in range(4):
                    load(N_CTX + 4 * g + c, cols(w_in2, c, at_))
            for g, (_, at_) in enumerate(MIX_GROUPS):
                for c in range(4):
                    load(N_MIX + 4 * g + c, cols(w_in2, c, at_))
            for g in range(4):
                for c in range(4):
                    load(N_WOUT2 + 4 * g + c, cols(w_out2, WOUT2_ORDER[c], CN * g))
            ffn(N_UP2, N_DOWN2, w_up2, w_down2)
            for h in range(2):
                for half in range(2):
                    sp.wait_ge(s["post_added"], 5 + 2 * h + half)
                    cols_ = slice(D // 2 * half, D // 2 * (half + 1))
                    sp.dma_start(out[h * P:(h + 1) * P, cols_], x_tok[:, h, cols_]).then_inc(s["out_stored"], 16)
            sp.wait_ge(s["out_stored"], 64)


        def keepers(key):
            return 2 if "kept_odd" in norm_sems[key] else 1

        def norm_kept(eng, key, pieces=8):
            eng.wait_ge(norm_sems[key]["kept"], pieces)
            if keepers(key) == 2:
                eng.wait_ge(norm_sems[key]["kept_odd"], pieces)

        def norm_bank(key, j, m):
            bank, at_ = (4 + j % 2, m * T) if keepers(key) == 1 else (4 + 2 * (j % 2) + m, 0)
            return PS[:, bank, at_:at_ + T]

        def block_half(v, size, half):
            v = v.rearrange("p (h m t) -> p h m t", h=GH, t=2 * size)
            return v[:, :, :, half * size:(half + 1) * size]

        def token_half(v, n, size, half):
            v = v[:, :, n * P:(n + 1) * P].rearrange("p h (m t) -> p h m t", t=2 * size)
            return v[:, :, :, half * size:(half + 1) * size]

        def bc(ap, shape):
            return ap.broadcast_to(shape)

        @block.tensor
        def _(pe):
            def chunk_tok(n, c, chunks, stat, bank, part=None):
                loaded(pe, n)
                for k in range(CK):
                    kt = CK * (c if part is None else part) + k
                    for h in range(2):
                        mm = pe.matmul(PS[:, bank + h, :], stat[:, kt, h * P:(h + 1) * P],
                                       ring[:, n % SLOTS, k, :], start=c + k == 0,
                                       stop=CK * c + k == CK * chunks - 1)
                mm.then_inc(weight_used, 1)

            def chunk_feat(n, c, chunks, mov, bank, i=None):
                loaded(pe, n) if i is None else loaded_in(pe, n, i)
                for k in range(CK):
                    kt = CK * c + k
                    for f in range(4):
                        mm = pe.matmul(PS[:, bank + f // 2, (f % 2) * T:(f % 2) * T + T],
                                       ring[:, n % SLOTS, k, f * P:(f + 1) * P], mov[:, kt, :],
                                       start=kt == 0 and f % 2 == 0, stop=kt == CK * chunks - 1,
                                       skip_group_check=True)
                mm.then_inc(weight_used, 1)

            def norm_piece(key, j, src):
                n = norm_sems[key]
                pe.wait_ge(n["tok"], j + 1)
                if j >= 2:
                    norm_kept(pe, key, j - 1)
                for m in range(2):
                    for h in range(2):
                        mm = pe.transpose(norm_bank(key, j, m)[:, h * P:(h + 1) * P],
                                          src[:, j % src.shape[1], h, m * P:(m + 1) * P], ident[:])
                mm.then_inc(n["turned"], 1)

            def norm_ahead(key, c, src):
                for j in range(4) if c == 0 else (2 * c + 2, 2 * c + 3) if c < 3 else ():
                    norm_piece(key, j, src)
                norm_kept(pe, key, 2 * c + 2)

            def turn(n):
                pe.wait_ge(s["proj_free"], n + 1)
                if n >= 1:
                    pe.wait_ge(s["qkv_kept"], n)
                heads = 2 if NORMED[n] == "kv" else 4
                for hd in range(heads):
                    for h in range(2):
                        at_ = (h * heads + hd) * P
                        mm = pe.transpose(PS[:, 4 + hd // 2, (hd % 2) * T + h * P:(hd % 2) * T + (h + 1) * P],
                                          tmp[1][:, at_:at_ + P], ident[:])
                mm.then_inc(s["turned"], 1)

            def mod_sum(done, odd):
                pe.wait_ge(s["job_acc"], done + 1)
                pe.wait_ge(s["job_kept"], done + 1)
                for q in range(4):
                    mm = pe.transpose(PS[:, 6 + odd, q * P:(q + 1) * P], acc[:, odd, q * P:(q + 1) * P], ident[:])
                mm.then_inc(s["job_summed"], 1)

            pe.sem_inc(s["attn_done"], 1)
            pe.wait_ge(s["first_loaded"], 32)

            for g in range(9):
                for c in range(4):
                    if g == 0:
                        norm_ahead("mix", c, norm_tmp)
                    elif g >= 2 and c == 0:
                        pe.wait_ge(s["proj_free"], g - 1)
                    chunk_tok(N_PROJ + 4 * g + c, c, 4, act_t, 2 * (g % 2))
                    if c == 2 and 1 <= g <= len(NORMED):
                        turn(g - 1)

            pe.wait_ge(s["qkv_kept"], 7)
            pe.wait_ge(s["proj_free"], 8)
            pe.sem_inc(s["job_summed"], 1)
            with pe.Fori(0, 4) as i:
                for u in range(2):
                    done = i * 2 + u
                    pe.wait_ge(s["head_staged"], done + 1)
                    for n, keys in ((0, ka_t[:, i // 2, :]), (1, kb_t[:, done, :])):
                        for b in range(2):
                            mm = pe.matmul(PS[:, 4 + n, b * T:(b + 1) * T], q_head[n][:, b * P:(b + 1) * P],
                                           keys, start=True, stop=True)
                    mm.then_inc(s["scores_done"], 1)
                    pe.wait_ge(s["gate_kept"], done + 1)
                    for c in range(4):
                        chunk_feat(N_GATE + 4 * u + c, c, 4, act_t, 2, i)
                        if c == 1:
                            pe.wait_ge(s["probs_ready"], done + 1)
                            for n, probs in ((0, score_a), (1, score_b)):
                                for b in range(2):
                                    for k in range(2):
                                        mm = pe.transpose(PS[:, 6 + n, k * T + b * P:k * T + (b + 1) * P],
                                                          probs[:, b, k * P:(k + 1) * P], ident[:])
                            mm.then_inc(s["probs_turned"], 1)
                        if c == 2:
                            pe.wait_ge(s["probs_t_ready"], done + 1)
                            pe.wait_ge(s["proj_free"], 9)
                            for n, probs in ((0, pt_a), (1, pt_b)):
                                for k in range(2):
                                    mm = pe.matmul(PS[:, n, 0:T], v_head[n][:, k, :], probs[:, k, :],
                                                   start=k == 0, stop=k == 1)
                            mm.then_inc(s["attn_done"], 1)

            pe.wait_ge(s["attn_kept"], 8)
            pe.wait_ge(s["gate_kept"], 9)
            for g in range(4):
                if g >= 2:
                    pe.wait_ge(s["merged"], g - 1)
                for c in range(4):
                    chunk_feat(N_BRANCH + 4 * g + c, c % 2, 2, oa_t if c < 2 else ob_t, 4 * (g % 2) + 2 * (c // 2))

            for g in range(4):
                pe.wait_ge(s["merged"], 3 + g // 2)
                for c in range(4):
                    pe.wait_ge(s["merged"], max(c + 1, 3 + g // 2))
                    chunk_tok(N_WOUT + 4 * g + c, c, 4, gates, 2 * g)

            def up_value(n, done, i=None):
                pe.wait_ge(s["up_v_free"], done + 1)
                for c in range(4):
                    chunk_feat(n + c, c, 4, act_t, 2, i)
                for odd in range(2):
                    mod_sum(done * LOOP_JOBS + odd, odd)

            for c in range(4):
                norm_ahead("ffn", c, norm_tmp)
                chunk_feat(N_UP + c, c, 4, act_t, 0)
            with pe.Fori(0, 10) as i:
                up_value(N_UP + 4, i, i)
                pe.wait_ge(s["up_g_free"], i + 1)
                for c in range(4):
                    chunk_feat(N_UP + 8 + c, c, 4, act_t, 0, i)
            up_value(N_UP + 84, 10)
            pe.wait_ge(s["hidden_ready"], 11)
            pe.wait_ge(s["up_g_free"], 11)
            for g in range(4):
                if g >= 2:
                    pe.wait_ge(s["down_added"], g - 1)
                for c in range(11):
                    if g == 0 and c == 10:
                        pe.wait_ge(s["hidden_ready"], 12)
                    chunk_tok(N_DOWN + 11 * g + c, c, 11, hidden, 2 * (g % 2))
                    for j in down_jobs(g, c):
                        mod_sum(j, j % 2)
                    if g == 3 and c >= 3:
                        norm_piece("ctx", c - 3, norm_tmp_c)

            def decay_proj(src, m):
                for k in range(KD):
                    mm = pe.matmul(PS[0:2 * RANK, 7, 0:T], w_d[:, k, :], src[:, k, :], start=k == 0,
                                   stop=k == KD - 1)
                mm.then_inc(s["d_done"], 1)

            def log_decay(m):
                pe.wait_ge(s["d_kept"], m + 1)
                pe.wait_ge(s["wd2_loaded"], 64)
                for h in range(2):
                    for r in range(2):
                        mm = pe.matmul(PS[:, 4 + 2 * h + r, :], d_t[:, h * P:(h + 1) * P],
                                       wd2[:, r * 512:(r + 1) * 512], start=True, stop=True)
                mm.then_inc(s["la_done"], 1)

            norm_kept(pe, "ctx")
            decay_proj(act_t, 0)
            for g in range(3):
                if g == 0:
                    pe.wait_ge(s["down_added"], 3)
                if g == 1:
                    pe.wait_ge(s["down_added"], 4)
                if g == 2:
                    pe.wait_ge(s["ctx_kept"], 1)
                for c in range(4):
                    chunk_tok(N_CTX + 4 * g + c, c, 4, act_t, 2 * (g % 2))
                    if g == 0 and c == 1:
                        log_decay(0)
                    if g == 1 and c == 0:
                        pe.wait_ge(s["masks_loaded"], 32)
                        pe.wait_ge(s["la_ready"], 1)
                        for r in range(2):
                            for h in range(2):
                                other = 1 - h
                                whole = (h == 0) if r == 0 else (h == 1)
                                mm = pe.matmul(PS[:, 4 + 2 * r + h, :], tri[:, 2 + r, :], la[:, h, r, :],
                                               start=True, stop=not whole)
                                if whole:
                                    mm = pe.matmul(PS[:, 4 + 2 * r + h, :], ones[:], la[:, other, r, :],
                                                   start=False, stop=True)
                        mm.then_inc(s["rem_done"], 1)
                    if (g, c) in ((1, 2), (1, 3), (2, 0), (2, 1)):
                        pe.wait_ge(s["rem_exp"], 1)
                        at_ = 2 * (4 * (g - 1) + c - 2)
                        norm_piece("mix2", at_, norm_tmp2)
                        norm_piece("mix2", at_ + 1, norm_tmp2)
            pe.wait_ge(s["ctx_kept"], 3)
            for r in range(2):
                pe.wait_ge(s["kdec_ready"], r + 1)
                for hd in range(GH):
                    for h in range(2):
                        mm = pe.matmul(PS[:, 4 + 2 * r + hd // 2, (hd % 2) * T:(hd % 2) * T + T],
                                       e_buf[:, h, hd * P:(hd + 1) * P] if r == 0 else qe[:, h, hd * P:(hd + 1) * P],
                                       vvc[:, h, hd * T:(hd + 1) * T], start=h == 0 and hd % 2 == 0, stop=h == 1,
                                       skip_group_check=True)
                mm.then_inc(s["state_done"], 1)

            def mix_bank(g):
                return 2 * (g % 2)

            lv = 0
            for item in sched:
                if item[0] == "mm":
                    _, g, c = item
                    if c == 0:
                        if g == 0:
                            norm_kept(pe, "mix2")
                        if g >= 2:
                            pe.wait_ge(s["grp_free"], g - 1)
                    kind = MIX_GROUPS[g][0]
                    if kind[0] in "kv":
                        chunk_tok(N_MIX + 4 * g + c, c, 4, hx_t, mix_bank(g))
                    else:
                        chunk_feat(N_MIX + 4 * g + c, c, 4, hx_t, mix_bank(g))
                elif item[0] == "d":
                    pe.wait_ge(s["state_ready"], 2)
                    decay_proj(hx_t, 1)
                elif item[0] == "la":
                    norm_kept(pe, "mix2")
                    log_decay(1)
                elif item[0] == "kt":
                    pe.wait_ge(s["grp_free"], 1)
                    pe.wait_ge(s["la_ready"], 2)
                    for hd in range(GH):
                        for h in range(2):
                            mm = pe.transpose(PS[:, 4 + hd // 2, (hd % 2) * T + h * P:(hd % 2) * T + (h + 1) * P],
                                              k_tok[:, h, hd * P:(hd + 1) * P], ident[:])
                    mm.then_inc(s["kt_done"], 1)
                elif item[0] == "cum":
                    pe.wait_ge(s["kt_kept"], 1)
                    for n in range(2):
                        for r in range(2):
                            for hd in range(GH):
                                mm = pe.matmul(PS[:, 4 + 2 * n + r, hd * P:(hd + 1) * P],
                                               la[:, n, r, hd * P:(hd + 1) * P], tri[:, r, :], start=True, stop=True)
                    mm.then_inc(s["cum_done"], 1)
                elif item[0] == "wst":
                    pe.wait_ge(s["cum_kept"], 1)
                    pe.wait_ge(s["mixer_loaded"], 16)
                    for hd in range(8):
                        mm = pe.transpose(PS[:, 4 + hd // 4, (hd % 4) * P:(hd % 4 + 1) * P],
                                          v_sgu[:, hd * P:(hd + 1) * P], ident[:])
                    mm.then_inc(s["ws_turned"], 1)
                elif item[0] == "wsum":
                    pe.wait_ge(s["ws_kept"], 1)
                    for hd in range(8):
                        mm = pe.matmul(PS[:, 4 + hd // 4, (hd % 4) * P:(hd % 4 + 1) * P], ones[:], ws_t[:, hd, :],
                                       start=True, stop=True)
                    mm.then_inc(s["ws_summed"], 1)
                elif item[0] == "rem":
                    r = item[1]
                    mm = pe.matmul(PS[:, 6 + r, :], tri[:, 2 + r, :], la[:, r, r, :], start=True, stop=True)
                    mm.then_inc(s["rem_done"], 1)
                elif item[0] == "upd":
                    r = item[1]
                    pe.wait_ge(s["kdec_ready"], 3 + r)
                    pe.wait_ge(s["grp_free"], 4)
                    pe.wait_ge(s["bs_added"], 1)
                    for hd in range(GH):
                        mm = pe.matmul(PS[:, 4 + 2 * r + hd // 2, (hd % 2) * T:(hd % 2) * T + T],
                                       e_buf[:, r, hd * P:(hd + 1) * P], vv[:, r, hd * T:(hd + 1) * T],
                                       start=True, stop=True)
                    mm.then_inc(s["state_done"], 1)
                elif item[0] == "level":
                    pe.wait_ge(s["lv_q"], lv + 1)
                    pe.wait_ge(s["lv_k"], lv + 1)
                    if lv:
                        pe.wait_ge(s["lv_taken"], lv)
                    else:
                        pe.wait_ge(s["state_ready"], 4)
                    for hd in range(GH):
                        mm = pe.matmul(PS[:, 4, hd * P:(hd + 1) * P], kl[:, lv % 2, hd * P:(hd + 1) * P],
                                       ql[:, lv % 2, hd * P:(hd + 1) * P], start=True, stop=True)
                    mm.then_inc(s["lv_done"], 1)
                    lv += 1
                elif item[0] == "o":
                    n = item[1]
                    pe.wait_ge(s["lv_taken"], 8 * (n + 1))
                    pe.wait_ge(s["qe_ready"], n + 1)
                    if n == 1:
                        pe.wait_ge(s["y_ready"], 1)
                    for hd in range(GH):
                        o = PS[:, 6 + hd // 2, (hd % 2) * T:(hd % 2) * T + T]
                        pe.matmul(o, s_t[:, hd, :], vv[:, n, hd * T:(hd + 1) * T], start=True, stop=False)
                        for r in range(2):
                            mm = pe.matmul(o, qe[:, r, hd * P:(hd + 1) * P],
                                           state[:, r, n if r == 0 else 1 - n, hd * T:(hd + 1) * T],
                                           start=False, stop=r == 1)
                    mm.then_inc(s["o_done"], 1)
                elif item[0] == "y":
                    n = item[1]
                    pe.wait_ge(s["y_ready"], n + 1)
                    if n == 1:
                        pe.wait_ge(s["y_kept"], 1)
                    for f in range(8):
                        mm = pe.transpose(PS[:, 6 + f // 4, (f % 4) * P:(f % 4 + 1) * P],
                                          y_tok[:, f * P:(f + 1) * P], ident[:])
                    mm.then_inc(s["y_turned"], 1)
                elif item[0] == "sgu":
                    _, m, n = item
                    pe.wait_ge(s["sgu_ready"], m + 1)
                    if m + n:
                        pe.wait_ge(s["sgu_taken"], 2 * m + n)
                    for hd in range(4):
                        mm = pe.matmul(PS[:, 5, hd * P:(hd + 1) * P],
                                       v_sgu[:, n * 512 + hd * P:n * 512 + (hd + 1) * P],
                                       ws_t[:, 4 * m + hd, :], start=True, stop=True)
                    mm.then_inc(s["sgu_mixed"], 1)

            def spread_gate(m, j):
                pe.wait_ge(s["post_w"], 4 * m + j + 1)
                if m + j:
                    pe.wait_ge(s["post_bc_kept"], 4 * m + j)
                for f in range(4):
                    mm = pe.matmul(PS[:, 7, f * P:(f + 1) * P], gate_w[:, j % 2, f, :], ident[:],
                                   start=True, stop=True)
                mm.then_inc(s["post_bc"], 1)

            for g in range(4):
                if g == 0:
                    pe.wait_ge(s["y_kept"], 2)
                elif g == 1:
                    pe.wait_ge(s["grp_free"], 10)
                else:
                    pe.wait_ge(s["post_scaled"], g - 1)
                for c in range(4):
                    if c == 3:
                        pe.wait_ge(s["cat_ready"], 2)
                    chunk_tok(N_WOUT2 + 4 * g + c, c, 4, cat_t, 2 * (g % 2), WOUT2_ORDER[c])
                    if g == 0:
                        spread_gate(0, c)

            for c in range(4):
                norm_ahead("ffn2", c, norm_tmp)
                chunk_feat(N_UP2 + c, c, 4, act_t, 0)
            with pe.Fori(0, 10) as i:
                pe.wait_ge(s["hidden2_ready"], i + 1)
                for c in range(4):
                    chunk_feat(N_UP2 + 4 + c, c, 4, act_t, 2, i)
                pe.wait_ge(s["up2_g_free"], i + 1)
                for c in range(4):
                    chunk_feat(N_UP2 + 8 + c, c, 4, act_t, 0, i)
            pe.wait_ge(s["hidden2_ready"], 11)
            for c in range(4):
                chunk_feat(N_UP2 + 84 + c, c, 4, act_t, 2)
            pe.wait_ge(s["up2_g_free"], 11)
            for g in range(4):
                if g >= 2:
                    pe.wait_ge(s["post_scaled"], 4 + g - 1)
                for c in range(11):
                    if g == 0 and c == 10:
                        pe.wait_ge(s["hidden2_ready"], 12)
                    chunk_tok(N_DOWN2 + 11 * g + c, c, 11, hidden, 2 * (g % 2))
                    if g == 0 and c < 4:
                        spread_gate(1, c)

        @block.vector
        def _(ve):
            def norm(key, src, dst, kept=None, gain=None, shift=None):
                n = norm_sems[key]
                ve.wait_ge(n["rstd"], 1)

                def keep(j):
                    kt = 2 * j + 1
                    ve.wait_ge(n["turned"], j + 1)
                    ps = norm_bank(key, j, 1)
                    if shift is None:
                        op = ve.tensor_scalar(kept[:, kt, :], ps, gain[:, kt:kt + 1], None, ALU.mult)
                    else:
                        op = ve.tensor_scalar(kept[:, kt, :], ps, gain[:, kt:kt + 1], shift[:, kt:kt + 1],
                                              ALU.mult, ALU.add)
                    op.then_inc(n["kept_odd"], 1)

                for j in range(8):
                    if kept is not None and j >= 2:
                        keep(j - 2)
                    if j >= dst.shape[1]:
                        ve.wait_ge(n["turned"], j - 3)
                    for h in range(2):
                        op = ve.tensor_scalar(dst[:, j % dst.shape[1], h, :], src[:, h, j * T:(j + 1) * T],
                                              norm_rs[:, h:h + 1], None, ALU.mult)
                    op.then_inc(n["tok"], 1)
                if kept is not None:
                    keep(6)
                    keep(7)

            def pair(bank, width=512):
                return PS[:, bank:bank + 2, 0:width]

            ve.memset(d_t[2 * RANK:2 * RANK + 1, :], 1.0)
            ve.sem_inc(s["bias_used"], 1)
            ve.wait_ge(s["x0_loaded"], 16)
            ve.wait_ge(s["x1_loaded"], 16)
            ve.wait_ge(s["first_loaded"], 32)
            norm("mix", x_tok, norm_tmp, act_t, g_mix)
            ve.wait_ge(s["consts_loaded"], 16 * N_CONSTS)

            for g, kind in enumerate(PROJ):
                if g >= len(NORMED):
                    group_done(ve, N_PROJ + 4 * g + 3)
                    at_ = 512 * (g - len(NORMED))
                    ve.tensor_copy(vb[:, :, at_:at_ + 512], pair(2 * (g % 2))).then_inc(s["proj_free"], 1)
                    continue
                heads = 2 if kind == "kv" else 4
                w = heads * HD
                sq, tok, rot = (t[:, 0:2 * w].rearrange("p (h n d) -> p h n d", h=2, d=HD) for t in tmp)
                ve.wait_ge(s["squared"], g + 1)
                ve.tensor_reduce(ss[:, 0:2 * heads], tmp[0][:, 0:2 * w].rearrange("p (n d) -> p n d", d=HD),
                                 AX, ALU.add).then_inc(s["summed"], 1)
                ve.wait_ge(s["rstd_ready"], g + 1)
                if g:
                    ve.wait_ge(s["turned"], g)
                ps = pair(2 * (g % 2), w).rearrange("p h (n d) -> p h n d", d=HD)
                rstd = rs[:, 0:2 * heads].rearrange("p (h n) -> p h n", h=2).unsqueeze(3)
                op = ve.tensor_tensor(tok, ps, bc(rstd, [P, 2, heads, HD]), ALU.mult)
                if g < 3:
                    if kind == "kv":
                        ve.tensor_copy(va[:], PS[:, 2 * (g % 2):2 * (g % 2) + 2, 256:512])
                    ve.drain()
                    flat = tmp[1][:, 0:2 * w].rearrange("p (n d) -> p n d", d=HD)
                    weight = (ak_bc if kind == "kv" else aq_bc).unsqueeze(1)
                    ve.tensor_tensor(flat, flat, bc(weight, [P, 2 * heads, HD]), ALU.mult)
                    ve.drain()
                    ve.tensor_tensor(sq, tok, bc(cos.unsqueeze(2), [P, 2, heads, HD]), ALU.mult)
                    half = HD // 2
                    lo = bc(sin[:, :, 0:half].unsqueeze(2), [P, 2, heads, half])
                    hi = bc(sin[:, :, half:HD].unsqueeze(2), [P, 2, heads, half])
                    ve.tensor_tensor(rot[:, :, :, 0:half], tok[:, :, :, half:HD], lo, ALU.mult)
                    ve.tensor_tensor(rot[:, :, :, half:HD], tok[:, :, :, 0:half], hi, ALU.mult)
                    ve.drain()
                    op = ve.tensor_tensor(tmp[1][:, 0:2 * w], tmp[0][:, 0:2 * w], tmp[2][:, 0:2 * w], ALU.add)
                op.then_inc(s["proj_free"], 1)

            scale = 1.0 / math.sqrt(HD)
            with ve.Fori(0, 4) as i:
                for u in range(2):
                    done = i * 2 + u
                    sink_col = sink[:, bass.ds(i * 2 + u, 1)]
                    ve.wait_ge(s["bias_loaded"], done * 64 + 64)
                    ve.wait_ge(s["scores_done"], done + 1)
                    ps = PS[:, 4:6, :].rearrange("p a (b t) -> p a b t", t=T)
                    ve.scalar_tensor_tensor(score_a[:], ps[:, 0], scale, mask_a[:], ALU.mult, ALU.add)
                    ve.scalar_tensor_tensor(score_b[:], ps[:, 1], scale, bias[:], ALU.mult, ALU.add)\
                        .then_inc(s["bias_used"], 1)
                    ve.drain()
                    ve.tensor_tensor(score_b[:], score_b[:], bc(mask_b.unsqueeze(1), [P, 2, T]), ALU.add)
                    ve.tensor_reduce(mx[:, 0:2], score_a[:], AX, ALU.max)
                    ve.drain()
                    ve.tensor_reduce(mx[:, 2:4], score_b[:], AX, ALU.max)
                    ve.tensor_scalar(mx[:, 0:2], mx[:, 0:2], sink_col, None, ALU.max)
                    ve.drain()
                    ve.tensor_scalar(mx[:, 4:8], mx[:, 0:4], -1.0, None, ALU.mult).then_inc(s["max_ready"], 1)
                    ve.wait_ge(s["exps_done"], done + 1)
                    ve.tensor_tensor(den[:, 0:2], den[:, 0:2], den[:, 4:6], ALU.add)
                    ve.drain()
                    ve.reciprocal(den[:, 4:8], den[:, 0:4])
                    ve.drain()
                    for n, probs in ((0, score_a), (1, score_b)):
                        for b in range(2):
                            op = ve.tensor_scalar(probs[:, b, :], probs[:, b, :],
                                                  den[:, 4 + 2 * n + b:5 + 2 * n + b], None, ALU.mult)
                    op.then_inc(s["probs_ready"], 1)

            for g in range(4):
                banks = 4 * (g % 2)
                ga = gates[:, 4 * g:4 * g + 4, :].rearrange("p (a b) t -> p a (b t)", a=2)
                gb = gates[:, 16 + 4 * g:20 + 4 * g, :].rearrange("p (a b) t -> p a (b t)", a=2)
                ve.wait_ge(s["gates_squashed"], g + 1)
                group_done(ve, N_BRANCH + 4 * g + 3)
                ve.tensor_tensor(ga, ga, pair(banks), ALU.mult)
                ve.tensor_tensor(gb, gb, pair(banks + 2), ALU.mult)
                ve.drain()
                ve.tensor_tensor(ga, ga, gb, ALU.add).then_inc(s["merged"], 1)

            for g in range(4):
                group_done(ve, N_WOUT + 4 * g + 3)
                part = x_tok[:, :, CN * g:CN * (g + 1)]
                ve.tensor_tensor(part, part, pair(2 * g), ALU.add).then_inc(s["wout_added"], 1)
            norm("ffn", x_tok, norm_tmp, act_t, g_ffn)

            def rows_times(load, c, sums, fresh):
                if not fresh:
                    ve.drain()
                ve.wait_ge(s[f"wmod_loaded{c}"], load * 16 + 16)
                for k in range(CK):
                    if k:
                        ve.drain()
                    for odd, c_at in sums:
                        col = c_vec[:, c_at + CK * c + k:c_at + CK * c + k + 1]
                        if fresh and k == 0:
                            op = ve.tensor_scalar(acc[:, odd, :], wmod[:, c, k, :], col, None, ALU.mult)
                        else:
                            op = ve.scalar_tensor_tensor(acc[:, odd, :], wmod[:, c, k, :], col, acc[:, odd, :],
                                                         ALU.mult, ALU.add)
                op.then_inc(s["wmod_used"], 1)

            def job(j, odd):
                ve.wait_ge(s["job_summed"], j)
                for c in range(4):
                    rows_times(j - SHARED, c, ((odd, 16),), c == 0)
                ve.drain().then_inc(s["job_acc"], 1)

            def keep_job(j, odd, col=None):
                ve.wait_ge(s["job_summed"], j + 2)
                ve.tensor_reduce(mod[:, bass.ds(j * 4 if col is None else col, 4)],
                                 PS[:, 6 + odd, :].rearrange("p (q r) -> p q r", r=P), AX, ALU.add)\
                    .then_inc(s["job_kept"], 1)

            def conv_sides(dst, bank, i, at_):
                for side in range(2):
                    for f in range(4):
                        ps = PS[:, bank + f // 2, (f % 2) * T:(f % 2) * T + T]
                        w = conv[:, bass.ds(i * 4 + (at_ + f), 1), 2 * side]
                        if side == 0:
                            o, src = dst[:, f, 1:T], ps[:, 0:T - 1]
                        else:
                            o, src = dst[:, f, 0:T - 1], ps[:, 1:T]
                        op = ve.scalar_tensor_tensor(o, src, w, o, ALU.mult, ALU.add)
                    if side == 0:
                        ve.drain()
                return op

            ve.wait_ge(s["c_ready"], 1)
            for name, free in (("up_v_free", 1), ("hidden_ready", 1), ("job_kept", 2)):
                ve.sem_inc(s[name], free)
            def conv_gate(i):
                ve.wait_ge(s["up_g_based"], i + 1)
                conv_sides(conv_g, 0, i, 0).then_inc(s["up_g_free"], 1)

            def conv_value(i):
                ve.wait_ge(s["up_v_based"], i + 1)
                conv_sides(conv_v, 2, i, KF).then_inc(s["up_v_free"], 1)
                ve.drain()
                ve.wait_ge(s["up_g_act"], i + 1)
                ve.tensor_tensor(hidden[:, bass.ds(i * 4, 4), :], conv_g[:], conv_v[:], ALU.mult)\
                    .then_inc(s["hidden_ready"], 1)

            with ve.Fori(0, SHARED) as i:
                both = ((0, 0), (1, 16))
                ve.wait_ge(s["job_summed"], i * LOOP_JOBS + 1)
                for c in range(2):
                    rows_times(i, c, both, c == 0)
                conv_gate(i)
                for c in range(2, 4):
                    rows_times(i, c, both, False)
                ve.drain().then_inc(s["job_acc"], 2)
                conv_value(i)
                keep_job(i * LOOP_JOBS, 0, i * 4)
                keep_job(i * LOOP_JOBS + 1, 1, i * 4 + 4 * SHARED)
            with ve.Fori(SHARED, 11) as i:
                job(i * LOOP_JOBS, 0)
                conv_gate(i)
                job(i * LOOP_JOBS + 1, 1)
                conv_value(i)
                for odd in range(2):
                    keep_job(i * LOOP_JOBS + odd, odd)

            ve.drain()
            ve.tensor_tensor(mod[:, 0:32], mod[:, 0:32], b_mod[:, 0:32], ALU.add)
            ve.drain()
            ve.scalar_tensor_tensor(scale_c, mod[:, 16:32], 1.0, g_pre1, ALU.add, ALU.mult)\
                .then_inc(s["mod_ready"], 1)
            for g in range(4):
                for c in range(11):
                    for j in down_jobs(g, c):
                        job(j, j % 2)
                        keep_job(j, j % 2)
                if g == 3:
                    norm("ctx", ctx_tok, norm_tmp_c)
                group_done(ve, N_DOWN + 11 * g + 10)
                part = x_tok[:, :, CN * g:CN * (g + 1)]
                ve.tensor_tensor(part, part, pair(2 * (g % 2)), ALU.add).then_inc(s["down_added"], 1)
            ve.drain()
            ve.tensor_tensor(mod[:, 32:128], mod[:, 32:128], b_mod[:, 0:96], ALU.add)
            ve.drain()
            ve.scalar_tensor_tensor(scale_x1, mod[:, 48:64], 1.0, g_pre1, ALU.add, ALU.mult)
            ve.scalar_tensor_tensor(scale_x2, mod[:, 96:112], 1.0, g_pre2, ALU.add, ALU.mult)\
                .then_inc(s["mod_ready"], 1)
            norm("mix2", x_tok, norm_tmp2)

            def log_decay(m):
                ve.wait_ge(s["la_exp"], m + 1)
                flat = la.rearrange("p a b c -> p (a b) c")
                ve.scalar_tensor_tensor(flat, PS[:, 4:8, :], 0.0, flat, ALU.min, ALU.subtract)
                ve.drain()
                ve.tensor_scalar(flat, flat, 1.0 / TAU, None, ALU.mult).then_inc(s["la_ready"], 1)

            log_decay(0)
            ve.wait_ge(s["rem_exp"], 1)
            ve.wait_ge(s["ctx_kept"], 1)
            for r, k in ((0, e_buf), (1, qe)):
                ve.tensor_tensor(k[:], k[:], kc_tok[:], ALU.mult).then_inc(s["kdec_ready"], 1)

            lv, taken = 0, 0
            ve.wait_ge(s["masks_loaded"], 32)

            def take(upto):
                nonlocal taken
                while taken < upto:
                    ve.wait_ge(s["lv_done"], taken + 1)
                    mask = bc(level_mask[:, taken % 8, :].unsqueeze(1), [P, GH, P]).bitcast(I32)
                    ve.copy_predicated(s_t[:], mask, PS[:, 4, :].rearrange("p (h i) -> p h i", i=P))\
                        .then_inc(s["lv_taken"], 1)
                    ve.drain()
                    taken += 1

            for item in sched:
                if item[0] == "la":
                    log_decay(1)
                elif item[0] == "rem":
                    r = item[1]
                    ve.wait_ge(s["rem_exp"], 2 + r)
                    ve.tensor_tensor(e_buf[:, r, :], e_buf[:, r, :], k_tok[:, r, :], ALU.mult)\
                        .then_inc(s["kdec_ready"], 1)
                elif item[0] == "upd":
                    r = item[1]
                    ve.wait_ge(s["state_done"], 3 + r)
                    ve.wait_ge(s["decay_ready"], r + 1)
                    for hd in range(GH):
                        op = ve.scalar_tensor_tensor(state[:, r, 1, hd * T:(hd + 1) * T],
                                                     state[:, r, 0, hd * T:(hd + 1) * T],
                                                     decay[:, 4 * r + hd:4 * r + hd + 1],
                                                     PS[:, 4 + 2 * r + hd // 2, (hd % 2) * T:(hd % 2) * T + T],
                                                     ALU.mult, ALU.add)
                    op.then_inc(s["state_ready"], 1)
                    if r == 1:
                        ve.memset(s_t[:], 0.0)
                elif item[0] == "qe":
                    n = item[1]
                    ve.wait_ge(s["qe_exp"], n + 1)
                    ve.wait_ge(s["grp_free"], 2)
                    qe4 = qe.rearrange("p r (h i) -> p r h i", i=P)
                    for r in range(2):
                        op = ve.tensor_tensor(qe4[:, r], qe4[:, r], q_t[:, :, n * P:(n + 1) * P], ALU.mult)
                    op.then_inc(s["qe_ready"], 1)
                elif item[0] == "level":
                    _, n, l = item
                    if n and l == 0:
                        ve.wait_ge(s["o_done"], 1)
                    if l < 7:
                        size = LEVELS[l]
                        if lv:
                            ve.drain()
                            ve.wait_ge(s["lv_k"], lv)
                        for r in range(2):
                            b = b_t[:, n, r, :].rearrange("p (m t) -> p m t", t=2 * size)
                            ref = bc(b[:, :, size - 1 + r:size + r], [P, 256 // size, 2 * size])
                            op = ve.tensor_tensor(e_buf[:, r, :].rearrange("p (m t) -> p m t", t=2 * size), b, ref,
                                                  ALU.subtract)
                        op.then_inc(s["lv_diff"], 1)
                        take(lv)
                        ve.wait_ge(s["lv_exp"], lv + 1 - n)
                        if lv >= 2:
                            ve.wait_ge(s["lv_done"], lv - 1)
                        for half in range(2):
                            op = ve.tensor_tensor(block_half(ql[:, lv % 2, :], size, half),
                                                  token_half(q_t, n, size, half),
                                                  block_half(e_buf[:, 1 - half, :], size, half), ALU.mult)
                        op.then_inc(s["lv_q"], 1)
                    else:
                        take(lv)
                        ve.tensor_scalar(ql[:, lv % 2, :].rearrange("p (h i) -> p h i", i=P),
                                         q_t[:, :, n * P:(n + 1) * P], 2.0, None, ALU.mult).then_inc(s["lv_q"], 1)
                    lv += 1
                elif item[0] == "o":
                    n = item[1]
                    take(8 * (n + 1))
                    ve.wait_ge(s["o_sq"], n + 1)
                    ve.tensor_reduce(ss[:, 0:4], y_tok.rearrange("p (h e) -> p h e", e=T), AX, ALU.add)\
                        .then_inc(s["o_sum"], 1)
                    ve.wait_ge(s["o_rs"], n + 1)
                    ve.tensor_tensor(y_tok.rearrange("p (h e) -> p h e", e=T),
                                     PS[:, 6:8, :].rearrange("p a (b e) -> p (a b) e", e=T),
                                     bc(rs[:, 0:4].unsqueeze(2), [P, 4, T]), ALU.mult).then_inc(s["y_ready"], 1)
                elif item[0] == "y":
                    n = item[1]
                    ve.wait_ge(s["y_turned"], n + 1)
                    ve.wait_ge(s["grp_free"], 6)
                    for f in range(8):
                        c = cat_t[:, 8 + f, n * P:(n + 1) * P]
                        op = ve.scalar_tensor_tensor(c, PS[:, 6 + f // 4, (f % 4) * P:(f % 4 + 1) * P],
                                                     out_g[:, f:f + 1], c, ALU.mult, ALU.mult)
                    op.then_inc(s["y_kept"], 1)
                elif item[0] == "wsum":
                    ve.wait_ge(s["ws_summed"], 1)
                    ve.wait_ge(s["bs_loaded"], 16)
                    for hd in range(8):
                        op = ve.scalar_tensor_tensor(bs_bc[:, hd, :], PS[:, 4 + hd // 4, (hd % 4) * P:(hd % 4 + 1) * P],
                                                     ln_b[:, hd:hd + 1], bs_bc[:, hd, :], ALU.mult, ALU.add)
                    op.then_inc(s["bs_added"], 1)
                elif item[0] == "post" and MIX_GROUPS[item[1]][0] in ("u0", "u1"):
                    m = int(MIX_GROUPS[item[1]][0][1])
                    ve.wait_ge(s["grp_free"], item[1] + 1)
                    ve.drain()
                    u_part = cat_t[:, 4 * m:4 * m + 4, :].rearrange("p h t -> p (h t)")
                    ve.tensor_tensor(u_part, u_part, v_tmp, ALU.mult).then_inc(s["cat_ready"], 1)
                elif item[0] == "post" and MIX_GROUPS[item[1]][0] in ("v0", "v1"):
                    m = int(MIX_GROUPS[item[1]][0][1])
                    v3 = v_sgu.rearrange("p (n d) -> p n d", d=HD)
                    ve.wait_ge(s["grp_free"], item[1] + 1)
                    ve.tensor_reduce(mean[:, 0:8], v3, AX, ALU.add)
                    ve.drain()
                    ve.tensor_scalar(mean[:, 0:8], mean[:, 0:8], -1.0 / HD, None, ALU.mult)
                    ve.drain()
                    ve.tensor_tensor(v3, v3, bc(mean[:, 0:8].unsqueeze(2), [P, 8, HD]), ALU.add)\
                        .then_inc(s["sgu_centred"], 1)
                    ve.wait_ge(s["sgu_sq"], m + 1)
                    ve.tensor_reduce(ss[:, 8:16], v_tmp.rearrange("p (n d) -> p n d", d=HD), AX, ALU.add)\
                        .then_inc(s["sgu_var"], 1)
                    ve.wait_ge(s["sgu_rs"], m + 1)
                    ve.tensor_tensor(v3, v3, bc(rs[:, 8:16].unsqueeze(2), [P, 8, HD]), ALU.mult)\
                        .then_inc(s["sgu_ready"], 1)
                elif item[0] == "sgu":
                    _, m, n = item
                    ve.wait_ge(s["sgu_mixed"], 2 * m + n + 1)
                    mixed = v_tmp.rearrange("p (h n i) -> p h n i", n=2, i=P)
                    for hd in range(4):
                        hh = 4 * m + hd
                        op = ve.scalar_tensor_tensor(mixed[:, hd, n, :], PS[:, 5, hd * P:(hd + 1) * P],
                                                     ln_g[:, hh:hh + 1], bs_bc[:, hh, :], ALU.mult, ALU.add)
                    op.then_inc(s["sgu_taken"], 1)

            def post(m, gate, g_post):
                ve.tensor_tensor(gate_col, gate, g_post, ALU.mult)
                ve.drain()
                for j in range(4):
                    if m or j >= 2:
                        ve.wait_ge(s["post_bc"], 4 * m + j - 1)
                    for f in range(4):
                        op = ve.tensor_scalar(gate_w[:, j % 2, f, :], ones[:], gate_col[:, 4 * j + f:4 * j + f + 1],
                                              None, ALU.mult)
                    op.then_inc(s["post_w"], 1)
                for g in range(4):
                    ve.wait_ge(s["post_bc_kept"], 4 * m + g + 1)
                    ve.wait_ge(s["post_squared"], 4 * m + g + 1)
                    gate_part = bc(gate_bc[:, CN * g:CN * (g + 1)].unsqueeze(1), [P, 2, CN])
                    ve.tensor_tensor(mix_out[:, :, CN * g:CN * (g + 1)], pair(2 * (g % 2)), gate_part, ALU.mult)\
                        .then_inc(s["post_scaled"], 1)
                ve.drain()
                ve.wait_ge(s["post_rs"], m + 1)
                for h in range(2):
                    for half in range(2):
                        part = x_tok[:, h, D // 2 * half:D // 2 * (half + 1)]
                        ve.scalar_tensor_tensor(part, mix_out[:, h, D // 2 * half:D // 2 * (half + 1)],
                                                norm_rs[:, h:h + 1], part, ALU.mult, ALU.add)\
                            .then_inc(s["post_added"], 1)

            post(0, mod[:, 64:80], g_post1)
            norm("ffn2", x_tok, norm_tmp, act_t, scale_x2, mod[:, 80:96])

            ve.sem_inc(s["hidden2_ready"], 1)
            with ve.Fori(0, 11) as i:
                ve.wait_ge(s["up2_g_free"], i + 1)
                group_done(ve, i * 8 + (N_UP2 + 7))
                ve.tensor_tensor(hidden[:, bass.ds(i * 4, 4), :].rearrange("p (a b) t -> p a (b t)", a=2),
                                 conv_g.rearrange("p (a b) t -> p a (b t)", a=2), pair(2), ALU.mult)\
                    .then_inc(s["hidden2_ready"], 1)
            post(1, mod[:, 112:128], g_post2)

        @block.scalar
        def _(act):
            def sum_squares(key, src, junk, parts=1, ready=None):
                w = D // parts
                junk = junk.rearrange("p a b c -> p (a b c)")[:, 0:w]
                order = [(h, part) for part in range(parts) for h in range(2)]
                if key == "ffn2":
                    order.sort()
                for h, part in order:
                    if ready:
                        ready(h, part)
                    act.activation(junk, src[:, h, w * part:w * (part + 1)], ACT.Square,
                                   accum_out=part_ss[:, 2 * part + h:2 * part + h + 1])
                    act.drain()
                act.drain().then_inc(norm_sems[key]["squared"], 1)

            def norm_keep(key, dst, gain, shift=None):
                n = norm_sems[key]
                for j in range(8):
                    act.wait_ge(n["turned"], j + 1)
                    for m in range(3 - keepers(key)):
                        kt = 2 * j + m
                        bias_ = 0.0 if shift is None else shift[:, kt:kt + 1]
                        op = act.activation(dst[:, kt, :], norm_bank(key, j, m), ACT.Identity,
                                            scale=gain[:, kt:kt + 1], bias=bias_)
                    op.then_inc(n["kept"], 1)

            act.dma_start(x_tok[:, 1, :], a["x"][P:T, :]).then_inc(s["x1_loaded"], 16)
            for dst, src in first:
                act.dma_start(dst, src).then_inc(s["first_loaded"], 16)
            act.wait_ge(s["setup_done"], 1)
            sum_squares("mix", x_tok, norm_tmp, ready=lambda h, part: act.wait_ge(s[f"x{h}_loaded"], 16))
            norm_keep("mix", act_t, g_mix)
            for dst, src in consts:
                act.dma_start(dst, src).then_inc(s["consts_loaded"], 16)
            act.wait_ge(s["consts_loaded"], 16 * N_CONSTS)
            act.activation(c_vec, c_vec, ACT.Silu).then_inc(s["c_ready"], 1)

            def pair(bank, width=512):
                return PS[:, bank:bank + 2, 0:width]

            for g, kind in enumerate(NORMED):
                heads = 2 if kind == "kv" else 4
                w = heads * HD
                group_done(act, N_PROJ + 4 * g + 3)
                if g:
                    act.wait_ge(s["proj_free"], g)
                act.activation(tmp[0][:, 0:2 * w].rearrange("p (h w) -> p h w", h=2), pair(2 * (g % 2), w),
                               ACT.Square).then_inc(s["squared"], 1)
                act.wait_ge(s["summed"], g + 1)
                act.activation(rs[:, 0:2 * heads], ss[:, 0:2 * heads], ACT.Ln, scale=1.0 / HD, bias=eps_col)
                act.drain()
                act.activation(rs[:, 0:2 * heads], rs[:, 0:2 * heads], ACT.Exp, scale=-0.5)\
                    .then_inc(s["rstd_ready"], 1)
                act.wait_ge(s["turned"], g + 1)
                dst = {"qa0": qa_t[:, 0:4], "qa1": qa_t[:, 4:8], "kv": ka_t[:], "qb0": qb_t[:, 0:4],
                       "qb1": qb_t[:, 4:8], "kb0": kb_t[:, 0:4], "kb1": kb_t[:, 4:8]}[kind]
                dst = dst.rearrange("p n t -> p (n t)")
                src = PS[:, 4:6, :].rearrange("p a b -> p (a b)")[:, 0:heads * T]
                if kind[1] == "b":
                    op = act.activation(dst, src, ACT.Copy, scale=bq_norm if kind[0] == "q" else bk_norm)
                else:
                    op = act.copy(dst, src)
                op.then_inc(s["qkv_kept"], 1)

            act.sem_inc(s["gate_kept"], 1)
            with act.Fori(0, 4) as i:
                for u in range(2):
                    done = i * 2 + u
                    act.wait_ge(s["max_ready"], done + 1)
                    for n, sc in ((0, score_a), (1, score_b)):
                        for b in range(2):
                            at_ = 2 * n + b
                            act.activation(sc[:, b, :], sc[:, b, :], ACT.Exp, bias=mx[:, 4 + at_:5 + at_],
                                           accum_out=den[:, at_:at_ + 1])
                    for b in range(2):
                        op = act.activation(den[:, 4 + b:5 + b], sink[:, bass.ds(i * 2 + u, 1)], ACT.Exp,
                                            bias=mx[:, 4 + b:5 + b])
                    op.then_inc(s["exps_done"], 1)
                    act.wait_ge(s["probs_turned"], done + 1)
                    act.copy(pt_a[:], PS[:, 6, :].rearrange("p (k t) -> p k t", t=T))
                    act.copy(pt_b[:], PS[:, 7, :].rearrange("p (k t) -> p k t", t=T)).then_inc(s["probs_t_ready"], 1)
                    act.wait_ge(s["attn_done"], done + 2)
                    act.copy(oa_t[:, done, :], PS[:, 0, 0:T])
                    act.copy(ob_t[:, done, :], PS[:, 1, 0:T]).then_inc(s["attn_kept"], 1)
                    group_done(act, i * 8 + (N_GATE + 4 * u + 3))
                    act.copy(gates[:, bass.ds(i * 8 + 4 * u, 4), :].rearrange("p (a b) t -> p a (b t)", a=2),
                             pair(2)).then_inc(s["gate_kept"], 1)
            act.drain()
            for g in range(4):
                for at_ in (0, 16):
                    ga = gates[:, at_ + 4 * g:at_ + 4 * g + 4, :]
                    op = act.activation(ga, ga, ACT.Sigmoid)
                op.then_inc(s["gates_squashed"], 1)

            sum_squares("ffn", x_tok, norm_tmp, 4, lambda h, part: act.wait_ge(s["wout_added"], part + 1))
            norm_keep("ffn", act_t, g_ffn)

            def conv_base(dst, bank, i, at_):
                for f in range(4):
                    w = conv[:, bass.ds(i * 4 + (at_ + f), 1), :]
                    op = act.activation(dst[:, f, :], PS[:, bank + f // 2, (f % 2) * T:(f % 2) * T + T],
                                        ACT.Identity, scale=w[:, 0, 1:2], bias=w[:, 0, 3:4])
                return op

            with act.Fori(0, 11) as i:
                act.wait_ge(s["hidden_ready"], i + 1)
                group_done(act, i * 8 + (N_UP + 3))
                conv_base(conv_g, 0, i, 0).then_inc(s["up_g_based"], 1)
                act.wait_ge(s["up_g_free"], i + 1)
                act.activation(conv_g[:], conv_g[:], ACT.Silu).then_inc(s["up_g_act"], 1)
                group_done(act, i * 8 + (N_UP + 7))
                conv_base(conv_v, 2, i, KF).then_inc(s["up_v_based"], 1)

            act.wait_ge(s["hidden_ready"], 12)
            act.wait_ge(s["mod_ready"], 1)
            act.wait_ge(s["ctx_loaded"], 32)
            sum_squares("ctx", ctx_tok, norm_tmp_c)
            norm_keep("ctx", act_t, scale_c, mod[:, 0:16])
            act.wait_ge(s["down_added"], 4)
            act.wait_ge(s["mod_ready"], 2)
            sum_squares("mix2", x_tok, norm_tmp2[:, 0:4])

            def keep_d(m):
                act.wait_ge(s["d_done"], m + 1)
                act.copy(d_t[0:2 * RANK, :], PS[0:2 * RANK, 7, 0:T]).then_inc(s["d_kept"], 1)

            def log_decay(m):
                flat = la.rearrange("p a b c -> p (a b) c")
                act.wait_ge(s["la_done"], m + 1)
                act.activation(flat, PS[:, 4:8, :], ACT.Abs)
                act.drain()
                act.activation(flat, flat, ACT.Exp, scale=-1.0)
                act.drain()
                act.activation(flat, flat, ACT.Ln, bias=one_col).then_inc(s["la_exp"], 1)

            keep_d(0)
            log_decay(0)
            group_done(act, N_CTX + 3)
            act.copy(kc_tok[:], pair(0)).then_inc(s["ctx_kept"], 1)
            act.wait_ge(s["rem_done"], 1)
            act.activation(e_buf[:], PS[:, 4:6, :], ACT.Exp)
            act.activation(qe[:], PS[:, 6:8, :], ACT.Exp).then_inc(s["rem_exp"], 1)
            norm_keep("mix2", hx_t, scale_x1, mod[:, 32:48])
            for m in range(2):
                group_done(act, N_CTX + 4 * m + 7)
                act.copy(vvc[:, :, 512 * m:512 * (m + 1)], pair(2 - 2 * m)).then_inc(s["ctx_kept"], 1)
            for r in range(2):
                act.wait_ge(s["state_done"], r + 1)
                act.copy(state[:, r, 0, :].rearrange("p (a b) -> p a b", a=2), pair(4 + 2 * r))\
                    .then_inc(s["state_ready"], 1)

            lv = 0
            for item in sched:
                if item[0] == "post":
                    g = item[1]
                    kind = MIX_GROUPS[g][0]
                    bank = 2 * (g % 2)
                    group_done(act, N_MIX + 4 * g + 3)
                    feat = lambda n: cat_t[:, n:n + 4, :].rearrange("p (a b) t -> p a (b t)", a=2)
                    if kind == "k":
                        op = act.copy(k_tok[:], pair(bank))
                    elif kind == "q":
                        op = act.activation(q_t.rearrange("p (a b) t -> p a (b t)", a=2), pair(bank), ACT.Copy,
                                            scale=float(HD) ** -0.5)
                    elif kind[:2] == "vv":
                        m = int(kind[2])
                        op = act.copy(vv[:, :, 512 * m:512 * (m + 1)], pair(bank))
                    elif kind[0] == "u":
                        op = act.activation(feat(4 * int(kind[1])), pair(bank), ACT.Gelu_apprx_tanh)
                    elif kind[0] == "g":
                        op = act.activation(feat(8 + 4 * int(kind[1])), pair(bank), ACT.Silu)
                    else:
                        if kind == "v1":
                            act.wait_ge(s["sgu_mixed"], 2)
                        op = act.activation(v_sgu.rearrange("p (a b) -> p a b", a=2), pair(bank),
                                            ACT.Gelu_apprx_tanh)
                    op.then_inc(s["grp_free"], 1)
                    if kind in ("v0", "v1"):
                        m = int(kind[1])
                        act.wait_ge(s["sgu_centred"], m + 1)
                        if m:
                            act.wait_ge(s["cat_ready"], 1)
                        act.activation(v_tmp, v_sgu, ACT.Square).then_inc(s["sgu_sq"], 1)
                        act.wait_ge(s["sgu_var"], m + 1)
                        act.activation(rs[:, 8:16], ss[:, 8:16], ACT.Ln, scale=1.0 / HD, bias=eps_col)
                        act.drain()
                        act.activation(rs[:, 8:16], rs[:, 8:16], ACT.Exp, scale=-0.5).then_inc(s["sgu_rs"], 1)
                elif item[0] == "d":
                    keep_d(1)
                elif item[0] == "la":
                    log_decay(1)
                elif item[0] == "kt":
                    act.wait_ge(s["kt_done"], 1)
                    act.copy(k_t.rearrange("p (a b) t -> p a (b t)", a=2), pair(4)).then_inc(s["kt_kept"], 1)
                elif item[0] == "cum":
                    act.wait_ge(s["cum_done"], 1)
                    act.copy(b_t.rearrange("p a b c -> p (a b) c"), PS[:, 4:8, :]).then_inc(s["cum_kept"], 1)
                elif item[0] == "wst":
                    act.wait_ge(s["ws_turned"], 1)
                    act.copy(ws_t.rearrange("p (a b) i -> p a (b i)", a=2), pair(4)).then_inc(s["ws_kept"], 1)
                elif item[0] == "rem":
                    r = item[1]
                    act.wait_ge(s["rem_done"], 2 + r)
                    act.activation(e_buf[:, r, :], PS[:, 6 + r, :], ACT.Exp).then_inc(s["rem_exp"], 1)
                elif item[0] == "upd":
                    r = item[1]
                    edge = HD - 1 if r == 0 else 0
                    act.activation(decay[:, 4 * r:4 * r + 4], b_t[:, r, r, edge:512:HD], ACT.Exp)\
                        .then_inc(s["decay_ready"], 1)
                elif item[0] == "qe":
                    n = item[1]
                    if n:
                        act.wait_ge(s["y_turned"], 1)
                    act.activation(qe[:], b_t[:, n], ACT.Exp).then_inc(s["qe_exp"], 1)
                elif item[0] == "level" and item[2] < 7:
                    lv += 1
                    act.wait_ge(s["lv_diff"], lv)
                    act.activation(e_buf[:], e_buf[:], ACT.Abs)
                    act.drain()
                    act.activation(e_buf[:], e_buf[:], ACT.Exp, scale=-1.0).then_inc(s["lv_exp"], 1)
                elif item[0] == "o":
                    n = item[1]
                    act.wait_ge(s["o_done"], n + 1)
                    act.activation(y_tok.rearrange("p (a b) -> p a b", a=2), PS[:, 6:8, :], ACT.Square)\
                        .then_inc(s["o_sq"], 1)
                    act.wait_ge(s["o_sum"], n + 1)
                    act.activation(rs[:, 0:4], ss[:, 0:4], ACT.Ln, scale=1.0 / T, bias=eps_col)
                    act.drain()
                    act.activation(rs[:, 0:4], rs[:, 0:4], ACT.Exp, scale=-0.5).then_inc(s["o_rs"], 1)

            def post(m, n0, chunks):
                for j in range(4):
                    act.wait_ge(s["post_bc"], 4 * m + j + 1)
                    act.copy(gate_bc[:, CN * j:CN * (j + 1)], PS[:, 7, :]).then_inc(s["post_bc_kept"], 1)
                for g in range(4):
                    group_done(act, n0 + chunks * (g + 1) - 1)
                    for h in range(2):
                        junk = norm_tmp.rearrange("p a b c -> p (a b c)")[:, CN * h:CN * (h + 1)]
                        act.activation(junk, PS[:, 2 * (g % 2) + h, :], ACT.Square,
                                       accum_out=part_ss[:, 2 * g + h:2 * g + h + 1])
                        act.drain()
                    act.drain().then_inc(s["post_squared"], 1)

            post(0, N_WOUT2, 4)
            sum_squares("ffn2", x_tok, norm_tmp, 2, lambda h, part: act.wait_ge(s["post_added"], 2 * h + part + 1))
            norm_keep("ffn2", act_t, scale_x2, mod[:, 80:96])
            with act.Fori(0, 11) as i:
                act.wait_ge(s["hidden2_ready"], i + 1)
                group_done(act, i * 8 + (N_UP2 + 3))
                act.activation(conv_g.rearrange("p (a b) t -> p a (b t)", a=2), pair(0), ACT.Silu)\
                    .then_inc(s["up2_g_free"], 1)
            post(1, N_DOWN2, 11)

        @block.gpsimd
        def _(pool):
            def rows_rstd(squared, count, parts, done):
                pool.wait_ge(squared, count)
                sums = part_ss[:, 0:2]
                if parts == 4:
                    pool.tensor_tensor(part_ss[:, 0:4], part_ss[:, 0:4], part_ss[:, 4:8], ALU.add)
                    pool.drain()
                if parts > 1:
                    pool.tensor_tensor(norm_ss, part_ss[:, 0:2], part_ss[:, 2:4], ALU.add)
                    pool.drain()
                    sums = norm_ss
                pool.tensor_scalar(norm_rs, sums, 1.0 / D, EPS, ALU.mult, ALU.add)
                pool.drain()
                pool.tensor_tensor(norm_rs, norm_rs, minus_half, ALU.pow).then_inc(done, 1)

            def norm_rstd(key, parts=1):
                rows_rstd(norm_sems[key]["squared"], 1, parts, norm_sems[key]["rstd"])

            pool.memset(ones[:], 1.0)
            pool.memset(eps_col, EPS)
            pool.memset(one_col, 1.0)
            pool.memset(minus_half, -0.5)
            pool.memset(rpb, 0.0)
            pool.drain().then_inc(s["setup_done"], 1)
            pool.wait_ge(s["setup_done"], 1)
            norm_rstd("mix")
            pool.wait_ge(weight_used, 4)
            for h in range(8):
                pool.dma_start(rpb[7 * h:7 * h + 7, 48:79], a["b_rpb"][h, 4:11, :]).then_inc(s["rpb_loaded"], 16)
            pool.wait_ge(s["rpb_loaded"], 128)
            src = bc(rpb[:, 0:P - 1].unsqueeze(1), [56, GRID, P - 1])
            pool.dma_start(skew.rearrange("r (q c) -> r q c", c=P)[:, :, 0:P - 1], src).then_inc(s["skew_written"], 16)
            pool.wait_ge(s["skew_written"], 16)
            pool.wait_ge(s["consts_loaded"], 16 * N_CONSTS)
            pool.wait_ge(s["proj_free"], 8)
            pool.wait_ge(s["qkv_kept"], 5)
            with pool.Fori(0, 4) as i:
                for u in range(2):
                    done = i * 2 + u
                    pool.wait_ge(s["bias_used"], done + 1)
                    for qr in range(4):
                        src = bass.AP(skew.tensor, i * (2 * 7 * 64 * P) + (u * 7 + 3 - qr) * 64 * P + GRID - 1,
                                      [[P - 1, GRID], [64 * P, 4], [1, GRID]])
                        dst = bias[(qr % 2) * GRID:(qr % 2 + 1) * GRID, qr // 2, :]
                        pool.dma_start(dst.rearrange("p (r c) -> p r c", c=GRID), src).then_inc(s["bias_loaded"], 16)
                    pool.wait_ge(s["attn_done"], done + 1)
                    if u:
                        pool.wait_ge(s["proj_free"], 9)
                    pool.tensor_copy(q_head[0], qa_t[:, done, :])
                    pool.tensor_copy(q_head[1], qb_t[:, done, :])
                    pool.tensor_copy(v_head[0][:], va[:, :, bass.ds(i // 2 * P, P)])
                    pool.tensor_copy(v_head[1][:], vb[:, :, bass.ds(i * (2 * P) + u * P, P)])
                    pool.drain().then_inc(s["head_staged"], 1)

            def load_job(j, cols):
                for c in range(4):
                    pool.wait_ge(s["wmod_used"], j * 4 + (c + 1))
                    pool.dma_start(wmod[:, c, :, :], w_mod[:, CK * c:CK * c + CK, cols])\
                        .then_inc(s[f"wmod_loaded{c}"], 16)

            norm_rstd("ffn", 4)
            group_done(pool, N_WOUT + 15)
            pool.sem_inc(s["wmod_used"], 4)
            with pool.Fori(0, SHARED) as i:
                load_job(i, bass.ds(i * CN, CN))
            norm_kept(pool, "ffn")
            for h in range(2):
                pool.dma_start(ctx_tok[:, h, :], a["ctx_2"][h * P:(h + 1) * P, :]).then_inc(s["ctx_loaded"], 16)
            with pool.Fori(SHARED, JOBS - SHARED) as i:
                load_job(i, bass.ds(i * CN, CN))
            norm_rstd("ctx")
            pool.wait_ge(norm_sems["ctx"]["turned"], 8)
            pool.wait_ge(s["job_kept"], 2 + JOBS)
            pool.memset(wd2, 0.0)
            pool.drain().then_inc(s["setup_done"], 1)
            pool.wait_ge(s["setup_done"], 2)
            for row, n, col, name in ((0, RANK, 0, "gla_wd2_fwd_2"), (RANK, RANK, 512, "gla_wd2_bwd_2"),
                                      (2 * RANK, 1, 0, "gla_bd_fwd_2"), (2 * RANK, 1, 512, "gla_bd_bwd_2")):
                pool.dma_start(wd2[row:row + n, col:col + 512], a[name]).then_inc(s["wd2_loaded"], 16)
            pool.dma_start(tri[:], a["t_tri"]).then_inc(s["masks_loaded"], 16)
            pool.dma_start(level_mask[:], a["t_levels"]).then_inc(s["masks_loaded"], 16)
            norm_rstd("mix2")
            group_done(pool, N_CTX + 11)
            pool.dma_start(v_sgu.rearrange("p (h j) -> p h j", j=P), a["gmlp_ws_2"].rearrange("h i j -> i h j"))\
                .then_inc(s["mixer_loaded"], 16)
            pool.dma_start(bs_bc.rearrange("p h i -> p (h i)"),
                           bass.AP(a["gmlp_bs_2"].tensor, 0, [[0, P], [1, 1024]])).then_inc(s["bs_loaded"], 16)
            lv = 0
            pool.wait_ge(s["kt_kept"], 1)
            for item in sched:
                if item[0] != "level":
                    continue
                _, n, l = item
                if lv >= 2:
                    pool.wait_ge(s["lv_done"], lv - 1)
                if l < 7:
                    size = LEVELS[l]
                    pool.wait_ge(s["lv_exp"], lv + 1 - n)
                    for half in range(2):
                        op = pool.tensor_tensor(block_half(kl[:, lv % 2, :], size, half),
                                                token_half(k_t, n, size, half),
                                                block_half(e_buf[:, half, :], size, half), ALU.mult)
                    op.then_inc(s["lv_k"], 1)
                else:
                    pool.tensor_copy(kl[:, lv % 2, :].rearrange("p (h i) -> p h i", i=P),
                                     k_t[:, :, n * P:(n + 1) * P]).then_inc(s["lv_k"], 1)
                lv += 1

            rows_rstd(s["post_squared"], 4, 4, s["post_rs"])
            norm_rstd("ffn2", 2)
            rows_rstd(s["post_squared"], 8, 4, s["post_rs"])


WEIGHTS = ["w_in", "w_branch_a", "w_branch_b", "w_out", "w_up", "w_down", "w_mod_2", "w_in_2", "w_out_2",
           "w_ffn_in_2", "w_ffn_out_2"]
FEATURE_MAJOR = {"norm_mix": 16, "norm_ffn": 16, "g_pre_mix_2": 16, "g_post_mix_2": 16, "g_pre_ffn_2": 16,
                 "g_post_ffn_2": 16, "b_mod_2": 96, "c_2": 16, "c_ctx_2": 16, "b_q_norm": 1, "b_k_norm": 1,
                 "gla_out_g_2": 8, "gmlp_ln_g_2": 8, "gmlp_ln_b_2": 8}
ROWS = ["gla_wd2_fwd_2", "gla_wd2_bwd_2", "gla_bd_fwd_2", "gla_bd_bwd_2", "a_q_norm", "a_k_norm", "a_sink"]


def kernel(**inputs):
    import numpy as _np
    import concourse.bacc as _bacc
    from concourse import mybir as _mybir
    from concourse.bass_utils import run_bass_kernel_spmd as _run

    get = lambda n: _np.asarray(inputs[n])
    laid = {n: get(n)[0] for n in WEIGHTS}
    laid["x"], laid["ctx_2"] = get("x")[0], get("ctx_2")[0]
    for n, cols in FEATURE_MAJOR.items():
        laid[n] = get(n).reshape(cols, P).T
    for n in ROWS:
        laid[n] = get(n).reshape(-1, get(n).shape[-1])
    laid["b_rpb"], laid["gmlp_ws_2"], laid["gmlp_bs_2"] = get("b_rpb")[0], get("gmlp_ws_2")[0], get("gmlp_bs_2")[0]
    conv = _np.concatenate([get("conv_w")[0], get("conv_b")], 0)
    laid["conv"] = conv.reshape(4, 2 * KF, P).transpose(2, 1, 0)
    decay_cols = laid["w_in_2"][:, -2 * RANK:]
    laid["w_decay"] = decay_cols.reshape(KD, P, 2 * RANK).transpose(1, 0, 2)
    laid.update(host_tables())

    nc = _bacc.Bacc("TRN2", target_bir_lowering=False, num_devices=1)
    arrays, args = {}, {}
    for name, arr in laid.items():
        arr = _np.ascontiguousarray(arr)
        arrays[f"in_{name}"] = arr
        args[name] = nc.dram_tensor(f"in_{name}", arr.shape, _mybir.dt.from_np(arr.dtype), kind="ExternalInput").ap()
    out = nc.dram_tensor("out", (T, D), F32, kind="ExternalOutput").ap()
    build(nc, args, out)
    r = _run(nc, [arrays], core_ids=[0])
    return r.results[0]["out"].reshape(1, T, D)
```
